# Optimizing a Trainium2 kernel written in Bass

```python
import math
import jax, jax.numpy as jnp
from jax import lax
import numpy as np

D_MODEL = 1024
BATCH = 1
SEQ = 1024
DEPTH = 1
DEC_BATCH = 8
DEC_SEQ = 4
PAST_LEN = 1024
PAGE_SIZE = 128

PLE_DIM = 256
GROUP_W = D_MODEL // 4
CONV_W = 3
POOL_WINDOWS = (2, 4, 8, 16)
POOL_GW = GROUP_W // len(POOL_WINDOWS)
POOL_BUF = max(POOL_WINDOWS) - 1
DSA_HEADS = 4
DSA_HD = GROUP_W // DSA_HEADS
IDX_HEADS = 8
IDX_HD = 64
IDX_SCALE = IDX_HEADS ** -0.5 * IDX_HD ** -0.5
TOPK_MAX = 256
DIFF_HEADS = 4
DIFF_VD = GROUP_W // DIFF_HEADS
DIFF_QD = DIFF_VD // 2
D_FF = 2816
Q_BLOCK = 128
EPS = 1e-6
SPLIT_SIZES = (GROUP_W, GROUP_W, GROUP_W,
               GROUP_W,
               DSA_HEADS * DSA_HD, DSA_HD, DSA_HD,
               IDX_HEADS * IDX_HD, IDX_HEADS, IDX_HD,
               DIFF_HEADS * 2 * DIFF_QD, DIFF_HEADS * 2 * DIFF_QD, DIFF_HEADS * DIFF_VD)
D_IN = sum(SPLIT_SIZES)

kernel_name = 'hymba_style_hybrid_decode_step'

def rmsnorm(x, g):
    xf = x.astype(jnp.float32)
    y = xf * lax.rsqrt(jnp.mean(xf * xf, axis=-1, keepdims=True) + EPS)
    return (y * g.astype(jnp.float32)).astype(x.dtype)

def causal_dwconv(buf, x, w):
    ext = jnp.concatenate([buf.astype(x.dtype), x], axis=1)
    T = x.shape[1]
    y = sum(ext[:, k:k + T] * w[k] for k in range(CONV_W))
    return y, ext[:, -(CONV_W - 1):]

def multiscale_pool(buf, v, pos0, maps, scale):
    Bt, T, C = v.shape
    ext = jnp.concatenate([buf.astype(v.dtype), v], axis=1).astype(jnp.float32)
    cs = jnp.concatenate([jnp.zeros((Bt, 1, C), jnp.float32), jnp.cumsum(ext, axis=1)], axis=1)
    end = cs[:, POOL_BUF + 1:POOL_BUF + 1 + T]
    pos = pos0 + jnp.arange(T)
    outs = []
    for g, w in enumerate(POOL_WINDOWS):
        sl = slice(g * POOL_GW, (g + 1) * POOL_GW)
        start = cs[:, POOL_BUF + 1 - w:POOL_BUF + 1 - w + T, sl]
        cnt = jnp.minimum(w, pos + 1).astype(jnp.float32)[None, :, None]
        outs.append((end[..., sl] - start) / cnt - ext[:, POOL_BUF:, sl])
    d = jnp.stack(outs, axis=2).astype(v.dtype)
    y = jnp.einsum('btgc,gcd->btgd', d, maps).reshape(Bt, T, C) * scale
    return y, ext[:, -POOL_BUF:].astype(v.dtype)

def dsa_block(q, qi, wi, qpos, k, v, ki, n_sel):
    S = k.shape[1]
    causal = jnp.arange(S)[None, :] <= qpos[:, None]
    s = jnp.einsum('bqhd,bsd->bqhs', qi, ki).astype(jnp.float32)
    score = jnp.einsum('bqhs,bqh->bqs', jax.nn.relu(s), wi.astype(jnp.float32)) * IDX_SCALE
    score = jnp.where(causal[None], score, -jnp.inf)
    _, sel = lax.top_k(score, n_sel)
    gather = jax.vmap(lambda a, i: a[i])
    k_sel = gather(k, sel)
    v_sel = gather(v, sel)
    valid = sel <= qpos[None, :, None]
    logits = jnp.einsum('bqhd,bqkd->bhqk', q, k_sel).astype(jnp.float32) * DSA_HD ** -0.5
    logits = jnp.where(valid[:, None], logits, -jnp.inf)
    a = jax.nn.softmax(logits, axis=-1).astype(v.dtype)
    return jnp.einsum('bhqk,bqkd->bqhd', a, v_sel)

def diff_block(q, qpos, k, v, lam):
    S = k.shape[1]
    causal = jnp.arange(S)[None, :] <= qpos[:, None]
    def probs(qh, kh):
        l = jnp.einsum('bqhd,bshd->bhqs', qh, kh).astype(jnp.float32) * DIFF_QD ** -0.5
        return jax.nn.softmax(jnp.where(causal, l, -jnp.inf), axis=-1)
    a = probs(q[..., :DIFF_QD], k[..., :DIFF_QD]) - lam * probs(q[..., DIFF_QD:], k[..., DIFF_QD:])
    return jnp.einsum('bhqs,bshd->bqhd', a.astype(v.dtype), v)

def over_query_blocks(fn, q_args, qpos):
    T = qpos.shape[0]
    if T <= Q_BLOCK:
        return fn(*q_args, qpos)
    nb = T // Q_BLOCK
    def split(a):
        return jnp.moveaxis(a.reshape(a.shape[0], nb, Q_BLOCK, *a.shape[2:]), 1, 0)
    xs = tuple(split(a) for a in q_args) + (qpos.reshape(nb, Q_BLOCK),)
    out = lax.map(lambda b: fn(*b), xs)
    out = jnp.moveaxis(out, 0, 1)
    return out.reshape(out.shape[0], T, *out.shape[3:])

def gather_pages(cache, page_table, i):
    g = cache[page_table, i]
    return g.reshape(g.shape[0], g.shape[1] * g.shape[2], *g.shape[3:])

def trunk_layer(i, h, p, conv_buf, pool_buf, ffn_buf, past_c, past_d, W):
    Bt, T, _ = h.shape
    P = 0 if past_c is None else past_c[0].shape[1]
    qpos = P + jnp.arange(T)
    xn = rmsnorm(h, W['norm_mix'][i])
    z = xn @ W['w_in'][i]
    cuts = np.cumsum(SPLIT_SIZES)[:-1].tolist()
    (gb, gc, gh, pv, cq, ck, cv, cqi, cwi, cki, dq, dk, dv) = jnp.split(z, cuts, axis=-1)
    conv_out, new_conv = causal_dwconv(conv_buf, gc * gh, W['conv_a'][i])
    y_a = gb * conv_out
    y_b, new_pool = multiscale_pool(pool_buf, pv, P, W['pool_maps'][i], W['pool_scale'][i])
    cq = cq.reshape(Bt, T, DSA_HEADS, DSA_HD)
    cqi = cqi.reshape(Bt, T, IDX_HEADS, IDX_HD)
    if past_c is None:
        kc, vc, kic = ck, cv, cki
    else:
        kc = jnp.concatenate([past_c[0].astype(ck.dtype), ck], axis=1)
        vc = jnp.concatenate([past_c[1].astype(cv.dtype), cv], axis=1)
        kic = jnp.concatenate([past_c[2].astype(cki.dtype), cki], axis=1)
    n_sel = min(TOPK_MAX, (P + T) // 4)
    y_c = over_query_blocks(lambda q_, qi_, wi_, qp_: dsa_block(q_, qi_, wi_, qp_, kc, vc, kic, n_sel),
                            (cq, cqi, cwi), qpos).reshape(Bt, T, GROUP_W)
    dq = dq.reshape(Bt, T, DIFF_HEADS, 2 * DIFF_QD)
    dk = dk.reshape(Bt, T, DIFF_HEADS, 2 * DIFF_QD)
    dv = dv.reshape(Bt, T, DIFF_HEADS, DIFF_VD)
    if past_d is None:
        kd, vd = dk, dv
    else:
        kd = jnp.concatenate([past_d[0].astype(dk.dtype), dk], axis=1)
        vd = jnp.concatenate([past_d[1].astype(dv.dtype), dv], axis=1)
    lam_init = 0.8 - 0.6 * math.exp(-0.3 * i)
    lp = W['diff_lambda'][i].astype(jnp.float32)
    lam = jnp.exp(jnp.sum(lp[0] * lp[1])) - jnp.exp(jnp.sum(lp[2] * lp[3])) + lam_init
    o = over_query_blocks(lambda q_, qp_: diff_block(q_, qp_, kd, vd, lam), (dq,), qpos)
    y_d = (rmsnorm(o, W['diff_subln'][i]) * (1.0 - lam_init)).reshape(Bt, T, GROUP_W)
    h = h + jnp.concatenate([y_a, y_b, y_c, y_d], axis=-1) @ W['w_out'][i]
    xn2 = rmsnorm(h, W['norm_ffn'][i])
    g_conv, new_ffn = causal_dwconv(ffn_buf, xn2 @ W['w_gate'][i], W['conv_ffn'][i])
    h = h + (jax.nn.silu(g_conv) * (xn2 @ W['w_up'][i])) @ W['w_down'][i]
    gate = jax.nn.sigmoid(rmsnorm(h, W['norm_ple'][i]) @ W['w_ple_gate'][i])
    h = h + (p @ W['w_ple'][i]) * gate
    return h, (new_conv, new_pool, new_ffn, ck, cv, cki, dk, dv)

def setup_inputs(seed: int = 0) -> dict:
    key = jax.random.key(seed)
    ks = list(jax.random.split(key, 40))
    def nrm(shape, s=1.0):
        return jax.random.normal(ks.pop(), shape, jnp.float32) * s
    n_pages = PAST_LEN // PAGE_SIZE
    n_used = DEC_BATCH * n_pages
    n_phys = (n_used * 5) // 4
    perm = jax.random.permutation(ks.pop(), n_phys)
    page_table = perm[:n_used].reshape(DEC_BATCH, n_pages).astype(jnp.int32)
    return {
        'x_prompt': nrm((BATCH, SEQ, D_MODEL)),
        'x_sample': nrm((DEC_BATCH, DEC_SEQ, D_MODEL)),
        'state_conv_a': nrm((DEPTH, DEC_BATCH, CONV_W - 1, GROUP_W)),
        'state_pool': nrm((DEPTH, DEC_BATCH, POOL_BUF, GROUP_W)),
        'state_ffn': nrm((DEPTH, DEC_BATCH, CONV_W - 1, D_FF)),
        'cache_c_k': nrm((n_phys, DEPTH, PAGE_SIZE, DSA_HD)),
        'cache_c_v': nrm((n_phys, DEPTH, PAGE_SIZE, DSA_HD)),
        'cache_c_idx': nrm((n_phys, DEPTH, PAGE_SIZE, IDX_HD)),
        'cache_d_k': nrm((n_phys, DEPTH, PAGE_SIZE, DIFF_HEADS, 2 * DIFF_QD)),
        'cache_d_v': nrm((n_phys, DEPTH, PAGE_SIZE, DIFF_HEADS, DIFF_VD)),
        'page_table': page_table,
        'p_prompt': nrm((DEPTH, BATCH, SEQ, PLE_DIM)),
        'p_sample': nrm((DEPTH, DEC_BATCH, DEC_SEQ, PLE_DIM)),
        'norm_mix': 1.0 + nrm((DEPTH, D_MODEL), 0.05),
        'w_in': nrm((DEPTH, D_MODEL, D_IN), D_MODEL ** -0.5),
        'conv_a': nrm((DEPTH, CONV_W, GROUP_W), 0.5),
        'pool_maps': nrm((DEPTH, len(POOL_WINDOWS), POOL_GW, POOL_GW), POOL_GW ** -0.5),
        'pool_scale': 1.0 + nrm((DEPTH, GROUP_W), 0.1),
        'diff_lambda': nrm((DEPTH, 4, DIFF_QD), 0.1),
        'diff_subln': 1.0 + nrm((DEPTH, DIFF_VD), 0.05),
        'w_out': nrm((DEPTH, D_MODEL, D_MODEL), D_MODEL ** -0.5),
        'norm_ffn': 1.0 + nrm((DEPTH, D_MODEL), 0.05),
        'w_gate': nrm((DEPTH, D_MODEL, D_FF), D_MODEL ** -0.5),
        'w_up': nrm((DEPTH, D_MODEL, D_FF), D_MODEL ** -0.5),
        'conv_ffn': nrm((DEPTH, CONV_W, D_FF), 0.5),
        'w_down': nrm((DEPTH, D_FF, D_MODEL), D_FF ** -0.5),
        'norm_ple': 1.0 + nrm((DEPTH, D_MODEL), 0.05),
        'w_ple_gate': nrm((DEPTH, D_MODEL, D_MODEL), D_MODEL ** -0.5),
        'w_ple': nrm((DEPTH, PLE_DIM, D_MODEL), PLE_DIM ** -0.5),
        'norm_final': 1.0 + nrm((D_MODEL,), 0.05),
    }

def reference(x_prompt, x_sample, state_conv_a, state_pool, state_ffn, cache_c_k, cache_c_v,
              cache_c_idx, cache_d_k, cache_d_v, page_table, p_prompt, p_sample, norm_mix, w_in,
              conv_a, pool_maps, pool_scale, diff_lambda, diff_subln, w_out, norm_ffn, w_gate,
              w_up, conv_ffn, w_down, norm_ple, w_ple_gate, w_ple, norm_final):
    W = dict(norm_mix=norm_mix, w_in=w_in, conv_a=conv_a, pool_maps=pool_maps,
             pool_scale=pool_scale, diff_lambda=diff_lambda, diff_subln=diff_subln, w_out=w_out,
             norm_ffn=norm_ffn, w_gate=w_gate, w_up=w_up, conv_ffn=conv_ffn, w_down=w_down,
             norm_ple=norm_ple, w_ple_gate=w_ple_gate, w_ple=w_ple)
    h = x_prompt
    bp = h.shape[0]
    outs_p = []
    for i in range(DEPTH):
        zc = jnp.zeros((bp, CONV_W - 1, GROUP_W), h.dtype)
        zp = jnp.zeros((bp, POOL_BUF, GROUP_W), h.dtype)
        zf = jnp.zeros((bp, CONV_W - 1, D_FF), h.dtype)
        h, st = trunk_layer(i, h, p_prompt[i], zc, zp, zf, None, None, W)
        outs_p.append(st)
    y_prompt = rmsnorm(h, norm_final)
    h = x_sample
    outs_s = []
    for i in range(DEPTH):
        past_c = (gather_pages(cache_c_k, page_table, i), gather_pages(cache_c_v, page_table, i),
                  gather_pages(cache_c_idx, page_table, i))
        past_d = (gather_pages(cache_d_k, page_table, i), gather_pages(cache_d_v, page_table, i))
        h, st = trunk_layer(i, h, p_sample[i], state_conv_a[i], state_pool[i], state_ffn[i],
                            past_c, past_d, W)
        outs_s.append(st)
    y_sample = rmsnorm(h, norm_final)

    def col(outs, j, axis):
        return jnp.stack([o[j] for o in outs], axis=axis)
    conv_a_p, conv_a_s = col(outs_p, 0, 0), col(outs_s, 0, 0)
    pool_p, pool_s = col(outs_p, 1, 0), col(outs_s, 1, 0)
    ffn_p, ffn_s = col(outs_p, 2, 0), col(outs_s, 2, 0)
    c_k_p, c_k_s = col(outs_p, 3, 1), col(outs_s, 3, 1)
    c_v_p, c_v_s = col(outs_p, 4, 1), col(outs_s, 4, 1)
    c_idx_p, c_idx_s = col(outs_p, 5, 1), col(outs_s, 5, 1)
    d_k_p, d_k_s = col(outs_p, 6, 1), col(outs_s, 6, 1)
    d_v_p, d_v_s = col(outs_p, 7, 1), col(outs_s, 7, 1)
    return (y_prompt, y_sample, conv_a_p, conv_a_s, pool_p, pool_s, ffn_p, ffn_s,
            c_k_p, c_k_s, c_v_p, c_v_s, c_idx_p, c_idx_s, d_k_p, d_k_s, d_v_p, d_v_s)


_drawn_inputs = setup_inputs


def setup_inputs(seed=0):
    import zlib

    import numpy as np

    out = dict(_drawn_inputs(seed))
    spreads = {}
    factors = {'diff_lambda': 8.0, 'diff_subln': 3.559, 'norm_ple': 24.554}
    for name, (base, spread) in spreads.items():
        noise = np.random.default_rng([zlib.crc32(name.encode()), seed]).standard_normal(out[name].shape)
        drawn = base * np.exp(spread * noise) if base else spread * noise
        out[name] = __import__('jax').numpy.asarray(drawn.astype(out[name].dtype))
    for name, factor in factors.items():
        out[name] = (out[name] * factor).astype(out[name].dtype)
    return out
```

```python
import math
from contextlib import ExitStack

import numpy as np
import concourse.bass as bass
from concourse import mybir

P = 128
D = 1024
KC = D // P
SEQ, DB, DT = 1024, 8, 4
NS = DB * DT
NT = SEQ + NS
TC = NT // 3
QT = SEQ // P
PAST, PAGE = 1024, 128
NPG = PAST // PAGE
NK = PAST + NS
FF = 2816
FC = FF // P
PLE = 256
TOPK = 256
HD = 64
IDXH = 8
IDX_SCALE = IDXH ** -0.5 * HD ** -0.5
DSA_SCALE = HD ** -0.5
DIFF_SCALE = 32 ** -0.5
LAM_INIT = 0.8 - 0.6 * math.exp(0.0)
EPS = 1e-6
BIG = 1e30

GB, GC, GH, PV = 0, 2, 4, 6
KA, KB, QI, CQ, DK, DQ, CV, DV = 8, 9, 10, 14, 16, 18, 20, 21
NZ = 23
IN_COLS = ([[(128 * j, 128)] for j in range(8)]
           + [[(1280, 64), (1928, 64)], [(1928, 64), (1280, 64)]]
           + [[(1408 + 128 * j, 128)] for j in range(4)]
           + [[(1024, 128)], [(1152, 128)]]
           + [[(2248, 128)], [(2376, 128)], [(1992, 128)], [(2120, 128)]]
           + [[(1344, 64), (1920, 8)], [(2504, 128)], [(2632, 128)]])
TILES = list(range(TOPK // P, QT))
SC_AT = {i: sum((j + 1) * P for j in TILES if j < i) for i in TILES}
SC_S = sum((j + 1) * P for j in TILES)
SC_N = SC_S + NK
NTOP = len(TILES) + 1


NW_USED = NZ + KC + 3 * FC + 2 + KC
NW = NW_USED + NW_USED % 2
OUTS = {"y": (KC, P, NT), "st_mix": (P, 2, 1 + DB, 17), "st_ffn": (P, FC, 1 + DB, 2), "c_k": (HD, NT), "c_v": (HD, NT),
        "c_idx": (HD, NT), "d_k": (2, P, NT), "d_v": (2, P, NT)}


def layout(pieces):
    at, out = 0, {}
    for name, n in pieces:
        out[name] = (at, n)
        at += n
    return out, at


CONST, CONST_N = layout([("ident", P), ("hsel", 8), ("sel0", 32), ("sel1", 32), ("e0", P), ("e1", P),
                         ("rep", P), ("newmask", NS), ("dmask", DB * NS), ("lam_a", 1), ("lam_b", 1),
                         ("inv_w", 2), ("inv_cnt", 32), ("headones", P), ("kneg", NTOP), ("kdiff", NTOP)])
PARAM, PARAM_N = layout([("g_mix", KC), ("g_ffn", KC), ("g_ple", KC), ("g_final", KC), ("conv_a", 6),
                         ("pool_scale", 2), ("conv_ffn", FC * 3), ("subln", 1), ("lam", P),
                         ("maps", 2 * P), ("st_conv", 2 * DB * 2), ("st_pool", 2 * DB * 15)])


def build(nc, d):
    f32, f32r, i32, u16 = mybir.dt.float32, mybir.dt.float32r, mybir.dt.int32, mybir.dt.uint16
    ALU, ACT, AX = mybir.AluOpType, mybir.ActivationFunctionType, mybir.AxisListType
    with ExitStack() as ctx:
        def sb(name, shape, dt=f32):
            return ctx.enter_context(nc.sbuf_tensor(name, shape, dt))

        def sem(name):
            return ctx.enter_context(nc.semaphore(name))

        arena_at = (nc.sbuf_base + 31) // 32 * 32
        arena = sb("arena", [P, 2 * KC * NT])
        xh = nc.alloc_sbuf_tensor_at("xh", [P, KC, NT], f32r, offset=arena_at)
        xl = nc.alloc_sbuf_tensor_at("xl", [P, KC, NT], f32r, offset=arena_at + 4 * KC * NT)
        taken = [0]

        def carve(n):
            taken[0] += n
            assert taken[0] <= 2 * KC * NT
            return arena[:, taken[0] - n:taken[0]]

        vtok = carve((QT + 1) * 384).rearrange("p (t f) -> p t f", f=384)
        SC = carve(SC_N)
        YF = carve(SC_N)
        YY = YF.bitcast(u16)
        y_hi, y_lo = YY[:, 0:SC_N], YY[:, SC_N:2 * SC_N]
        kring = carve(2 * NPG * PAGE).rearrange("p (s g c) -> p s g c", s=2, c=PAGE)
        qis = carve(IDXH * NS).rearrange("p (b h t) -> p b h t", b=DB, h=IDXH)
        wsel = carve(2 * NS).rearrange("p (g t) -> p g t", g=2)
        wcol = carve(2)
        tk = carve(12 * NTOP).rearrange("p (a j) -> p a j", j=NTOP)
        mx = carve(4)
        nm = carve(4)
        sm = carve(4)
        cf = carve(4)
        rs4 = carve(20)
        lamw = carve(4)
        CP = carve(P)
        newcp = carve(NS)
        if True:
            ST = sb("ST", [P, 2, 1 + DB, 17])
        z_at = (nc.sbuf_base + 31) // 32 * 32
        Z = sb("Z", [P, NZ, NT])
        ah = nc.alloc_sbuf_tensor_at("ah", [P, 2, 2, NT], f32r, offset=z_at)
        al = nc.alloc_sbuf_tensor_at("al", [P, 2, 2, NT], f32r, offset=z_at + 16 * NT)
        wr = sb("wr", [P, 2, KC, P])
        wh = sb("wh", [P, 2, KC, P], f32r)
        wl = sb("wl", [P, 2, KC, P], f32r)
        cst = sb("cst", [P, CONST_N])
        par = sb("par", [P, PARAM_N])
        ones = sb("ones", [P, P])
        ptab = sb("ptab", [1, DB * NPG], i32)
        TN = sb("TN", [P, 3, NT])
        small = sb("small", [P, 40])
        ps = [ctx.enter_context(nc.psum_tensor(f"ps{j}", [P, 4, 512], f32)) for j in range(2)]

        def c_(name, rows=P):
            at, n = CONST[name]
            return cst[0:rows, at:at + n]

        def p_(name):
            at, n = PARAM[name]
            return par[:, at:at + n]

        class Chain:

            def __init__(self, eng, name):
                self.eng, self.sem, self.n = eng, sem(name), 0

            def link(self, ins):
                self.n += 1
                ins.then_inc(self.sem, 1)
                self.eng.wait_ge(self.sem, self.n)

        s_const = sem("constants_loaded")
        outs_stored = sem("outputs_stored")
        x_loaded = [sem(f"x_loaded{k}") for k in range(KC)]
        ones_set = sem("ones_set")

        w_raw = [sem("w_raw0"), sem("w_raw1")]
        w_hi = sem("w_hi_split")
        w_lo = sem("w_lo_split")
        w_used = sem("w_used")
        evac = sem("evacuated")

        def split_hi(act, n, slot, load_no):
            act.wait_ge(w_raw[slot], 16 * load_no)
            nc.scalar.activation(wh[:, slot], wr[:, slot], ACT.Copy).then_inc(w_hi, 1)

        def split_lo(dve, n, slot):
            dve.wait_ge(w_hi, n + 1)
            nc.vector.tensor_tensor(wl[:, slot], wr[:, slot], wh[:, slot].bitcast(f32), ALU.subtract).then_inc(w_lo, 1)

        def three_pass(out, w_at, x_at, start, stop):
            for t, (w, x) in enumerate(((wh, xh), (wl, xh), (wh, xl))):
                last = nc.tensor.matmul(out, w_at(w), x_at(x), start=start and t == 0, stop=stop and t == 2)
            return last

        def bank(j):
            return ps[j // 4][:, j % 4]

        class Norm:
            def __init__(self, name, src, gain, split=True):
                self.src, self.gain, self.split = src, p_(gain), split
                self.sq, self.sum, self.stat = sem(name + "_squares"), sem(name + "_sums"), sem(name + "_stat")
                self.std, self.diag, self.bcast = sem(name + "_std"), sem(name + "_diag"), sem(name + "_bcast")
                self.xn, self.hi, self.lo = sem(name + "_scaled"), sem(name + "_hi"), sem(name + "_lo")
                self.rec = sem(name + "_rec")

            def act(self, act, ready):
                for k in range(KC):
                    ready(act, k)
                    if k >= 3:
                        act.wait_ge(self.sum, k - 2)
                    dst = TN[:, 0] if k == 0 else TN[:, 1 + k % 2]
                    nc.scalar.activation(dst, self.src(k), ACT.Square).then_inc(self.sq, 1)
                act.wait_ge(self.stat, 1)
                nc.scalar.activation(small[:, 0:QT], bank(0)[:, 0:QT], ACT.Identity, bias=eps[:, :], scale=1.0 / D)
                nc.scalar.activation(small[0:NS, QT:QT + 1], bank(0)[0:NS, QT:QT + 1], ACT.Identity, bias=eps[0:NS, :],
                                     scale=1.0 / D).then_inc(self.std, 1)
                if self.split:
                    for k in range(KC):
                        act.wait_ge(self.xn, k + 1)
                        nc.scalar.activation(xh[:, k], TN[:, 1 + k % 2], ACT.Copy).then_inc(self.hi, 1)

            def dve(self, dve):
                for k in range(1, KC):
                    dve.wait_ge(self.sq, k + 1)
                    if k > 1:
                        dve.wait_ge(self.sum, k - 1)
                    nc.vector.tensor_tensor(TN[:, 0], TN[:, 0], TN[:, 1 + k % 2], ALU.add).then_inc(self.sum, 1)
                dve.wait_ge(self.rec, 1)
                for t in range(QT):
                    nc.vector.tensor_scalar(TN[:, 0, t * P:(t + 1) * P], c_("ident"), small[:, 10 + t:11 + t], None, ALU.mult)
                nc.vector.tensor_scalar(diag_s[:, :], c_("ident", NS)[:, 0:NS], small[0:NS, 10 + QT:11 + QT], None,
                                        ALU.mult).then_inc(self.diag, 1)
                dve.wait_ge(self.bcast, 1)
                for k in range(KC):
                    if k >= 2:
                        self.wait_row(dve, k)
                    nc.vector.scalar_tensor_tensor(TN[:, 1 + k % 2], self.src(k), self.gain[:, k:k + 1], rstd_bc,
                                                   ALU.mult, ALU.mult).then_inc(self.xn, 1)
                    if self.split:
                        dve.wait_ge(self.hi, k + 1)
                        nc.vector.tensor_tensor(xl[:, k], TN[:, 1 + k % 2], xh[:, k].bitcast(f32),
                                                ALU.subtract).then_inc(self.lo, 1)

            def pool(self, pool):
                pool.wait_ge(self.std, 1)
                nc.gpsimd.tensor_tensor(small[:, 10:10 + QT], small[:, 0:QT], neghalf[:, 0:QT], ALU.pow)
                nc.gpsimd.tensor_tensor(small[0:NS, 10 + QT:11 + QT], small[0:NS, QT:QT + 1], neghalf[0:NS, 0:1],
                                        ALU.pow).then_inc(self.rec, 1)

            def wait_row(self, dve, k):
                if self.split:
                    dve.wait_ge(self.lo, k - 1)

            def pe(self, pe):
                pe.wait_ge(self.sum, KC - 1)
                for t in range(QT + 1):
                    w = P if t < QT else NS
                    last = nc.tensor.matmul(bank(0)[0:w, t:t + 1], TN[:, 0, t * P:t * P + w], ones[:, 0:1],
                                            start=True, stop=True)
                last.then_inc(self.stat, 1)
                pe.wait_ge(self.diag, 1)
                for t in range(QT + 1):
                    w = P if t < QT else NS
                    rhs = TN[:, 0, t * P:(t + 1) * P] if t < QT else diag_s[:, :]
                    last = nc.tensor.matmul(rstd_bc[:, t * P:t * P + w], ones[0:w, :], rhs, start=True, stop=True)
                last.then_inc(self.bcast, 1)

        rstd_bc = ps[1][:, :, :].rearrange("p a b -> p (a b)")[:, 0:NT]
        diag_s = sb("diag_s", [NS, NS])
        eps = sb("eps", [P, 1])
        neghalf = sb("neghalf", [P, QT])

        norm_mix = Norm("norm_mix", lambda k: Z[:, k], "g_mix")

        def project_pe(pe, n, slot, first):
            pe.wait_ge(w_lo, n + 1)
            if not first:
                pe.wait_ge(evac, n - 1)
            for c in range(3):
                for k in range(KC):
                    last = three_pass(ps[slot][:, c, 0:TC], lambda w: w[:, slot, k], lambda x: x[:, k, c * TC:(c + 1) * TC],
                                      k == 0, k == KC - 1)
            last.then_inc(w_used, 1)


        relu = TN[:, 0:2]
        CM = TN[:, 2, 0:SEQ]
        Pb = Z[:, QI:QI + 4].rearrange("p (a b) t -> p a b t", a=2)
        PT = Z[:, CV:CV + 2]
        junk = TN[:, 0, 0:NT // 2].bitcast(u16)
        ones16 = TN[:, 0, NT // 2:NT].bitcast(u16)
        ot, osq, yt = (TN[:, 1, a * 256:(a + 1) * 256] for a in range(3))

        v_tr, v_cp = sem("v_transposed"), sem("v_copied")
        masks_set = sem("masks_set")
        idx_mm, idx_relu, idx_acc = sem("idx_product"), sem("idx_relu"), sem("idx_sum")
        d_mixed, maps_mm, maps_cp = sem("pool_input"), sem("pool_mapped"), sem("pool_copied")
        lam_sum, lam_exp = sem("lambda_sums"), sem("lambda_exps")
        IDX = [(i, h) for i in TILES for h in range(IDXH)]

        def causal(i):
            return CM[:, SEQ - (i + 1) * P:SEQ]

        def scores(j):
            if j < len(TILES):
                i = TILES[j]
                return SC_AT[i], (i + 1) * P, P
            return SC_S, NK, NS

        ITEMS = [(kind, i, h) for kind in ("diff", "dsa") for i in range(QT) for h in range(4)]
        NI = len(ITEMS)

        def maps_of(n):
            return 2 if ITEMS[n][0] == "diff" else 1

        def unit(n, m=0):
            return sum(maps_of(a) for a in range(n)) + m

        def tile_no(n):
            return n // 4

        qk_mm = sem("logits_product")
        row_max = sem("logits_masked")
        neg_max = sem("negated_maxima")
        exp_done = sem("exponentials")
        combined = sem("maps_combined")
        p_tr = sem("probs_transposed")
        p_cp = sem("probs_copied")
        pv_mm = sem("values_product")
        ss_ready = sem("head_squares")
        head_rstd = sem("head_rstd")
        yt_ready = sem("tile_output")
        o_tr = sem("tile_transposed")
        o_cp = sem("tile_stored")

        def flat(pair, rows=slice(0, P)):
            return ps[pair // 2][rows, 2 * (pair % 2):2 * (pair % 2) + 2].rearrange("p a b -> p (a b)")

        def pe_values(pe):
            for t in range(QT + 1):
                w = P if t < QT else NS
                if t >= 2:
                    pe.wait_ge(v_cp, t - 1)
                for j in range(3):
                    last = nc.tensor.transpose(bank(6 + t % 2)[0:w, j * P:(j + 1) * P], Z[:, CV + j, t * P:t * P + w], c_("ident"))
                last.then_inc(v_tr, 1)

        def pe_idx(pe):
            for u, (i, h) in enumerate(IDX):
                if u >= 3:
                    pe.wait_ge(idx_relu, u - 2)
                half = slice(HD * (h % 2), HD * (h % 2) + HD)
                keys = KA if h % 2 else KB
                S = (i + 1) * P
                for a in range(0, S, 512):
                    w = min(512, S - a)
                    last = nc.tensor.matmul(flat(u % 3)[:, a:a + w], Z[half, QI + h // 2, i * P:(i + 1) * P],
                                            Z[half, keys, a:a + w], start=True, stop=True)
                last.then_inc(idx_mm, 1)

        def pe_maps(pe):
            pe.wait_ge(idx_relu, len(IDX))
            for c in range(2):
                pe.wait_ge(d_mixed, c + 1)
                for a in range(3):
                    last = nc.tensor.matmul(bank(3 * c + a)[:, 0:TC], p_("maps")[:, c * P:(c + 1) * P],
                                            Z[:, PV + c, a * TC:(a + 1) * TC], start=True, stop=True)
                last.then_inc(maps_mm, 1)

        def pe_item(pe, n):
            if n < NI:
                kind, i, h = ITEMS[n]
                S = (i + 1) * P
                for m in range(maps_of(n)):
                    u = unit(n, m)
                    if u >= 2:
                        pe.wait_ge(row_max, u - 1)
                    if kind == "diff":
                        r = HD * (h % 2) + 32 * m
                        part, q, k = slice(r, r + 32), DQ + h // 2, DK + h // 2
                    else:
                        part, q, k = slice(HD * (h % 2), HD * (h % 2) + HD), CQ + h // 2, KB if h % 2 else KA
                    for a in range(0, S, 512):
                        w = min(512, S - a)
                        last = nc.tensor.matmul(flat(u % 2)[:, a:a + w], Z[part, q, i * P:(i + 1) * P],
                                                Z[part, k, a:a + w], start=True, stop=True)
                    last.then_inc(qk_mm, 1)
            if 0 <= n - 2 < NI:
                kind, i, h = ITEMS[n - 2]
                pe.wait_ge(p_cp, n - 1)
                if h == 0 and tile_no(n - 2) >= 2:
                    pe.wait_ge(o_cp, tile_no(n - 2) - 1)
                v = P + HD * h if kind == "diff" else 0
                for b in range(i + 1):
                    last = nc.tensor.matmul(bank(6 + tile_no(n - 2) % 2)[:, h * HD:(h + 1) * HD], PT[:, n % 2, b * P:(b + 1) * P],
                                            vtok[:, b, v:v + HD], start=b == 0, stop=b == i)
                last.then_inc(pv_mm, 1)
            if 0 <= n - 1 < NI:
                kind, i, h = ITEMS[n - 1]
                pe.wait_ge(combined, n)
                if n >= 2:
                    pe.wait_ge(p_cp, n - 1)
                for b in range(i + 1):
                    last = nc.tensor.transpose(bank(4 + b // 4)[:, (b % 4) * P:(b % 4 + 1) * P],
                                               Pb[:, (n - 1) % 2, 0, b * P:(b + 1) * P], c_("ident"))
                last.then_inc(p_tr, 1)
            if 0 <= n - 4 < NI and ITEMS[n - 4][2] == 3:
                tile = tile_no(n - 4)
                pe.wait_ge(yt_ready, tile + 1)
                for j in range(2):
                    last = nc.tensor.transpose(bank(6 + tile % 2)[:, 256 + j * P:256 + (j + 1) * P], yt[:, j * P:(j + 1) * P], c_("ident"))
                last.then_inc(o_tr, 1)

        def act_values(act):
            for t in range(QT + 1):
                w = P if t < QT else NS
                act.wait_ge(v_tr, t + 1)
                nc.scalar.activation(vtok[0:w, t], bank(6 + t % 2)[0:w, 0:384], ACT.Copy).then_inc(v_cp, 1)

        def act_idx(act):
            for u, (i, h) in enumerate(IDX):
                S = (i + 1) * P
                act.wait_ge(idx_mm, u + 1)
                if u >= 2:
                    act.wait_ge(idx_acc, u - 1)
                nc.scalar.activation(relu[:, u % 2, 0:S], flat(u % 3)[:, 0:S], ACT.Relu, scale=IDX_SCALE).then_inc(idx_relu, 1)

        def act_lambda(act):
            act.wait_ge(lam_sum, 1)
            nc.scalar.activation(lamw[:, 2:4], lamw[:, 0:2], ACT.Exp).then_inc(lam_exp, 1)

        def act_maps(act):
            for c in range(2):
                act.wait_ge(maps_mm, c + 1)
                for a in range(3):
                    last = nc.scalar.activation(Z[:, GC + c, a * TC:(a + 1) * TC], bank(3 * c + a)[:, 0:TC], ACT.Copy,
                                                scale=p_("pool_scale")[:, c:c + 1])
                last.then_inc(maps_cp, 1)

        def act_item(act, n):
            if n < NI:
                kind, i, h = ITEMS[n]
                S = (i + 1) * P
                act.wait_ge(neg_max, n + 1)
                for m in range(maps_of(n)):
                    col = 2 * (n % 2) + m
                    nc.scalar.activation(Pb[:, n % 2, m, 0:S], Pb[:, n % 2, m, 0:S], ACT.Exp, bias=nm[:, col:col + 1],
                                         scale=DIFF_SCALE if kind == "diff" else DSA_SCALE,
                                         accum_out=sm[:, col:col + 1]).then_inc(exp_done, 1)
            if 0 <= n - 1 < NI:
                i = ITEMS[n - 1][1]
                act.wait_ge(p_tr, n)
                if n - 1 >= 2:
                    act.wait_ge(pv_mm, n - 2)
                for b in range(0, i + 1, 4):
                    w = min(4, i + 1 - b) * P
                    last = nc.scalar.activation(PT[:, (n - 1) % 2, b * P:b * P + w], bank(4 + b // 4)[:, 0:w], ACT.Copy)
                last.then_inc(p_cp, 1)
            if 0 <= n - 4 < NI and ITEMS[n - 4][2] == 3:
                kind, i, h = ITEMS[n - 4]
                tile = tile_no(n - 4)
                act.wait_ge(o_tr, tile + 1)
                for j in range(2):
                    src = bank(6 + tile % 2)[:, 256 + j * P:256 + (j + 1) * P]
                    dst = Z[:, (PV if kind == "diff" else GH) + j, i * P:(i + 1) * P]
                    last = nc.scalar.activation(dst, src, ACT.Copy, scale=subln[:, :] if kind == "diff" else 1.0)
                last.then_inc(o_cp, 1)

        subln = sb("subln", [P, 1])

        def dve_idx(dve):
            for u, (i, h) in enumerate(IDX):
                at, S = SC_AT[i], (i + 1) * P
                dve.wait_ge(idx_relu, u + 1)
                if u:
                    dve.wait_ge(idx_acc, u)
                before = causal(i) if h == 0 else SC[:, at:at + S]
                nc.vector.scalar_tensor_tensor(SC[:, at:at + S], relu[:, u % 2, 0:S], vtok[:, i, HD + h:HD + h + 1], before,
                                               ALU.mult, ALU.add).then_inc(idx_acc, 1)

        def dve_conv(dve, link, c):
            n = 2 + SEQ + DB * 6
            U, T = YF[:, 0:n], YF[:, n:2 * n]
            Us, Ts = (a[:, 2 + SEQ:n].rearrange("p (b t) -> p b t", t=6) for a in (U, T))
            st = p_("st_conv").rearrange("p (c b t) -> p c b t", c=2, t=2)[:, c]
            w = p_("conv_a")[:, 3 * c:3 * c + 3]
            tok = lambda slot: Z[:, slot, SEQ:NT].rearrange("p (b t) -> p b t", t=DT)
            nc.vector.memset(U[:, 0:2], 0.0)
            nc.vector.tensor_copy(Us[:, :, 0:2], st)
            nc.vector.tensor_tensor(U[:, 2:2 + SEQ], Z[:, GC + c, 0:SEQ], Z[:, GH + c, 0:SEQ], ALU.mult)
            link(nc.vector.tensor_tensor(Us[:, :, 2:6], tok(GC + c), tok(GH + c), ALU.mult))
            link(nc.vector.tensor_scalar(T[:, 0:n - 2], U[:, 0:n - 2], w[:, 0:1], None, ALU.mult))
            link(nc.vector.scalar_tensor_tensor(T[:, 0:n - 2], U[:, 1:n - 1], w[:, 1:2], T[:, 0:n - 2], ALU.mult, ALU.add))
            link(nc.vector.scalar_tensor_tensor(T[:, 0:n - 2], U[:, 2:n], w[:, 2:3], T[:, 0:n - 2], ALU.mult, ALU.add))
            nc.vector.tensor_tensor(Z[:, GB + c, 0:SEQ], Z[:, GB + c, 0:SEQ], T[:, 0:SEQ], ALU.mult)
            nc.vector.tensor_tensor(tok(GB + c), tok(GB + c), Ts[:, :, 0:DT], ALU.mult)
            nc.vector.tensor_copy(ST[:, c, 0, 0:2], U[:, SEQ:SEQ + 2])
            link(nc.vector.tensor_copy(ST[:, c, 1:1 + DB, 0:2], Us[:, :, 4:6]))

        def dve_pool(dve, link, c):
            n = 15 + SEQ + DB * 19
            E, A, B = (YF[:, a * n:(a + 1) * n] for a in range(3))
            s_of = lambda x: x[:, 15 + SEQ:n].rearrange("p (b t) -> p b t", t=19)
            tok = Z[:, PV + c, SEQ:NT].rearrange("p (b t) -> p b t", t=DT)
            nc.vector.memset(E[:, 0:15], 0.0)
            nc.vector.tensor_copy(s_of(E)[:, :, 0:15], p_("st_pool").rearrange("p (c b t) -> p c b t", c=2, t=15)[:, c])
            nc.vector.tensor_copy(E[:, 15:15 + SEQ], Z[:, PV + c, 0:SEQ])
            link(nc.vector.tensor_copy(s_of(E)[:, :, 15:19], tok))
            nc.vector.tensor_copy(ST[:, c, 0, 2:17], E[:, SEQ:SEQ + 15])
            nc.vector.tensor_copy(ST[:, c, 1:1 + DB, 2:17], s_of(E)[:, :, 4:19])

            def double(dst, src, step):
                link(nc.vector.tensor_tensor(dst[:, 0:n - 2 * step + 1], src[:, 0:n - 2 * step + 1],
                                             src[:, step:n - step + 1], ALU.add))

            def finish(half, sums, win):
                r = slice(HD * half, HD * half + HD)
                inv = c_("inv_w")[r, c:c + 1]
                off = 16 - win
                table = c_("inv_cnt")[r, 16 * c:16 * c + 16]
                link(nc.vector.tensor_tensor(small[r, 0:16], sums[r, off:off + 16], table, ALU.mult))
                nc.vector.scalar_tensor_tensor(Z[r, PV + c, 0:SEQ], sums[r, off:off + SEQ], inv, E[r, 15:15 + SEQ], ALU.mult, ALU.subtract)
                link(nc.vector.scalar_tensor_tensor(tok[r], s_of(sums)[r, :, off:off + DT], inv, s_of(E)[r, :, 15:19],
                                                    ALU.mult, ALU.subtract))
                return nc.vector.tensor_tensor(Z[r, PV + c, 0:16], small[r, 0:16], E[r, 15:31], ALU.subtract)

            double(A, E, 1)
            if c == 0:
                double(B, A, 2)
                finish(0, A, 2)
                last = finish(1, B, 4)
            else:
                double(B, A, 2)
                double(A, B, 4)
                double(B, A, 8)
                finish(0, A, 8)
                last = finish(1, B, 16)
            last.then_inc(d_mixed, 1)
            dve.wait_ge(d_mixed, c + 1)

        def dve_lambda(dve, link):
            lp = p_("lam")
            link(nc.vector.tensor_tensor_reduce(out=small[:, 0:32], in0=lp[:, 0:32], in1=lp[:, 32:64], scale=1.0, scalar=0.0,
                                                op0=ALU.mult, op1=ALU.add, accum_out=lamw[:, 0:1]))
            nc.vector.tensor_tensor_reduce(out=small[:, 0:32], in0=lp[:, 64:96], in1=lp[:, 96:128], scale=1.0, scalar=0.0,
                                           op0=ALU.mult, op1=ALU.add, accum_out=lamw[:, 1:2]).then_inc(lam_sum, 1)
            dve.wait_ge(lam_exp, 1)
            link(nc.vector.tensor_tensor(small[:, 32:33], lamw[:, 3:4], lamw[:, 2:3], ALU.subtract))
            link(nc.vector.tensor_scalar(small[:, 32:33], small[:, 32:33], -LAM_INIT, None, ALU.add))
            nc.vector.tensor_scalar(subln[:, :], p_("subln"), 1.0 - LAM_INIT, None, ALU.mult)
            link(nc.vector.scalar_tensor_tensor(small[:, 33:34], c_("lam_b"), small[:, 32:33], c_("lam_a"), ALU.mult, ALU.add))

        CNT, POS, SGN, KK, THI, CAND, GE, TLO, NEED, TMAG, THR = range(11)

        def col(a, j=None, rows=P):
            return tk[0:rows, a] if j is None else tk[0:rows, a, j:j + 1]

        def count(j, src, scalar, op, out=None):
            at, S, rows = scores(j)
            out = junk[0:rows, 0:S] if out is None else out
            scalar = scalar if type(scalar) is float else col(scalar, j, rows)
            return nc.vector.tensor_scalar(out, src[0:rows, at:at + S], scalar, 0.0, op, ALU.add, accum_out=col(CNT, j, rows))

        def top_prepare(dve, link):
            link(nc.vector.memset(tk[:, :, :], 0.0))
            for j in range(NTOP):
                link(count(j, SC, 0.0, ALU.is_ge))
            link(nc.vector.tensor_scalar(col(POS), col(CNT), float(TOPK), None, ALU.is_ge))
            link(nc.vector.tensor_scalar(col(SGN), col(POS), 2.0, -1.0, ALU.mult, ALU.add))
            link(nc.vector.tensor_tensor(col(KK), col(POS), c_("kdiff"), ALU.mult))
            link(nc.vector.tensor_tensor(col(KK), col(KK), c_("kneg"), ALU.add))
            y = TN[:, 0]
            for j in range(NTOP):
                at, S, rows = scores(j)
                link(nc.vector.tensor_scalar(y[0:rows, 0:S], SC[0:rows, at:at + S], col(SGN, j, rows), 0.0, ALU.mult, ALU.max))
                w, seen = (P, CP) if rows == P else (NS, newcp)
                link(nc.vector.tensor_tensor(y[0:rows, S - w:S], y[0:rows, S - w:S], seen[0:rows, :], ALU.min))
                halves = y.bitcast(u16)
                nc.vector.tensor_copy(y_hi[0:rows, at:at + S], halves[0:rows, 1:2 * S:2])
                link(nc.vector.tensor_copy(y_lo[0:rows, at:at + S], halves[0:rows, 0:2 * S:2]))

        def top_bit(dve, link, src, T, b):
            link(nc.vector.tensor_scalar(col(CAND), col(T), float(2 ** b), None, ALU.add))
            for j in range(NTOP):
                link(count(j, src, CAND, ALU.is_ge))
            link(nc.vector.tensor_tensor(col(GE), col(CNT), col(KK), ALU.is_ge))
            link(nc.vector.scalar_tensor_tensor(col(T), col(GE), float(2 ** b), col(T), ALU.mult, ALU.add))

        def top_middle(dve, link):
            for j in range(NTOP):
                at, S, rows = scores(j)
                link(count(j, y_hi, THI, ALU.is_gt))
                last = nc.vector.scalar_tensor_tensor(y_lo[0:rows, at:at + S], y_hi[0:rows, at:at + S], col(THI, j, rows),
                                                      y_lo[0:rows, at:at + S], ALU.is_equal, ALU.mult)
            link(last)
            link(nc.vector.tensor_tensor(col(KK), col(KK), col(CNT), ALU.subtract))

        def top_finish(dve, link):
            nc.vector.memset(ones16, 1.0)
            bits = col(TMAG).bitcast(u16)
            nc.vector.tensor_copy(bits[:, 1:2 * NTOP:2], col(THI))
            link(nc.vector.tensor_copy(bits[:, 0:2 * NTOP:2], col(TLO)))
            link(nc.vector.tensor_tensor(col(THR), col(TMAG), col(SGN), ALU.mult))
            for j in range(NTOP):
                at, S, rows = scores(j)
                count(j, SC, THR, ALU.is_gt, out=y_hi[0:rows, at:at + S])
                last = nc.vector.tensor_scalar(y_lo[0:rows, at:at + S], SC[0:rows, at:at + S], col(THR, j, rows), None, ALU.is_equal)
            link(last)
            link(nc.vector.tensor_scalar(col(NEED), col(CNT), -1.0, float(TOPK), ALU.mult, ALU.add))
            for j in range(NTOP):
                at, S, rows = scores(j)
                cols = (slice(0, rows), slice(at, at + S))
                link(nc.vector.tensor_tensor_scan(junk[0:rows, 0:S], ones16[0:rows, 0:S], y_lo[cols], 0.0, ALU.mult, ALU.add))
                link(nc.vector.scalar_tensor_tensor(y_lo[cols], junk[0:rows, 0:S], col(NEED, j, rows), y_lo[cols],
                                                    ALU.is_le, ALU.mult))
                link(nc.vector.scalar_tensor_tensor(SC[cols], y_hi[cols], -1.0, y_lo[cols], ALU.add, ALU.add))
                link(nc.vector.tensor_scalar(SC[cols], SC[cols], BIG, None, ALU.mult))

        def top_step(dve, link, n):
            if n == 0:
                top_prepare(dve, link)
            if n < 15:
                top_bit(dve, link, y_hi, THI, 14 - n)
            if n == 15:
                top_middle(dve, link)
            if 15 <= n < 31:
                top_bit(dve, link, y_lo, TLO, 30 - n)
            if n == 31:
                top_finish(dve, link)

        def dve_item(dve, link, n):
            if n < NI:
                kind, i, h = ITEMS[n]
                S = (i + 1) * P
                if n >= 2:
                    dve.wait_ge(p_tr, n - 1)
                if n == NI // 2:
                    link(nc.vector.tensor_copy(small[:, 34:35], small[:, 32:33]))
                for m in range(maps_of(n)):
                    u = unit(n, m)
                    dve.wait_ge(qk_mm, u + 1)
                    mask = causal(i) if kind == "diff" or i not in TILES else SC[:, SC_AT[i]:SC_AT[i] + S]
                    c = 2 * (n % 2) + m
                    nc.vector.tensor_tensor_reduce(out=Pb[:, n % 2, m, 0:S], in0=flat(u % 2)[:, 0:S], in1=mask, scale=1.0,
                                                   scalar=-3e38, op0=ALU.add, op1=ALU.max, accum_out=mx[:, c:c + 1]).then_inc(row_max, 1)
                dve.wait_ge(row_max, unit(n) + maps_of(n))
                c = 2 * (n % 2)
                nc.vector.tensor_scalar(nm[:, c:c + maps_of(n)], mx[:, c:c + maps_of(n)],
                                        -(DIFF_SCALE if kind == "diff" else DSA_SCALE), None, ALU.mult).then_inc(neg_max, 1)
            if 0 <= n - 1 < NI:
                kind, i, h = ITEMS[n - 1]
                S, c = (i + 1) * P, 2 * ((n - 1) % 2)
                dve.wait_ge(exp_done, unit(n - 1) + maps_of(n - 1))
                if kind == "diff":
                    link(nc.vector.reciprocal(cf[:, c:c + 2], sm[:, c:c + 2]))
                    link(nc.vector.tensor_tensor(cf[:, c + 1:c + 2], cf[:, c + 1:c + 2], small[:, 32:33], ALU.mult))
                    p0, p1 = (Pb[:, (n - 1) % 2, m, 0:S] for m in range(2))
                    link(nc.vector.tensor_scalar(p0, p0, cf[:, c:c + 1], None, ALU.mult))
                    nc.vector.scalar_tensor_tensor(p0, p1, cf[:, c + 1:c + 2], p0, ALU.mult, ALU.add).then_inc(combined, 1)
                else:
                    a = 4 * (i % 2) + h
                    nc.vector.reciprocal(rs4[:, a:a + 1], sm[:, c:c + 1]).then_inc(combined, 1)
            if 0 <= n - 3 < NI and ITEMS[n - 3][2] == 3:
                kind, i, h = ITEMS[n - 3]
                tile = tile_no(n - 3)
                dve.wait_ge(pv_mm, n - 2)
                if tile >= 1:
                    dve.wait_ge(o_tr, tile)
                o = bank(6 + tile % 2)[:, 0:256].rearrange("p (h d) -> p h d", d=HD)
                heads = lambda x: x.rearrange("p (h d) -> p h d", d=HD)
                if kind == "diff":
                    link(nc.vector.tensor_copy(heads(ot), o))
                    link(nc.vector.tensor_tensor(osq, ot, ot, ALU.mult))
                    link(nc.vector.tensor_reduce(rs4[:, 8:12], heads(osq), AX.X, ALU.add))
                    nc.vector.tensor_scalar(rs4[:, 12:16], rs4[:, 8:12], 1.0 / HD, EPS, ALU.mult, ALU.add).then_inc(ss_ready, 1)
                    dve.wait_ge(head_rstd, tile + 1)
                    nc.vector.tensor_tensor(heads(yt), heads(ot), rs4[:, 16:20].unsqueeze(2).to_broadcast([P, 4, HD]),
                                            ALU.mult).then_inc(yt_ready, 1)
                else:
                    a = 4 * (i % 2)
                    nc.vector.tensor_tensor(heads(yt), o, rs4[:, a:a + 4].unsqueeze(2).to_broadcast([P, 4, HD]),
                                            ALU.mult).then_inc(yt_ready, 1)


        ex = Z[:, DV + 1]
        qcz = ex[0:HD, 0:256].rearrange("p (b r) -> p b r", r=32)
        qdz = ex[:, 256:768].rearrange("p (c b r) -> p c b r", c=2, r=32)
        ka_new, dk_new = ex[:, 768:800], ex[:, 800:864].rearrange("p (c t) -> p c t", c=2)
        dring = [YF[:, 0:NPG * 512].rearrange("p (g c) -> p g c", c=512), SC[:, 0:NPG * 512].rearrange("p (g c) -> p g c", c=512)]
        cache_c = Z[:, 8:20].rearrange("p s t -> p (s t)")[:, 0:DB * NPG * 192].rearrange("p (b g c) -> p b g c", b=DB, c=192)
        td = TN[:, 2]
        maskd = TN[:, 1]
        PTd = Z[:, CV:CV + 2]
        PTc = PTd.rearrange("p a t -> p (a t)")[:, 0:(NPG + 1) * P]
        k_in = [sem("idx_pages0"), sem("idx_pages1")]
        d_in = [sem("diff_pages0"), sem("diff_pages1")]
        c_in, pt_in = sem("dsa_pages"), sem("page_table_loaded")
        zeroed, copied, wcol_mm, wsel_set = sem("sample_zeroed"), sem("sample_copied"), sem("wcol_product"), sem("wsel_set")
        sidx_mm, sidx_relu, sscore_mm, sscored = sem("sidx_product"), sem("sidx_relu"), sem("sscore_product"), sem("sample_scored")
        dqk_mm, dneg, dexp, dscaled = sem("dqk_product"), sem("dneg_max"), sem("dexp_done"), sem("dprobs_scaled")
        dp_tr, dp_cp, dpv_mm, dpv_cp = sem("dprobs_transposed"), sem("dprobs_copied"), sem("dvalues_product"), sem("dvalues_copied")
        dsq, dsum_mm, dmean, drstd, dy = sem("dhead_squares"), sem("dhead_sums"), sem("dhead_means"), sem("dhead_rstd"), sem("dhead_out")
        rep_mm, rep_cp, cqk_mm, cneg, cexp = sem("mask_spread"), sem("mask_copied"), sem("cqk_product"), sem("cneg_max"), sem("cexp_done")
        cscaled, cp_tr, cp_cp, cpv_mm, cpv_cp = (sem("cprobs_scaled"), sem("cprobs_transposed"), sem("cprobs_copied"),
                                                 sem("cvalues_product"), sem("cvalues_copied"))
        COLS = [(0, 512), (512, 512), (1024, NS)]
        samples = lambda a: a[:, SEQ:NT].rearrange("p (b t) -> p b t", t=DT)

        def three(first, rows=slice(0, P)):
            return ps[first // 4][rows, first % 4:first % 4 + 3].rearrange("p a b -> p (a b)")[:, 0:NK]

        def load_page(sp, dst, src_of, no, done):
            page = sp.value_load(ptab[0:1, bass.ds(no, 1)], min_val=0, max_val=d["c_pages"].shape[0] - 1)
            sp.dma_start(dst, src_of(bass.ds(page, 1))).then_inc(done, 16)

        def sp_idx_pages(sp):
            sp.wait_ge(pt_in, 16)
            sp.wait_ge(w_used, NZ)
            for b in range(DB):
                if b >= 2:
                    sp.wait_ge(sidx_mm, b - 1)
                for g in range(NPG):
                    load_page(sp, kring[:, b % 2, g], lambda i: d["c_pages"][i, :, 0:P].rearrange("o p c -> p (o c)"),
                              b * NPG + g, k_in[b % 2])

        def sp_diff_pages(sp):
            for b in range(DB):
                if b == 0:
                    sp.wait_ge(row_max, unit(NI // 2) + 4 * (TOPK // P) + 1)
                if b == 1:
                    sp.wait_ge(row_max, unit(NI - 1) + 1)
                if b >= 2:
                    sp.wait_ge(dpv_mm, b - 1)
                for g in range(NPG):
                    load_page(sp, dring[b % 2][:, g], lambda i: d["d_pages"][i].rearrange("o p c -> p (o c)"),
                              b * NPG + g, d_in[b % 2])

        def sp_dsa_pages(sp):
            sp.wait_ge(pv_mm, NI)
            sp.wait_ge(copied, 4)
            for b in range(DB):
                for g in range(NPG):
                    load_page(sp, cache_c[:, b, g], lambda i: d["c_pages"][i].rearrange("o p c -> p (o c)"),
                              b * NPG + g, c_in)

        def act_sample_copies(act):
            act.wait_ge(zeroed, 1)
            act.wait_ge(outs_stored, 16 * 7)
            for h in range(IDXH):
                half = slice(HD * (h % 2), HD * (h % 2) + HD)
                last = nc.scalar.activation(qis[HD:P, :, h], samples(Z[half, QI + h // 2]), ACT.Copy)
            last.then_inc(copied, 1)
            for h in range(4):
                half = slice(HD * (h % 2), HD * (h % 2) + HD)
                for par in range(2):
                    last = nc.scalar.activation(qcz[:, par:DB:2, par * 16 + h * 4:par * 16 + h * 4 + 4],
                                                samples(Z[half, CQ + h // 2])[:, par:DB:2], ACT.Copy)
            last.then_inc(copied, 1)
            for c in range(2):
                for r in range(4):
                    part = slice(32 * r, 32 * r + 32)
                    at = 16 * c + 4 * r
                    last = nc.scalar.activation(qdz[part, c, :, at:at + 4], samples(Z[part, DQ + c]), ACT.Copy)
            last.then_inc(copied, 1)
            nc.scalar.activation(ka_new, Z[:, KA, SEQ:NT], ACT.Copy)
            nc.scalar.activation(dk_new, Z[:, DK:DK + 2, SEQ:NT], ACT.Copy).then_inc(copied, 1)

        def pe_wcol(pe):
            for g in range(2):
                last = nc.tensor.matmul(bank(7)[:, 8 * g:8 * g + 8], c_(f"e{g}", NS), vtok[0:NS, QT, HD:HD + 8], start=True, stop=True)
            last.then_inc(wcol_mm, 1)

        def dve_wsel(dve, link):
            dve.wait_ge(wcol_mm, 1)
            for g in range(2):
                link(nc.vector.tensor_tensor_reduce(out=small[:, 20:28], in0=bank(7)[:, 8 * g:8 * g + 8], in1=c_("hsel"), scale=1.0,
                                                    scalar=0.0, op0=ALU.mult, op1=ALU.add, accum_out=wcol[:, g:g + 1]))
                nc.vector.tensor_scalar(wsel[:, g], c_(f"sel{g}"), wcol[:, g:g + 1], None, ALU.mult).then_inc(wsel_set, 1)

        def pe_sidx(pe):
            pe.wait_ge(copied, 1)
            pe.wait_ge(idx_relu, len(IDX))
            for b in range(DB):
                pe.wait_ge(k_in[b % 2], 16 * NPG * (b // 2 + 1))
                g, r = b // 4, 32 * (b % 4)
                for j, (a, w) in enumerate(COLS):
                    keys = kring[HD:P, b % 2].rearrange("p g c -> p (g c)")[:, a:a + w] if j < 2 else Z[HD:P, KA, SEQ:NT]
                    last = nc.tensor.matmul(bank(3 * g + j)[r:r + 32, 0:w], qis[HD:P, b].rearrange("p h t -> p (h t)"), keys, start=True, stop=True)
                last.then_inc(sidx_mm, 1)
            pe.wait_ge(wsel_set, 2)
            pe.wait_ge(sidx_relu, 2)
            for j, (a, w) in enumerate(COLS):
                out = bank((6, 7, 0)[j])[0:NS, 0:w]
                for g in range(2):
                    last = nc.tensor.matmul(out, wsel[:, g], relu[:, g, a:a + w], start=g == 0, stop=g == 1)
            last.then_inc(sscore_mm, 1)

        def act_sidx(act):
            act.wait_ge(idx_acc, len(IDX))
            for g in range(2):
                act.wait_ge(sidx_mm, 4 * g + 4)
                for j, (a, w) in enumerate(COLS):
                    last = nc.scalar.activation(relu[:, g, a:a + w], bank(3 * g + j)[:, 0:w], ACT.Relu, scale=IDX_SCALE)
                last.then_inc(sidx_relu, 1)

        def dve_sscore(dve):
            dve.wait_ge(sscore_mm, 1)
            for j, (a, w) in enumerate(COLS[:2]):
                nc.vector.tensor_copy(SC[0:NS, SC_S + a:SC_S + a + w], bank(6 + j)[0:NS, 0:w])
            nc.vector.tensor_tensor(SC[0:NS, SC_S + PAST:SC_N], bank(0)[0:NS, 0:NS], c_("newmask", NS), ALU.add).then_inc(sscored, 1)

        def pe_sdiff(pe, b):
            if b < DB:
                pe.wait_ge(d_in[b % 2], 16 * NPG * (b // 2 + 1))
                if b >= 2:
                    pe.wait_ge(dneg, b - 1)
                for j, (a, w) in enumerate(COLS):
                    for c in range(2):
                        keys = dring[b % 2][:, 4 * j:4 * j + 4, c * P:(c + 1) * P] if j < 2 else dk_new[:, c]
                        last = nc.tensor.matmul(bank(4 * (b % 2) + j)[0:32, 0:w], qdz[:, c, b], keys, start=c == 0, stop=c == 1)
                last.then_inc(dqk_mm, 1)
            if b >= 1:
                e = b - 1
                pe.wait_ge(dscaled, e + 1)
                if e >= 1:
                    pe.wait_ge(dp_cp, e)
                for g in range(NPG + 1):
                    w = P if g < NPG else NS
                    last = nc.tensor.transpose(bank(3)[0:w, g * 32:g * 32 + 32], TN[0:32, e % 2, g * P:g * P + w], c_("ident", 32)[:, 0:32])
                last.then_inc(dp_tr, 1)
                pe.wait_ge(dp_cp, e + 1)
                for c in range(2):
                    for g in range(NPG + 1):
                        v = dring[e % 2][:, g, 256 + c * P:256 + (c + 1) * P] if g < NPG else vtok[0:NS, QT, P + c * P:P + (c + 1) * P]
                        rows = P if g < NPG else NS
                        at = e * 64 + c * 32
                        last = nc.tensor.matmul(bank(7)[:, at:at + 32], v, PTd[0:rows, e % 2, g * 32:g * 32 + 32], start=g == 0, stop=g == NPG)
                last.then_inc(dpv_mm, 1)

        def dve_sdiff(dve, link, b):
            if b < DB:
                p = TN[0:32, b % 2]
                dve.wait_ge(dqk_mm, b + 1)
                if b >= 2:
                    dve.wait_ge(dp_tr, b - 1)
                src = three(4 * (b % 2), slice(0, 32))
                link(nc.vector.tensor_copy(p[:, 0:PAST], src[:, 0:PAST]))
                link(nc.vector.tensor_tensor(p[:, PAST:NK], src[:, PAST:NK], c_("dmask", NS)[:, b * NS:(b + 1) * NS], ALU.add))
                link(nc.vector.tensor_reduce(small[0:32, 20:21], p, AX.X, ALU.max))
                nc.vector.tensor_scalar(small[0:32, 22 + b % 2:23 + b % 2], small[0:32, 20:21], -DIFF_SCALE, None, ALU.mult).then_inc(dneg, 1)
            if b >= 1:
                e = b - 1
                dve.wait_ge(dexp, e + 1)
                k = small[0:32, 26 + e % 2:27 + e % 2]
                link(nc.vector.reciprocal(k, small[0:32, 24 + e % 2:25 + e % 2]))
                link(nc.vector.tensor_tensor(k, k, small[0:32, 33:34], ALU.mult))
                nc.vector.tensor_scalar(TN[0:32, e % 2], TN[0:32, e % 2], k, None, ALU.mult).then_inc(dscaled, 1)

        def act_sdiff(act, b):
            if b < DB:
                act.wait_ge(dneg, b + 1)
                nc.scalar.activation(TN[0:32, b % 2], TN[0:32, b % 2], ACT.Exp, bias=small[0:32, 22 + b % 2:23 + b % 2], scale=DIFF_SCALE,
                                     accum_out=small[0:32, 24 + b % 2:25 + b % 2]).then_inc(dexp, 1)
            if b >= 1:
                e = b - 1
                act.wait_ge(dp_tr, e + 1)
                if e >= 2:
                    act.wait_ge(dpv_mm, e - 1)
                nc.scalar.activation(PTd[:, e % 2, 0:NPG * 32], bank(3)[:, 0:NPG * 32], ACT.Copy)
                nc.scalar.activation(PTd[0:NS, e % 2, NPG * 32:NPG * 32 + 32], bank(3)[0:NS, NPG * 32:NPG * 32 + 32], ACT.Copy).then_inc(dp_cp, 1)

        def act_sdiff_tail(act):
            act.wait_ge(dpv_mm, DB)
            nc.scalar.activation(td[:, 0:512], bank(7)[:, 0:512], ACT.Copy).then_inc(dpv_cp, 1)
            act.wait_ge(dsum_mm, 1)
            nc.scalar.activation(td[:, 640:704], bank(3)[:, 0:64], ACT.Identity, bias=eps[:, :], scale=1.0 / HD).then_inc(dmean, 1)

        def dve_sdiff_tail(dve, link):
            dve.wait_ge(dpv_cp, 1)
            O = td[:, 0:512].rearrange("p (b c r) -> p c b r", b=DB, c=2)
            od = td[:, 512:576].rearrange("p (c b t) -> p c b t", c=2, t=DT)
            for h in range(4):
                c, half = h // 2, slice(HD * (h % 2), HD * (h % 2) + HD)
                last = nc.vector.tensor_tensor(od[half, c], O[half, c, :, 8 * h:8 * h + 4], O[half, c, :, 8 * h + 4:8 * h + 8], ALU.add)
            link(last)
            nc.vector.tensor_tensor(td[:, 576:640], td[:, 512:576], td[:, 512:576], ALU.mult).then_inc(dsq, 1)
            dve.wait_ge(drstd, 1)
            for c in range(2):
                nc.vector.scalar_tensor_tensor(Z[:, PV + c, SEQ:NT], td[:, 512 + 32 * c:544 + 32 * c], subln[:, :],
                                               td[:, 704 + 32 * c:736 + 32 * c], ALU.mult, ALU.mult).then_inc(dy, 1)

        def pool_sdiff_tail(pool):
            pool.wait_ge(dmean, 1)
            nc.gpsimd.tensor_tensor(td[:, 704:768], td[:, 640:704], neghalf[:, 0:1].to_broadcast([P, 64]), ALU.pow).then_inc(drstd, 1)

        def pe_sdiff_tail(pe):
            pe.wait_ge(dsq, 1)
            nc.tensor.matmul(bank(3)[:, 0:64], c_("headones"), td[:, 576:640], start=True, stop=True).then_inc(dsum_mm, 1)

        def pe_sdsa(pe):
            pe.wait_ge(dneg, DB)
            for j, (a, w) in enumerate(COLS):
                last = nc.tensor.matmul(bank(4 + j)[:, 0:w], c_("rep", NS), SC[0:NS, SC_S + a:SC_S + a + w], start=True, stop=True)
            last.then_inc(rep_mm, 1)
            pe.wait_ge(c_in, 16 * DB * NPG)
            for j, (a, w) in enumerate(COLS):
                for b in range(DB):
                    r = 32 * (b // 2)
                    keys = cache_c[0:HD, b, 4 * j:4 * j + 4, 0:P] if j < 2 else ka_new[0:HD, :]
                    last = nc.tensor.matmul(bank(j)[r:r + 32, 0:w], qcz[:, b], keys, start=b % 2 == 0, stop=b % 2 == 1)
            last.then_inc(cqk_mm, 1)
            pe.wait_ge(cscaled, 1)
            for g in range(NPG + 1):
                w = P if g < NPG else NS
                last = nc.tensor.transpose(bank(4 + g // 4)[0:w, (g % 4) * P:(g % 4 + 1) * P], TN[:, 0, g * P:g * P + w], c_("ident"))
            last.then_inc(cp_tr, 1)
            pe.wait_ge(cp_cp, 1)
            for b in range(DB):
                for g in range(NPG + 1):
                    v = cache_c[:, b, g, P:P + HD] if g < NPG else vtok[0:NS, QT, 0:HD]
                    rows = P if g < NPG else NS
                    last = nc.tensor.matmul(bank(0)[0:HD, b * 16:b * 16 + 16], v, PTc[0:rows, g * P + b * 16:g * P + b * 16 + 16],
                                            start=g == 0, stop=g == NPG)
            last.then_inc(cpv_mm, 1)

        def act_sdsa(act):
            act.wait_ge(rep_mm, 1)
            act.wait_ge(dp_tr, DB)
            nc.scalar.activation(maskd[:, 0:NK], three(4), ACT.Copy).then_inc(rep_cp, 1)
            act.wait_ge(cneg, 1)
            nc.scalar.activation(TN[:, 0], TN[:, 0], ACT.Exp, bias=small[:, 29:30], scale=DSA_SCALE, accum_out=small[:, 30:31]).then_inc(cexp, 1)
            act.wait_ge(cp_tr, 1)
            act.wait_ge(dpv_mm, DB)
            nc.scalar.activation(PTc[:, 0:NPG * P], ps[1][:, 0:2].rearrange("p a b -> p (a b)"), ACT.Copy)
            nc.scalar.activation(PTc[0:NS, NPG * P:(NPG + 1) * P], bank(6)[0:NS, 0:P], ACT.Copy).then_inc(cp_cp, 1)
            act.wait_ge(cpv_mm, 1)
            o = bank(0)[0:HD, 0:P].rearrange("p (b h t) -> p h b t", b=DB, h=4)
            for h in range(4):
                half = slice(HD * (h % 2), HD * (h % 2) + HD)
                last = nc.scalar.activation(samples(Z[half, GH + h // 2]), o[:, h], ACT.Copy)
            last.then_inc(cpv_cp, 1)

        def dve_sdsa(dve, link):
            dve.wait_ge(rep_cp, 1)
            dve.wait_ge(cqk_mm, 1)
            link(nc.vector.tensor_tensor_reduce(out=TN[:, 0], in0=three(0), in1=maskd[:, 0:NK], scale=1.0, scalar=-3e38,
                                                op0=ALU.add, op1=ALU.max, accum_out=small[:, 28:29]))
            nc.vector.tensor_scalar(small[:, 29:30], small[:, 28:29], -DSA_SCALE, None, ALU.mult).then_inc(cneg, 1)
            dve.wait_ge(cexp, 1)
            link(nc.vector.reciprocal(small[:, 31:32], small[:, 30:31]))
            nc.vector.tensor_scalar(TN[:, 0], TN[:, 0], small[:, 31:32], None, ALU.mult).then_inc(cscaled, 1)


        H = Z[:, 8:16]
        W_OUT = NZ
        W_FF = W_OUT + KC
        W_PLE = W_FF + 3 * FC
        W_PG = W_PLE + 2
        EXT = 2 + SEQ + DB * 6
        tail = Z[:, 16:23].rearrange("p s t -> p (s t)")
        ge = [tail[:, a * EXT:(a + 1) * EXT] for a in range(2)]
        gv = [tail[:, a * EXT:(a + 1) * EXT] for a in range(2, 4)]
        gu = [tail[:, 4 * EXT + a * NT:4 * EXT + (a + 1) * NT] for a in range(2)]
        st_in = tail[:, 4 * EXT + 2 * NT:][:, 0:FC * DB * 2].rearrange("p (f b t) -> p f b t", f=FC, b=DB)
        st_out = TN[:, 2, 0:FC * 9 * 2].rearrange("p (f b t) -> p f b t", f=FC, b=1 + DB)
        GROUPS = FC // 2
        y_hi_cp, y_lo_cp = sem("mixer_hi"), sem("mixer_lo")
        x_again = [sem(f"x_again{k}") for k in range(KC)]
        h_out = sem("residual_mixed")
        st_loaded, st_stored = sem("ffn_state_loaded"), sem("ffn_state_stored")
        g_cp = sem("gate_copied")
        g_conv = sem("gate_convolved")
        g_silu = sem("gate_silu")
        act_mul = sem("gate_times_up")
        a_hi, a_lo = sem("mlp_hi"), sem("mlp_lo")
        d_mm, h_ffn = sem("down_product"), sem("residual_mlp")
        p_in, p_hi, p_lo = sem("ple_loaded"), sem("ple_hi"), sem("ple_lo")
        ple_mm, ple_cp = sem("ple_product"), sem("ple_copied")
        s_gate, h_ple = sem("ple_gate"), sem("residual_ple")
        mix_stored = sem("mixer_state_stored")
        y_rows = [sem("y_row0"), sem("y_row1")]
        PP = [Z[:, s] for s in (0, 1, 4, 5, 18, 19, 20, 21)]
        norm_ffn = Norm("norm_ffn", lambda k: H[:, k], "g_ffn")
        norm_ple = Norm("norm_ple", lambda k: H[:, k], "g_ple")
        norm_final = Norm("norm_final", lambda k: H[:, k], "g_final", split=False)

        def hi_next(act, n, load_no=None):
            split_hi(act, n, n % 2, n // 2 + 1 if load_no is None else load_no)

        def act_mixers(act):
            act.wait_ge(cpv_mm, 1)
            act.wait_ge(cpv_cp, 1)
            act.wait_ge(dy, 2)
            for k in range(KC):
                nc.scalar.activation(xh[:, k], Z[:, k], ACT.Copy).then_inc(y_hi_cp, 1)

        def dve_mixers(dve):
            for k in range(KC):
                dve.wait_ge(y_hi_cp, k + 1)
                nc.vector.tensor_tensor(xl[:, k], Z[:, k], xh[:, k].bitcast(f32), ALU.subtract).then_inc(y_lo_cp, 1)

        def pool_reload(pool):
            pool.wait_ge(cpv_mm, 1)
            for k in range(KC):
                pool.dma_start(H[:, k], d["xT"][k]).then_inc(x_again[k], 16)

        def pe_out(pe):
            pe.wait_ge(y_lo_cp, KC)
            pe.wait_ge(cpv_cp, 1)
            for m in range(KC):
                n = W_OUT + m
                pe.wait_ge(w_lo, n + 1)
                if m >= 2:
                    pe.wait_ge(h_out, m - 1)
                block_product(n).then_inc(w_used, 1)

        def block_product(n):
            slot = n % 2
            for c in range(3):
                for k in range(KC):
                    last = three_pass(ps[slot][:, c, 0:TC], lambda w: w[:, slot, k], lambda x: x[:, k, c * TC:(c + 1) * TC],
                                      k == 0, k == KC - 1)
            return last

        def act_out(act):
            for m in range(KC):
                act.wait_ge(w_used, W_OUT + m + 1)
                hi_next(act, W_OUT + m + 2)

        def by_bank(a):
            return a.rearrange("p (c t) -> p c t", c=3)

        def dve_out(dve):
            for m in range(KC):
                dve.wait_ge(w_used, W_OUT + m + 1)
                dve.wait_ge(x_again[m], 16)
                nc.vector.tensor_tensor(by_bank(H[:, m]), by_bank(H[:, m]), ps[(W_OUT + m) % 2][:, 0:3, 0:TC], ALU.add).then_inc(h_out, 1)
                split_lo(dve, W_OUT + m + 2, (W_OUT + m) % 2)

        def gate_block(f):
            g, q = divmod(f, 2)
            return W_FF + (0 if g == 0 else 6 * g - 2) + 2 * q

        def down_block(g):
            return W_FF + (6 * g + 8 if g < GROUPS - 1 else 6 * g + 4)

        def used_before(n):
            return n + 1 - sum(1 for g in range(GROUPS) for half in range(2) if down_block(g) + half <= n)

        def pe_gate_up(pe, g):
            for f in (2 * g, 2 * g + 1):
                n = gate_block(f)
                pe.wait_ge(w_lo, n + 1)
                if f:
                    pe.wait_ge(g_cp, f)
                block_product(n).then_inc(w_used, 1)
                pe.wait_ge(w_lo, n + 2)
                if f:
                    pe.wait_ge(act_mul, f)
                block_product(n + 1).then_inc(w_used, 1)

        def pe_down(pe, g):
            pe.wait_ge(a_lo, 2 * g + 2)
            for m in range(KC):
                n = down_block(g) + m // 4
                if m % 4 == 0:
                    pe.wait_ge(w_lo, n + 1)
                for c in range(3):
                    v = (g * KC + m) * 3 + c
                    if v >= 2:
                        pe.wait_ge(h_ffn, v - 1)
                    for q in range(2):
                        for t, (w, x) in enumerate(((wh, ah), (wl, ah), (wh, al))):
                            last = nc.tensor.matmul(bank(3 + 4 * (v % 2))[:, 0:TC], w[:, n % 2, 4 * q + m % 4],
                                                    x[:, g % 2, q, c * TC:(c + 1) * TC], start=q == 0 and t == 0, stop=q == 1 and t == 2)
                    last.then_inc(d_mm, 1)

        def act_gate_up(act, g):
            for f in (2 * g, 2 * g + 1):
                n = gate_block(f)
                act.wait_ge(w_used, used_before(n))
                hi_next(act, n + 2)
                if f >= 2:
                    act.wait_ge(g_conv, f - 1)
                e, gate = ge[f % 2], ps[n % 2]
                nc.scalar.activation(e[:, 2:2 + 2 * TC].rearrange("p (c t) -> p c t", c=2), gate[:, 0:2, 0:TC], ACT.Copy)
                nc.scalar.activation(e[:, 2 + 2 * TC:2 + SEQ], gate[:, 2, 0:SEQ - 2 * TC], ACT.Copy)
                nc.scalar.activation(e[:, 2 + SEQ:].rearrange("p (b t) -> p b t", t=6)[:, :, 2:6],
                                     gate[:, 2, SEQ - 2 * TC:TC].rearrange("p (b t) -> p b t", t=DT), ACT.Copy).then_inc(g_cp, 1)
                act.wait_ge(g_conv, f + 1)
                nc.scalar.activation(gv[f % 2][:, 0:EXT - 2], gv[f % 2][:, 0:EXT - 2], ACT.Silu).then_inc(g_silu, 1)
                act.wait_ge(w_used, used_before(n + 1))
                hi_next(act, n + 3)
                act.wait_ge(act_mul, f + 1)
                if g >= 2:
                    act.wait_ge(d_mm, (g - 1) * KC * 3)
                nc.scalar.activation(ah[:, g % 2, f % 2], gu[f % 2], ACT.Copy).then_inc(a_hi, 1)

        def act_down(act, g):
            for half in range(2):
                act.wait_ge(d_mm, g * KC * 3 + 12 * (half + 1))
                if down_block(g) + half + 2 < NW_USED:
                    hi_next(act, down_block(g) + half + 2)

        def dve_gate_up(dve, link, g):
            for f in (2 * g, 2 * g + 1):
                n = gate_block(f)
                split_lo(dve, n + 2, n % 2)
                e, v = ge[f % 2], gv[f % 2]
                es = e[:, 2 + SEQ:].rearrange("p (b t) -> p b t", t=6)
                if f < 2:
                    nc.vector.memset(e[:, 0:2], 0.0)
                nc.vector.tensor_copy(es[:, :, 0:2], st_in[:, f])
                dve.wait_ge(g_cp, f + 1)
                nc.vector.tensor_copy(st_out[:, f, 0], e[:, SEQ:SEQ + 2])
                link(nc.vector.tensor_copy(st_out[:, f, 1:], es[:, :, 4:6]))
                w = p_("conv_ffn")[:, 3 * f:3 * f + 3]
                link(nc.vector.tensor_scalar(v[:, 0:EXT - 2], e[:, 0:EXT - 2], w[:, 0:1], None, ALU.mult))
                link(nc.vector.scalar_tensor_tensor(v[:, 0:EXT - 2], e[:, 1:EXT - 1], w[:, 1:2], v[:, 0:EXT - 2], ALU.mult, ALU.add))
                nc.vector.scalar_tensor_tensor(v[:, 0:EXT - 2], e[:, 2:EXT], w[:, 2:3], v[:, 0:EXT - 2], ALU.mult, ALU.add).then_inc(g_conv, 1)
                split_lo(dve, n + 3, (n + 1) % 2)
                dve.wait_ge(g_silu, f + 1)
                up, u = ps[(n + 1) % 2], gu[f % 2]
                nc.vector.tensor_tensor(u[:, 0:2 * TC].rearrange("p (c t) -> p c t", c=2), v[:, 0:2 * TC].rearrange("p (c t) -> p c t", c=2),
                                        up[:, 0:2, 0:TC], ALU.mult)
                nc.vector.tensor_tensor(u[:, 2 * TC:SEQ], v[:, 2 * TC:SEQ], up[:, 2, 0:SEQ - 2 * TC], ALU.mult)
                nc.vector.tensor_tensor(u[:, SEQ:NT].rearrange("p (b t) -> p b t", t=DT),
                                        v[:, 2 + SEQ:EXT].rearrange("p (b t) -> p b t", t=6)[:, :, 0:DT],
                                        up[:, 2, SEQ - 2 * TC:TC].rearrange("p (b t) -> p b t", t=DT), ALU.mult).then_inc(act_mul, 1)
                dve.wait_ge(a_hi, f + 1)
                nc.vector.tensor_tensor(al[:, g % 2, f % 2], u, ah[:, g % 2, f % 2].bitcast(f32), ALU.subtract).then_inc(a_lo, 1)

        def dve_down(dve, g):
            for m in range(KC):
                for c in range(3):
                    v = (g * KC + m) * 3 + c
                    dve.wait_ge(d_mm, v + 1)
                    if v >= KC * 3:
                        dve.wait_ge(h_ffn, v + 1 - KC * 3)
                    cols = H[:, m, c * TC:(c + 1) * TC]
                    nc.vector.tensor_tensor(cols, cols, bank(3 + 4 * (v % 2))[:, 0:TC], ALU.add).then_inc(h_ffn, 1)
                if m % 4 == 3 and down_block(g) + m // 4 + 2 < NW_USED:
                    split_lo(dve, down_block(g) + m // 4 + 2, (down_block(g) + m // 4) % 2)

        ALL_FF = GROUPS * KC * 3

        def pool_ple(pool):
            pool.wait_ge(act_mul, FC)
            pool.wait_ge(a_lo, FC)
            for k in range(2):
                pool.dma_start(Z[:, 16 + k], d["pT"][k]).then_inc(p_in, 16)
            pool.dma_start(d["st_ffn"], st_out).then_inc(st_stored, 16)

        def act_ple_split(act):
            act.wait_ge(p_in, 32)
            act.wait_ge(d_mm, ALL_FF)
            for k in range(2):
                nc.scalar.activation(ah[:, 1, k], Z[:, 16 + k], ACT.Copy).then_inc(p_hi, 1)

        def dve_ple_split(dve):
            for k in range(2):
                dve.wait_ge(p_hi, k + 1)
                nc.vector.tensor_tensor(al[:, 1, k], Z[:, 16 + k], ah[:, 1, k].bitcast(f32), ALU.subtract).then_inc(p_lo, 1)

        def pe_ple(pe):
            pe.wait_ge(p_lo, 2)
            pe.wait_ge(h_ffn, ALL_FF)
            for m in range(KC):
                n = W_PLE + m // 4
                pe.wait_ge(w_lo, n + 1)
                for c in range(3):
                    v = 3 * m + c
                    if v >= 2:
                        pe.wait_ge(ple_cp, v - 1)
                    for q in range(2):
                        for t, (w, x) in enumerate(((wh, ah), (wl, ah), (wh, al))):
                            last = nc.tensor.matmul(bank(3 + 4 * (v % 2))[:, 0:TC], w[:, n % 2, 4 * q + m % 4],
                                                    x[:, 1, q, c * TC:(c + 1) * TC], start=q == 0 and t == 0, stop=q == 1 and t == 2)
                    last.then_inc(ple_mm, 1)

        def act_ple(act):
            for m in range(KC):
                for c in range(3):
                    v = 3 * m + c
                    act.wait_ge(ple_mm, v + 1)
                    nc.scalar.activation(PP[m][:, c * TC:(c + 1) * TC], bank(3 + 4 * (v % 2))[:, 0:TC], ACT.Copy).then_inc(ple_cp, 1)
                if m % 4 == 3:
                    hi_next(act, W_PLE + m // 4 + 2)

        def pe_ple_gate(pe):
            pe.wait_ge(norm_ple.lo, KC)
            for m in range(KC):
                pe.wait_ge(w_lo, W_PG + m + 1)
                if m >= 2:
                    pe.wait_ge(s_gate, m - 1)
                block_product(W_PG + m).then_inc(w_used, 1)

        def act_ple_gate(act):
            for m in range(KC):
                act.wait_ge(w_used, used_before(W_PLE - 1) + m + 1)
                if m + 2 < KC:
                    hi_next(act, W_PG + m + 2)
                if m >= 2:
                    act.wait_ge(h_ple, m - 1)
                nc.scalar.activation(by_bank(TN[:, 1 + m % 2]), ps[(W_PG + m) % 2][:, 0:3, 0:TC], ACT.Sigmoid).then_inc(s_gate, 1)

        def dve_ple_gate(dve, link):
            for m in range(KC):
                if m + 2 < KC:
                    split_lo(dve, W_PG + m + 2, (W_PG + m) % 2)
                dve.wait_ge(s_gate, m + 1)
                link(nc.vector.tensor_tensor(TN[:, 1 + m % 2], TN[:, 1 + m % 2], PP[m], ALU.mult))
                nc.vector.tensor_tensor(H[:, m], H[:, m], TN[:, 1 + m % 2], ALU.add).then_inc(h_ple, 1)

        def final_row_free(dve, k):
            dve.wait_ge(y_rows[k % 2], 16 * (k // 2))
        norm_final.wait_row = final_row_free

        def sp_store(sp):
            for k in range(KC):
                sp.wait_ge(norm_final.xn, k + 1)
                sp.dma_start(d["y"][k], TN[:, 1 + k % 2]).then_inc(y_rows[k % 2], 16)

        block = ctx.enter_context(nc.Block())

        @block.sync
        def _(sp):
            sp.dma_start(cst[:, :], d["consts"]).then_inc(s_const, 16)
            sp.dma_start(par[:, :], d["params"]).then_inc(s_const, 16)
            sp.dma_start(ptab[:, :], d["page_table"]).then_inc(pt_in, 16)
            for k in range(KC):
                sp.dma_start(Z[:, k], d["xT"][k]).then_inc(x_loaded[k], 16)
            for n in range(2):
                sp.dma_start(wr[:, n], d["weights"][n]).then_inc(w_raw[n], 16)
            with sp.Fori(1, (NZ + 3) // 2) as j:
                for slot in range(2):
                    sp.wait_ge(w_lo, 2 * j + slot - 1)
                    sp.dma_start(wr[:, slot], d["weights"][bass.ds(2 * j + slot, 1)].rearrange("o p k m -> p (o k) m")).then_inc(w_raw[slot], 16)

            sp_idx_pages(sp)
            sp_diff_pages(sp)
            sp_dsa_pages(sp)
            with sp.Fori((NZ + 3) // 2, NW // 2) as j:
                for slot in range(2):
                    sp.wait_ge(w_lo, 2 * j + slot - 1)
                    sp.dma_start(wr[:, slot], d["weights"][bass.ds(2 * j + slot, 1)].rearrange("o p k m -> p (o k) m")).then_inc(w_raw[slot], 16)
            sp_store(sp)
            for a in range(2):
                sp.wait_ge(y_rows[a], 16 * KC // 2)


        @block.gpsimd
        def _(pool):
            pool.wait_ge(ones_set, 1)
            norm_mix.pool(pool)
            pool.wait_ge(norm_mix.lo, KC)
            nc.gpsimd.memset(CM, 0.0).then_inc(masks_set, 1)
            pool.wait_ge(masks_set, 1)
            nc.gpsimd.affine_select(out=CM[:, SEQ - P:SEQ], in_=CM[:, SEQ - P:SEQ], compare_op=ALU.is_ge, fill=-BIG, base=0,
                                    pattern=[[-1, P]], channel_multiplier=1).then_inc(masks_set, 1)
            pool.wait_ge(evac, NZ)
            outs = [(d["c_k"], Z[0:HD, KA]), (d["c_idx"], Z[HD:P, KA]), (d["c_v"], Z[0:HD, CV])]
            outs += [(d[name][j], Z[:, at + j]) for name, at in (("d_k", DK), ("d_v", DV)) for j in range(2)]
            for dst, src in outs:
                pool.dma_start(dst, src).then_inc(outs_stored, 16)
            for tile in range(QT):
                pool.wait_ge(ss_ready, tile + 1)
                nc.gpsimd.tensor_tensor(rs4[:, 16:20], rs4[:, 12:16], neghalf[:, 0:4], ALU.pow).then_inc(head_rstd, 1)
            pool_sdiff_tail(pool)
            pool_reload(pool)
            pool.dma_start(st_in, d["st_ffn_in"]).then_inc(st_loaded, 16)
            pool.dma_start(d["st_mix"], ST[:, :, :, :]).then_inc(mix_stored, 16)
            norm_ffn.pool(pool)
            pool_ple(pool)
            norm_ple.pool(pool)
            norm_final.pool(pool)
            pool.wait_ge(outs_stored, 16 * len(outs))
            pool.wait_ge(mix_stored, 16)
            pool.wait_ge(st_stored, 16)


        @block.scalar
        def _(act):
            act.wait_ge(ones_set, 1)
            norm_mix.act(act, lambda e, k: e.wait_ge(x_loaded[k], 16))
            for n in range(2):
                split_hi(act, n, n, 1)
            def step(n, slot, load_no):
                act.wait_ge(w_used, n + 1)
                split_hi(act, n + 2, slot, load_no)
                nc.scalar.activation(z_slot(n), ps[slot][:, 0:3, 0:TC], ACT.Copy).then_inc(evac, 1)

            def z_slot(n):
                return (Z[:, n] if type(n) is int else Z[:, bass.ds(n, 1)].rearrange("p o t -> p (o t)")).rearrange("p (c t) -> p c t", c=3)
            with act.Fori(0, (NZ - 1) // 2) as j:
                for slot in range(2):
                    step(2 * j + slot, slot, j + 2)
            step(NZ - 1, (NZ - 1) % 2, (NZ + 1) // 2 + 1)
            act_values(act)
            act_lambda(act)
            act_sample_copies(act)
            act_idx(act)
            act_sidx(act)
            act_maps(act)
            for n in range(NI + 5):
                act_item(act, n)
            for b in range(DB + 1):
                act_sdiff(act, b)
            act_sdiff_tail(act)
            act_sdsa(act)
            act_mixers(act)
            act_out(act)
            norm_ffn.act(act, lambda e, k: e.wait_ge(h_out, k + 1))
            act_gate_up(act, 0)
            for g in range(GROUPS):
                if g + 1 < GROUPS:
                    act_gate_up(act, g + 1)
                act_down(act, g)
            act_ple_split(act)
            act.wait_ge(st_stored, 16)
            norm_ple.act(act, lambda e, k: e.wait_ge(h_ffn, ALL_FF))
            act_ple(act)
            act_ple_gate(act)
            norm_final.act(act, lambda e, k: e.wait_ge(h_ple, KC if k else 1))


        @block.vector
        def _(dve):
            nc.vector.memset(eps[:, :], EPS)
            nc.vector.memset(neghalf[:, :], -0.5)
            nc.vector.memset(ones[:, :], 1.0).then_inc(ones_set, 1)
            dve.wait_ge(s_const, 32)
            norm_mix.dve(dve)
            for n in range(2):
                split_lo(dve, n, n)
            with dve.Fori(1, (NZ + 1) // 2) as j:
                for slot in range(2):
                    split_lo(dve, 2 * j + slot, slot)
            split_lo(dve, NZ + 1, (NZ + 1) % 2)
            link = Chain(dve, "dve_chain").link
            dve.wait_ge(masks_set, 2)
            dve.wait_ge(v_cp, QT + 1)
            nc.vector.tensor_scalar(CP, CM[:, SEQ - P:SEQ], BIG, None, ALU.add)
            link(nc.vector.tensor_scalar(newcp, c_("newmask"), BIG, None, ALU.add))
            dve.wait_ge(outs_stored, 16 * 7)
            nc.vector.memset(ex[:, 0:768], 0.0).then_inc(zeroed, 1)
            dve_lambda(dve, link)
            dve_wsel(dve, link)
            dve_idx(dve)
            dve_sscore(dve)
            for c in range(2):
                dve_conv(dve, link, c)
            for c in range(2):
                dve_pool(dve, link, c)
            for n in range(NI + 5):
                dve_item(dve, link, n)
                if n < NI // 2:
                    top_step(dve, link, n)
            dve.wait_ge(o_tr, NI // 4)
            for b in range(DB + 1):
                dve_sdiff(dve, link, b)
            dve_sdiff_tail(dve, link)
            dve_sdsa(dve, link)
            dve_mixers(dve)
            dve_out(dve)
            norm_ffn.dve(dve)
            dve.wait_ge(st_loaded, 16)
            dve_gate_up(dve, link, 0)
            for g in range(GROUPS):
                if g + 1 < GROUPS:
                    dve_gate_up(dve, link, g + 1)
                dve_down(dve, g)
            dve_ple_split(dve)
            norm_ple.dve(dve)
            for half in range(2):
                split_lo(dve, W_PG + half, (W_PG + half) % 2)
            dve_ple_gate(dve, link)
            norm_final.dve(dve)


        @block.tensor
        def _(pe):
            pe.wait_ge(ones_set, 1)
            norm_mix.pe(pe)
            pe.wait_ge(norm_mix.lo, KC)
            for n in range(2):
                project_pe(pe, n, n, True)
            with pe.Fori(1, (NZ - 1) // 2) as j:
                for slot in range(2):
                    project_pe(pe, 2 * j + slot, slot, False)
            project_pe(pe, NZ - 1, (NZ - 1) % 2, False)
            pe.wait_ge(evac, NZ)
            pe_values(pe)
            pe.wait_ge(masks_set, 2)
            pe.wait_ge(v_cp, QT + 1)
            pe_wcol(pe)
            pe_idx(pe)
            pe_sidx(pe)
            pe.wait_ge(sscored, 1)
            pe_maps(pe)
            pe.wait_ge(maps_cp, 2)
            pe.wait_ge(outs_stored, 16 * 7)
            for n in range(NI + 5):
                pe_item(pe, n)
            pe.wait_ge(o_cp, NI // 4)
            for b in range(DB + 1):
                pe_sdiff(pe, b)
            pe_sdiff_tail(pe)
            pe_sdsa(pe)
            pe_out(pe)
            norm_ffn.pe(pe)
            pe.wait_ge(norm_ffn.lo, KC)
            pe_gate_up(pe, 0)
            for g in range(GROUPS):
                if g + 1 < GROUPS:
                    pe_gate_up(pe, g + 1)
                pe_down(pe, g)
            norm_ple.pe(pe)
            pe_ple(pe)
            pe_ple_gate(pe)
            norm_final.pe(pe)





def weight_blocks(w_in, w_out, w_gate, w_up, w_down, w_ple, w_ple_gate):
    def rows(w):
        return w.reshape(KC, P, P).transpose(1, 0, 2)

    out = []
    for pieces in IN_COLS:
        w = np.concatenate([w_in[:, a:a + n] for a, n in pieces], axis=1)
        out.append(rows(np.pad(w, ((0, 0), (0, P - w.shape[1])))))
    out += [rows(w_out[:, m * P:(m + 1) * P]) for m in range(KC)]

    def gate_up(g):
        return [rows(w[:, f * P:(f + 1) * P]) for f in (2 * g, 2 * g + 1) for w in (w_gate, w_up)]

    def down(g):
        w = w_down[2 * g * P:(2 * g + 2) * P].reshape(2, P, 2, 4, P)
        return [w[:, :, half].transpose(1, 0, 2, 3).reshape(P, KC, P) for half in range(2)]

    out += gate_up(0)
    for g in range(FC // 2 - 1):
        out += gate_up(g + 1) + down(g)
    out += down(FC // 2 - 1)
    w = w_ple.reshape(2, P, 2, 4, P)
    out += [w[:, :, half].transpose(1, 0, 2, 3).reshape(P, KC, P) for half in range(2)]
    out += [rows(w_ple_gate[:, m * P:(m + 1) * P]) for m in range(KC)]
    assert len(out) == NW_USED
    out += [out[-1]] * (NW - NW_USED)
    return np.stack(out)


def constants():
    c = np.zeros((P, CONST_N), np.float32)

    def put(name, a):
        at, n = CONST[name]
        c[0:a.shape[0], at:at + n] = a

    tok = np.arange(NS)
    put("ident", np.eye(P))
    row = np.arange(P)
    put("hsel", (row[:, None] % 32 // 4 == np.arange(8)[None]))
    put("headones", (row[:, None] // HD == row[None] // HD))
    for g in range(2):
        sel = (4 * g + row[:, None] // 32 == tok[None] // DT) & (row[:, None] % DT == tok[None] % DT)
        put(f"sel{g}", sel)
        put(f"e{g}", sel.T)
    own = (np.arange(DB)[None, :, None] == tok // DT) & (tok % DT <= tok[:, None, None] % DT)
    put("dmask", np.where(own, 0.0, -BIG).reshape(NS, DB * NS))
    rep = (row[None] // 16 == tok[:, None] // DT) & (row[None] % DT == tok[:, None] % DT)
    put("rep", rep)
    put("newmask", np.where((tok[:, None] // DT == tok[None] // DT) & (tok[None] % DT <= tok[:, None] % DT), 0.0, -BIG))
    m = row % 8 // 4
    put("lam_a", (m == 0)[:, None])
    put("lam_b", (m == 1)[:, None])
    win = np.array([[2, 8], [4, 16]])[row // HD]
    put("inv_w", 1.0 / win)
    cnt = np.minimum(win[:, :, None], np.arange(1, 17)[None, None])
    put("inv_cnt", (1.0 / cnt).reshape(P, 32))
    valid = np.stack([i * P + row + 1 for i in TILES] + [PAST + row % DT + 1], 1)
    kneg = valid - TOPK + 1
    put("kneg", kneg)
    put("kdiff", TOPK - kneg)
    return c


def parameters(i):
    p = np.zeros((P, PARAM_N), np.float32)

    def put(name, a):
        at, n = PARAM[name]
        p[0:a.shape[0], at:at + n] = a.reshape(a.shape[0], n)

    put("g_mix", i["norm_mix"][0].reshape(KC, P).T)
    put("g_ffn", i["norm_ffn"][0].reshape(KC, P).T)
    put("g_ple", i["norm_ple"][0].reshape(KC, P).T)
    put("g_final", i["norm_final"].reshape(KC, P).T)
    put("conv_a", i["conv_a"][0].reshape(3, 2, P).transpose(2, 1, 0))
    put("pool_scale", i["pool_scale"][0].reshape(2, P).T)
    put("conv_ffn", i["conv_ffn"][0].reshape(3, FC, P).transpose(2, 1, 0))
    put("subln", np.tile(i["diff_subln"][0], 2)[:, None])
    put("lam", np.broadcast_to(i["diff_lambda"][0].reshape(1, P), (P, P)))
    maps = np.zeros((P, 2, P), np.float32)
    for g in range(4):
        r = (g % 2) * HD
        maps[r:r + HD, g // 2, r:r + HD] = i["pool_maps"][0, g]
    put("maps", maps)
    put("st_conv", i["state_conv_a"][0].reshape(DB, 2, 2, P).transpose(3, 2, 0, 1))
    put("st_pool", i["state_pool"][0].reshape(DB, 15, 2, P).transpose(3, 2, 0, 1))
    return p


def kernel(**inputs):
    import numpy as _np
    import concourse.bacc as _bacc
    from concourse import mybir as _mybir
    from concourse.bass_utils import run_bass_kernel_spmd as _run

    i = {k: _np.asarray(v) for k, v in inputs.items()}
    xT = _np.concatenate([i["x_prompt"][0].T, i["x_sample"].reshape(NS, D).T], axis=1).reshape(KC, P, NT)
    pT = _np.concatenate([i["p_prompt"][0, 0].T, i["p_sample"][0].reshape(NS, PLE).T], axis=1).reshape(2, P, NT)
    ck, cv, ci = (i[n][:, 0] for n in ("cache_c_k", "cache_c_v", "cache_c_idx"))
    c_pages = _np.concatenate([_np.concatenate([ck, ci], axis=2).transpose(0, 2, 1), cv], axis=2)
    dk, dv = i["cache_d_k"][:, 0], i["cache_d_v"][:, 0]
    n_phys = dk.shape[0]
    dkT = dk.reshape(n_phys, PAGE, 2, P).transpose(0, 3, 2, 1).reshape(n_phys, P, 2 * PAGE)
    d_pages = _np.concatenate([dkT, dv.reshape(n_phys, PAGE, 256)], axis=2)
    arrays = {
        "xT": xT, "pT": pT, "c_pages": c_pages, "d_pages": d_pages,
        "weights": weight_blocks(i["w_in"][0], i["w_out"][0], i["w_gate"][0], i["w_up"][0], i["w_down"][0],
                                 i["w_ple"][0], i["w_ple_gate"][0]),
        "consts": constants(), "params": parameters(i), 
        "st_ffn_in": i["state_ffn"][0].reshape(DB, 2, FC, P).transpose(3, 2, 0, 1), "page_table": i["page_table"].reshape(1, -1),
    }
    arrays = {k: _np.ascontiguousarray(v) for k, v in arrays.items()}
    nc = _bacc.Bacc("TRN2", target_bir_lowering=False, num_devices=1)
    d = {}
    for name, a in arrays.items():
        d[name] = nc.dram_tensor(f"in_{name}", a.shape, _mybir.dt.from_np(a.dtype), kind="ExternalInput").ap()
    for name, shape in OUTS.items():
        d[name] = nc.dram_tensor(f"out_{name}", shape, _mybir.dt.float32, kind="ExternalOutput").ap()
    build(nc, d)
    r = _run(nc, [{f"in_{k}": v for k, v in arrays.items()}], core_ids=[0]).results[0]
    o = {name: _np.asarray(r[f"out_{name}"]) for name in OUTS}

    def rows(a, width):
        a = a.reshape(-1, NT)[0:width]
        return a[:, :SEQ].T, a[:, SEQ:].T.reshape(DB, DT, width)

    y_p, y_s = rows(o["y"], D)
    res = [y_p[None], y_s]
    st = o["st_mix"]
    conv = st[:, :, :, 0:2]
    pool = st[:, :, :, 2:17]
    for s in (conv, pool):
        s = s.transpose(2, 3, 1, 0).reshape(1 + DB, s.shape[3], 256)
        res += [s[0:1][None], s[1:][None]]
    s = o["st_ffn"].reshape(P, FC, 1 + DB, 2).transpose(2, 3, 1, 0).reshape(1 + DB, 2, FF)
    res += [s[0:1][None], s[1:][None]]
    for a in (o["c_k"], o["c_v"], o["c_idx"]):
        p, s = rows(a, HD)
        res += [p[None, None], s[:, None]]
    for a in (o["d_k"], o["d_v"]):
        p, s = rows(a, 256)
        res += [p.reshape(1, 1, SEQ, 4, HD), s.reshape(DB, 1, DT, 4, HD)]
    return tuple(_np.ascontiguousarray(a) for a in res)
```

```python
import math
from contextlib import ExitStack

import numpy as np
import concourse.bass as bass
from concourse import mybir

P = 128
D = 1024
KC = D // P
SEQ, DB, DT = 1024, 8, 4
NS = DB * DT
NT = SEQ + NS
TC = NT // 3
QT = SEQ // P
PAST, PAGE = 1024, 128
NPG = PAST // PAGE
NK = PAST + NS
FF = 2816
FC = FF // P
PLE = 256
TOPK = 256
HD = 64
IDXH = 8
IDX_SCALE = IDXH ** -0.5 * HD ** -0.5
DSA_SCALE = HD ** -0.5
DIFF_SCALE = 32 ** -0.5
LAM_INIT = 0.8 - 0.6 * math.exp(0.0)
EPS = 1e-6
BIG = 1e30

GB, GC, GH, PV = 0, 2, 4, 6
KA, KB, QI, CQ, DK, DQ, CV, DV = 8, 9, 10, 14, 16, 18, 20, 21
NZ = 23
IN_COLS = ([[(128 * j, 128)] for j in range(8)]
           + [[(1280, 64), (1928, 64)], [(1928, 64), (1280, 64)]]
           + [[(1408 + 128 * j, 128)] for j in range(4)]
           + [[(1024, 128)], [(1152, 128)]]
           + [[(2248, 128)], [(2376, 128)], [(1992, 128)], [(2120, 128)]]
           + [[(1344, 64), (1920, 8)], [(2504, 128)], [(2632, 128)]])
TILES = list(range(TOPK // P, QT))
SC_AT = {i: sum((j + 1) * P for j in TILES if j < i) for i in TILES}
SC_S = sum((j + 1) * P for j in TILES)
SC_N = SC_S + NK
NTOP = len(TILES) + 1


NW = NZ + KC + 3 * FC + 2 + KC
OUTS = {"y": (KC, P, NT), "st_mix": (P, 2, 1 + DB, 17), "st_ffn": (P, FC, 1 + DB, 2), "c_k": (HD, NT), "c_v": (HD, NT),
        "c_idx": (HD, NT), "d_k": (2, P, NT), "d_v": (2, P, NT)}


def layout(pieces):
    at, out = 0, {}
    for name, n in pieces:
        out[name] = (at, n)
        at += n
    return out, at


CONST, CONST_N = layout([("ident", P), ("hsel", 8), ("sel0", 32), ("sel1", 32), ("e0", P), ("e1", P),
                         ("rep", P), ("newmask", NS), ("dmask", DB * NS), ("lam_a", 1), ("lam_b", 1),
                         ("inv_w", 2), ("inv_cnt", 32), ("headones", P), ("kneg", NTOP), ("kdiff", NTOP)])
PARAM, PARAM_N = layout([("g_mix", KC), ("g_ffn", KC), ("g_ple", KC), ("g_final", KC), ("conv_a", 6),
                         ("pool_scale", 2), ("conv_ffn", FC * 3), ("subln", 1), ("lam", P),
                         ("maps", 2 * P), ("st_conv", 2 * DB * 2), ("st_pool", 2 * DB * 15)])


def build(nc, d):
    f32, f32r, i32, u16 = mybir.dt.float32, mybir.dt.float32r, mybir.dt.int32, mybir.dt.uint16
    ALU, ACT, AX = mybir.AluOpType, mybir.ActivationFunctionType, mybir.AxisListType
    with ExitStack() as ctx:
        def sb(name, shape, dt=f32):
            return ctx.enter_context(nc.sbuf_tensor(name, shape, dt))

        def sem(name):
            return ctx.enter_context(nc.semaphore(name))

        arena_at = (nc.sbuf_base + 31) // 32 * 32
        arena = sb("arena", [P, 2 * KC * NT])
        xh = nc.alloc_sbuf_tensor_at("xh", [P, KC, NT], f32r, offset=arena_at)
        xl = nc.alloc_sbuf_tensor_at("xl", [P, KC, NT], f32r, offset=arena_at + 4 * KC * NT)
        taken = [0]

        def carve(n):
            taken[0] += n
            assert taken[0] <= 2 * KC * NT
            return arena[:, taken[0] - n:taken[0]]

        vtok = carve((QT + 1) * 384).rearrange("p (t f) -> p t f", f=384)
        SC = carve(SC_N)
        YF = carve(SC_N)
        YY = YF.bitcast(u16)
        y_hi, y_lo = YY[:, 0:SC_N], YY[:, SC_N:2 * SC_N]
        kring = carve(2 * NPG * PAGE).rearrange("p (s g c) -> p s g c", s=2, c=PAGE)
        qis = carve(IDXH * NS).rearrange("p (b h t) -> p b h t", b=DB, h=IDXH)
        wsel = carve(2 * NS).rearrange("p (g t) -> p g t", g=2)
        wcol = carve(2)
        tk = carve(12 * NTOP).rearrange("p (a j) -> p a j", j=NTOP)
        mx = carve(4)
        nm = carve(4)
        sm = carve(4)
        cf = carve(4)
        rs4 = carve(20)
        lamw = carve(4)
        CP = carve(P)
        newcp = carve(NS)
        if True:
            ST = sb("ST", [P, 2, 1 + DB, 17])
        z_at = (nc.sbuf_base + 31) // 32 * 32
        Z = sb("Z", [P, NZ, NT])
        ah = nc.alloc_sbuf_tensor_at("ah", [P, 2, 2, NT], f32r, offset=z_at)
        al = nc.alloc_sbuf_tensor_at("al", [P, 2, 2, NT], f32r, offset=z_at + 16 * NT)
        ring_at = (nc.sbuf_base + 31) // 32 * 32
        pages = sb("pages", [P, 3 * 2 * KC * P])
        wr = nc.alloc_sbuf_tensor_at("wr", [P, 2, KC, P], f32, offset=ring_at)
        wh = nc.alloc_sbuf_tensor_at("wh", [P, 2, KC, P], f32r, offset=ring_at + 8 * KC * P)
        wl = nc.alloc_sbuf_tensor_at("wl", [P, 2, KC, P], f32r, offset=ring_at + 16 * KC * P)
        cst = sb("cst", [P, CONST_N])
        par = sb("par", [P, PARAM_N])
        ones = sb("ones", [P, P])
        ptab = sb("ptab", [1, DB * NPG], i32)
        TN = sb("TN", [P, 3, NT])
        small = sb("small", [P, 40])
        ps = [ctx.enter_context(nc.psum_tensor(f"ps{j}", [P, 4, 512], f32)) for j in range(2)]

        def c_(name, rows=P):
            at, n = CONST[name]
            return cst[0:rows, at:at + n]

        def p_(name):
            at, n = PARAM[name]
            return par[:, at:at + n]

        class Chain:

            def __init__(self, eng, name):
                self.eng, self.sem, self.n = eng, sem(name), 0

            def link(self, ins):
                self.n += 1
                ins.then_inc(self.sem, 1)
                self.eng.wait_ge(self.sem, self.n)

        s_const = sem("constants_loaded")
        outs_stored = sem("outputs_stored")
        x_loaded = [sem(f"x_loaded{k}") for k in range(KC)]
        ones_set = sem("ones_set")

        w_raw = [sem("w_raw0"), sem("w_raw1")]
        w_hi = sem("w_hi_split")
        w_lo = sem("w_lo_split")
        w_used = sem("w_used")
        evac = sem("evacuated")

        def split_hi(act, n, slot, load_no):
            act.wait_ge(w_raw[slot], 16 * load_no)
            nc.scalar.activation(wh[:, slot], wr[:, slot], ACT.Copy).then_inc(w_hi, 1)

        def split_lo(dve, n, slot):
            dve.wait_ge(w_hi, n + 1)
            nc.vector.tensor_tensor(wl[:, slot], wr[:, slot], wh[:, slot].bitcast(f32), ALU.subtract).then_inc(w_lo, 1)

        def three_pass(out, w_at, x_at, start, stop):
            for t, (w, x) in enumerate(((wh, xh), (wl, xh), (wh, xl))):
                last = nc.tensor.matmul(out, w_at(w), x_at(x), start=start and t == 0, stop=stop and t == 2)
            return last

        def bank(j):
            return ps[j // 4][:, j % 4]

        class Norm:
            def __init__(self, name, src, gain, split=True):
                self.src, self.gain, self.split = src, p_(gain), split
                self.sq, self.sum, self.stat = sem(name + "_squares"), sem(name + "_sums"), sem(name + "_stat")
                self.std, self.diag, self.bcast = sem(name + "_std"), sem(name + "_diag"), sem(name + "_bcast")
                self.xn, self.hi, self.lo = sem(name + "_scaled"), sem(name + "_hi"), sem(name + "_lo")
                self.rec = sem(name + "_rec")

            def act(self, act, ready):
                for k in range(KC):
                    ready(act, k)
                    if k >= 3:
                        act.wait_ge(self.sum, k - 2)
                    dst = TN[:, 0] if k == 0 else TN[:, 1 + k % 2]
                    nc.scalar.activation(dst, self.src(k), ACT.Square).then_inc(self.sq, 1)
                act.wait_ge(self.stat, 1)
                nc.scalar.activation(small[:, 0:QT], bank(0)[:, 0:QT], ACT.Identity, bias=eps[:, :], scale=1.0 / D)
                nc.scalar.activation(small[0:NS, QT:QT + 1], bank(0)[0:NS, QT:QT + 1], ACT.Identity, bias=eps[0:NS, :],
                                     scale=1.0 / D).then_inc(self.std, 1)
                if self.split:
                    for k in range(KC):
                        act.wait_ge(self.xn, k + 1)
                        nc.scalar.activation(xh[:, k], TN[:, 1 + k % 2], ACT.Copy).then_inc(self.hi, 1)

            def dve(self, dve):
                for k in range(1, KC):
                    dve.wait_ge(self.sq, k + 1)
                    if k > 1:
                        dve.wait_ge(self.sum, k - 1)
                    nc.vector.tensor_tensor(TN[:, 0], TN[:, 0], TN[:, 1 + k % 2], ALU.add).then_inc(self.sum, 1)
                dve.wait_ge(self.rec, 1)
                for t in range(QT):
                    nc.vector.tensor_scalar(TN[:, 0, t * P:(t + 1) * P], c_("ident"), small[:, 10 + t:11 + t], None, ALU.mult)
                nc.vector.tensor_scalar(diag_s[:, :], c_("ident", NS)[:, 0:NS], small[0:NS, 10 + QT:11 + QT], None,
                                        ALU.mult).then_inc(self.diag, 1)
                dve.wait_ge(self.bcast, 1)
                for k in range(KC):
                    if k >= 2:
                        self.wait_row(dve, k)
                    nc.vector.scalar_tensor_tensor(TN[:, 1 + k % 2], self.src(k), self.gain[:, k:k + 1], rstd_bc,
                                                   ALU.mult, ALU.mult).then_inc(self.xn, 1)
                    if self.split:
                        dve.wait_ge(self.hi, k + 1)
                        nc.vector.tensor_tensor(xl[:, k], TN[:, 1 + k % 2], xh[:, k].bitcast(f32),
                                                ALU.subtract).then_inc(self.lo, 1)

            def pool(self, pool):
                pool.wait_ge(self.std, 1)
                nc.gpsimd.tensor_tensor(small[:, 10:10 + QT], small[:, 0:QT], neghalf[:, 0:QT], ALU.pow)
                nc.gpsimd.tensor_tensor(small[0:NS, 10 + QT:11 + QT], small[0:NS, QT:QT + 1], neghalf[0:NS, 0:1],
                                        ALU.pow).then_inc(self.rec, 1)

            def wait_row(self, dve, k):
                if self.split:
                    dve.wait_ge(self.lo, k - 1)

            def pe(self, pe):
                pe.wait_ge(self.sum, KC - 1)
                for t in range(QT + 1):
                    w = P if t < QT else NS
                    last = nc.tensor.matmul(bank(0)[0:w, t:t + 1], TN[:, 0, t * P:t * P + w], ones[:, 0:1],
                                            start=True, stop=True)
                last.then_inc(self.stat, 1)
                pe.wait_ge(self.diag, 1)
                for t in range(QT + 1):
                    w = P if t < QT else NS
                    rhs = TN[:, 0, t * P:(t + 1) * P] if t < QT else diag_s[:, :]
                    last = nc.tensor.matmul(rstd_bc[:, t * P:t * P + w], ones[0:w, :], rhs, start=True, stop=True)
                last.then_inc(self.bcast, 1)

        rstd_bc = ps[1][:, :, :].rearrange("p a b -> p (a b)")[:, 0:NT]
        diag_s = sb("diag_s", [NS, NS])
        eps = sb("eps", [P, 1])
        neghalf = sb("neghalf", [P, QT])

        norm_mix = Norm("norm_mix", lambda k: Z[:, k], "g_mix")

        def project_pe(pe, n, slot, first):
            pe.wait_ge(w_lo, n + 1)
            if not first:
                pe.wait_ge(evac, n - 1)
            for c in range(3):
                for k in range(KC):
                    last = three_pass(ps[slot][:, c, 0:TC], lambda w: w[:, slot, k], lambda x: x[:, k, c * TC:(c + 1) * TC],
                                      k == 0, k == KC - 1)
            last.then_inc(w_used, 1)


        relu = TN[:, 0:2]
        CM = TN[:, 2, 0:SEQ]
        Pb = Z[:, QI:QI + 4].rearrange("p (a b) t -> p a b t", a=2)
        PT = Z[:, CV:CV + 2]
        junk = [TN[:, 0, a * NT // 2:(a + 1) * NT // 2].bitcast(u16) for a in range(2)]
        ones16 = TN[:, 0, NT // 2:NT].bitcast(u16)
        ot, osq, yt = (TN[:, 1, a * 256:(a + 1) * 256] for a in range(3))

        scratch = TN[:, :, :].rearrange("p a t -> p (a t)")
        samples = lambda a: a[:, SEQ:NT].rearrange("p (b t) -> p b t", t=DT)
        v_tr, v_cp = sem("v_transposed"), sem("v_copied")
        masks_set = sem("masks_set")
        idx_mm, idx_relu, idx_acc = sem("idx_product"), sem("idx_relu"), sem("idx_sum")
        d_mixed, maps_mm, maps_cp = sem("pool_input"), sem("pool_mapped"), sem("pool_copied")
        lam_sum, lam_exp = sem("lambda_sums"), sem("lambda_exps")
        IDX = [(i, h) for i in TILES for h in range(IDXH)]

        def causal(i):
            return CM[:, SEQ - (i + 1) * P:SEQ]

        def scores(j):
            if j < len(TILES):
                i = TILES[j]
                return SC_AT[i], (i + 1) * P, P
            return SC_S, NK, NS

        ITEMS = []
        for i in range(QT):
            ITEMS += [("diff", i, h) for h in range(4)] + [("sdiff", i, 0)]
        for i in range(QT):
            ITEMS += [("dsa", i, h) for h in range(4)] + ([("sdsa", i // 2, 0)] if i % 2 else [])
        NI = len(ITEMS)
        PROMPT = ("diff", "dsa")
        FIRST_DSA = ITEMS.index(("dsa", 0, 0))

        def maps_of(n):
            return 1 if ITEMS[n][0] == "dsa" else 2

        def unit(n, m=0):
            return sum(maps_of(a) for a in range(n)) + m

        def tile_no(n):
            return sum(ITEMS[a][0] in PROMPT for a in range(n)) // 4

        def sample_no(n):
            return sum(ITEMS[a][0] not in PROMPT for a in range(n))

        def ends_tile(n):
            return ITEMS[n][0] in PROMPT and ITEMS[n][2] == 3

        qk_mm = sem("logits_product")
        row_max = sem("logits_masked")
        neg_max = sem("negated_maxima")
        exp_done = sem("exponentials")
        combined = sem("maps_combined")
        p_tr = sem("probs_transposed")
        p_cp = sem("probs_copied")
        pv_mm = sem("values_product")
        so_cp = sem("sample_output")
        ss_ready = sem("head_squares")
        head_rstd = sem("head_rstd")
        yt_ready = sem("tile_output")
        o_tr = sem("tile_transposed")
        o_cp = sem("tile_stored")

        def flat(pair, rows=slice(0, P)):
            return ps[pair // 2][rows, 2 * (pair % 2):2 * (pair % 2) + 2].rearrange("p a b -> p (a b)")

        def pe_values(pe):
            for t in range(QT + 1):
                w = P if t < QT else NS
                if t >= 2:
                    pe.wait_ge(v_cp, t - 1)
                for j in range(3):
                    last = nc.tensor.transpose(bank(6 + t % 2)[0:w, j * P:(j + 1) * P], Z[:, CV + j, t * P:t * P + w], c_("ident"))
                last.then_inc(v_tr, 1)

        PER_SAMPLE = len(IDX) // DB

        def pe_idx(pe):
            for u, (i, h) in enumerate(IDX):
                if u >= 2:
                    pe.wait_ge(idx_relu, u - 1)
                half = slice(HD * (h % 2), HD * (h % 2) + HD)
                keys = KA if h % 2 else KB
                S = (i + 1) * P
                for a in range(0, S, 512):
                    w = min(512, S - a)
                    last = nc.tensor.matmul(flat(u % 2)[:, a:a + w], Z[half, QI + h // 2, i * P:(i + 1) * P],
                                            Z[half, keys, a:a + w], start=True, stop=True)
                last.then_inc(idx_mm, 1)
                if u % PER_SAMPLE == PER_SAMPLE - 1:
                    pe_sidx(pe, u // PER_SAMPLE)

        def pe_maps(pe):
            for c in range(2):
                pe.wait_ge(d_mixed, c + 1)
                for a in range(3):
                    last = nc.tensor.matmul(bank(3 * c + a)[:, 0:TC], p_("maps")[:, c * P:(c + 1) * P],
                                            Z[:, PV + c, a * TC:(a + 1) * TC], start=True, stop=True)
                last.then_inc(maps_mm, 1)

        def pe_logits(pe, n):
            kind, i, h = ITEMS[n]
            for m in range(maps_of(n)):
                u = unit(n, m)
                if u >= 2:
                    pe.wait_ge(row_max, u - 1)
                out = flat(u % 2)
                if kind in PROMPT:
                    S = (i + 1) * P
                    if kind == "diff":
                        r = HD * (h % 2) + 32 * m
                        part, q, k = slice(r, r + 32), DQ + h // 2, DK + h // 2
                    else:
                        part, q, k = slice(HD * (h % 2), HD * (h % 2) + HD), CQ + h // 2, KB if h % 2 else KA
                    for a in range(0, S, 512):
                        w = min(512, S - a)
                        last = nc.tensor.matmul(out[:, a:a + w], Z[part, q, i * P:(i + 1) * P], Z[part, k, a:a + w],
                                                start=True, stop=True)
                elif kind == "sdiff":
                    if m == 0:
                        pe.wait_ge(d_in[i % 2], 16 * NPG * (i // 2 + 1))
                    for half in range(1 if m else 2):
                        for c in range(2):
                            keys = dk_new[:, c] if m else diff_pages(i, half)[:, :, c * P:(c + 1) * P]
                            w = NS if m else 512
                            last = nc.tensor.matmul(out[0:32, half * 512:half * 512 + w], qdz[:, c, i], keys, start=c == 0, stop=c == 1)
                else:
                    if m == 0:
                        pe.wait_ge(c_in[i % 2], 16 * 2 * NPG * (i // 2 + 1))
                    for half in range(1 if m else 2):
                        w = NS if m else 512
                        at = PAST * m + 512 * half
                        dst = out[0:32, half * 512:half * 512 + w]
                        for b in range(2):
                            keys = ka_new[0:HD, :] if m else dsa_pages(i, b)[0:HD, 4 * half:4 * half + 4, 0:P]
                            nc.tensor.matmul(dst, qcz[:, 2 * i + b], keys, start=b == 0, stop=False)
                        last = nc.tensor.matmul(dst, c_("rep", NS)[:, 32 * i:32 * i + 32], SC[0:NS, SC_S + at:SC_S + at + w],
                                                start=False, stop=True)
                last.then_inc(qk_mm, 1)

        def pe_outputs(pe, n):
            kind, i, h = ITEMS[n]
            pe.wait_ge(p_cp, n + 1)
            pt = PT[:, n % 2]
            if kind in PROMPT:
                if h == 0 and tile_no(n) >= 2:
                    pe.wait_ge(o_cp, tile_no(n) - 1)
                v = P + HD * h if kind == "diff" else 0
                for b in range(i + 1):
                    last = nc.tensor.matmul(bank(6 + tile_no(n) % 2)[:, h * HD:(h + 1) * HD], pt[:, b * P:(b + 1) * P],
                                            vtok[:, b, v:v + HD], start=b == 0, stop=b == i)
            else:
                for c in range(2):
                    for g in range(NPG + 1):
                        rows = P if g < NPG else NS
                        if kind == "sdiff":
                            v = diff_pages(i, g // 4)[:, g % 4, 256 + c * P:256 + (c + 1) * P] if g < NPG else vtok[0:NS, QT, P + c * P:P + (c + 1) * P]
                            out, p = bank(5)[:, c * 32:c * 32 + 32], pt[0:rows, g * 32:g * 32 + 32]
                        else:
                            v = dsa_pages(i, c)[:, g, P:P + HD] if g < NPG else vtok[0:NS, QT, 0:HD]
                            out, p = bank(5)[0:HD, c * 16:c * 16 + 16], pt[0:rows, g * 32 + c * 16:g * 32 + c * 16 + 16]
                        last = nc.tensor.matmul(out, v, p, start=g == 0, stop=g == NPG)
            last.then_inc(pv_mm, 1)

        def pe_transposes(pe, n):
            kind, i, h = ITEMS[n]
            pe.wait_ge(combined, n + 1)
            if n >= 1:
                pe.wait_ge(p_cp, n)
            if n >= 1 and ITEMS[n - 1][0] not in PROMPT:
                pe.wait_ge(so_cp, sample_no(n))
            if kind in PROMPT:
                for b in range(i + 1):
                    last = nc.tensor.transpose(bank(4 + b // 4)[:, (b % 4) * P:(b % 4 + 1) * P],
                                               Pb[:, n % 2, 0, b * P:(b + 1) * P], c_("ident"))
            else:
                for g in range(NPG + 1):
                    w = P if g < NPG else NS
                    last = nc.tensor.transpose(bank(4)[0:w, g * 32:g * 32 + 32], Pb[0:32, n % 2, 0, g * P:g * P + w], c_("ident", 32)[:, 0:32])
            last.then_inc(p_tr, 1)

        def pe_item(pe, n):
            if n < NI:
                pe_logits(pe, n)
            if 0 <= n - 2 < NI:
                pe_outputs(pe, n - 2)
            if 0 <= n - 1 < NI:
                pe_transposes(pe, n - 1)
            if 0 <= n - 4 < NI and ends_tile(n - 4):
                tile = tile_no(n - 4)
                pe.wait_ge(yt_ready, tile + 1)
                for j in range(2):
                    last = nc.tensor.transpose(bank(6 + tile % 2)[:, 256 + j * P:256 + (j + 1) * P], yt[:, j * P:(j + 1) * P], c_("ident"))
                last.then_inc(o_tr, 1)

        def act_values(act):
            for t in range(QT + 1):
                w = P if t < QT else NS
                act.wait_ge(v_tr, t + 1)
                nc.scalar.activation(vtok[0:w, t], bank(6 + t % 2)[0:w, 0:384], ACT.Copy).then_inc(v_cp, 1)

        def act_idx(act):
            for u, (i, h) in enumerate(IDX):
                S = (i + 1) * P
                act.wait_ge(idx_mm, u + 1)
                if u >= 2:
                    act.wait_ge(idx_acc, u - 1)
                nc.scalar.activation(relu[:, u % 2, 0:S], flat(u % 2)[:, 0:S], ACT.Relu, scale=IDX_SCALE).then_inc(idx_relu, 1)
                if u % (4 * PER_SAMPLE) == 4 * PER_SAMPLE - 1:
                    act_sidx(act, u // (4 * PER_SAMPLE))

        def act_lambda(act):
            act.wait_ge(lam_sum, 1)
            nc.scalar.activation(lamw[:, 2:4], lamw[:, 0:2], ACT.Exp).then_inc(lam_exp, 1)

        def act_maps(act):
            for c in range(2):
                act.wait_ge(maps_mm, c + 1)
                for a in range(3):
                    last = nc.scalar.activation(Z[:, GC + c, a * TC:(a + 1) * TC], bank(3 * c + a)[:, 0:TC], ACT.Copy,
                                                scale=p_("pool_scale")[:, c:c + 1])
                last.then_inc(maps_cp, 1)

        SCALE = {"diff": DIFF_SCALE, "sdiff": DIFF_SCALE, "dsa": DSA_SCALE, "sdsa": DSA_SCALE}

        def act_item(act, n):
            if 0 <= n - 2 < NI and ITEMS[n - 2][0] not in PROMPT:
                kind, i, h = ITEMS[n - 2]
                act.wait_ge(pv_mm, n - 1)
                if kind == "sdiff":
                    last = nc.scalar.activation(so[:, i], bank(5)[:, 0:64], ACT.Copy)
                else:
                    o = bank(5)[0:HD, 0:32].rearrange("p (b h t) -> p h b t", b=2, h=4)
                    for h in range(4):
                        half = slice(HD * (h % 2), HD * (h % 2) + HD)
                        last = nc.scalar.activation(samples(Z[half, GH + h // 2])[:, 2 * i:2 * i + 2], o[:, h], ACT.Copy)
                last.then_inc(so_cp, 1)
            if n < NI:
                kind, i, h = ITEMS[n]
                act.wait_ge(neg_max, n + 1)
                prompt = kind in PROMPT
                rows, S = (P, (i + 1) * P) if prompt else (32, NK)
                for m in range(maps_of(n) if prompt else 1):
                    col = 2 * (n % 2) + m
                    p = Pb[0:rows, n % 2, m, 0:S]
                    last = nc.scalar.activation(p, p, ACT.Exp, bias=nm[0:rows, col:col + 1], scale=SCALE[kind], accum_out=sm[0:rows, col:col + 1])
                last.then_inc(exp_done, 1)
            if 0 <= n - 1 < NI:
                kind, i, h = ITEMS[n - 1]
                act.wait_ge(p_tr, n)
                if n - 1 >= 2:
                    act.wait_ge(pv_mm, n - 2)
                pt = PT[:, (n - 1) % 2]
                if kind in PROMPT:
                    for b in range(0, i + 1, 4):
                        w = min(4, i + 1 - b) * P
                        last = nc.scalar.activation(pt[:, b * P:b * P + w], bank(4 + b // 4)[:, 0:w], ACT.Copy)
                else:
                    nc.scalar.activation(pt[:, 0:NPG * 32], bank(4)[:, 0:NPG * 32], ACT.Copy)
                    last = nc.scalar.activation(pt[0:NS, NPG * 32:NPG * 32 + 32], bank(4)[0:NS, NPG * 32:NPG * 32 + 32], ACT.Copy)
                last.then_inc(p_cp, 1)
            if 0 <= n - 4 < NI and ends_tile(n - 4):
                kind, i, h = ITEMS[n - 4]
                tile = tile_no(n - 4)
                act.wait_ge(o_tr, tile + 1)
                for j in range(2):
                    src = bank(6 + tile % 2)[:, 256 + j * P:256 + (j + 1) * P]
                    dst = Z[:, (PV if kind == "diff" else GH) + j, i * P:(i + 1) * P]
                    last = nc.scalar.activation(dst, src, ACT.Copy, scale=subln[:, :] if kind == "diff" else 1.0)
                last.then_inc(o_cp, 1)

        subln = sb("subln", [P, 1])

        def dve_idx(dve):
            for u, (i, h) in enumerate(IDX):
                at, S = SC_AT[i], (i + 1) * P
                dve.wait_ge(idx_relu, u + 1)
                if u:
                    dve.wait_ge(idx_acc, u)
                before = causal(i) if h == 0 else SC[:, at:at + S]
                nc.vector.scalar_tensor_tensor(SC[:, at:at + S], relu[:, u % 2, 0:S], vtok[:, i, HD + h:HD + h + 1], before,
                                               ALU.mult, ALU.add).then_inc(idx_acc, 1)

        def dve_conv(dve, link, c):
            n = 2 + SEQ + DB * 6
            U, T = scratch[:, 0:n], scratch[:, n:2 * n]
            Us, Ts = (a[:, 2 + SEQ:n].rearrange("p (b t) -> p b t", t=6) for a in (U, T))
            st = p_("st_conv").rearrange("p (c b t) -> p c b t", c=2, t=2)[:, c]
            w = p_("conv_a")[:, 3 * c:3 * c + 3]
            tok = lambda slot: Z[:, slot, SEQ:NT].rearrange("p (b t) -> p b t", t=DT)
            nc.vector.memset(U[:, 0:2], 0.0)
            nc.vector.tensor_copy(Us[:, :, 0:2], st)
            nc.vector.tensor_tensor(U[:, 2:2 + SEQ], Z[:, GC + c, 0:SEQ], Z[:, GH + c, 0:SEQ], ALU.mult)
            link(nc.vector.tensor_tensor(Us[:, :, 2:6], tok(GC + c), tok(GH + c), ALU.mult))
            link(nc.vector.tensor_scalar(T[:, 0:n - 2], U[:, 0:n - 2], w[:, 0:1], None, ALU.mult))
            link(nc.vector.scalar_tensor_tensor(T[:, 0:n - 2], U[:, 1:n - 1], w[:, 1:2], T[:, 0:n - 2], ALU.mult, ALU.add))
            link(nc.vector.scalar_tensor_tensor(T[:, 0:n - 2], U[:, 2:n], w[:, 2:3], T[:, 0:n - 2], ALU.mult, ALU.add))
            nc.vector.tensor_tensor(Z[:, GB + c, 0:SEQ], Z[:, GB + c, 0:SEQ], T[:, 0:SEQ], ALU.mult)
            nc.vector.tensor_tensor(tok(GB + c), tok(GB + c), Ts[:, :, 0:DT], ALU.mult)
            nc.vector.tensor_copy(ST[:, c, 0, 0:2], U[:, SEQ:SEQ + 2])
            link(nc.vector.tensor_copy(ST[:, c, 1:1 + DB, 0:2], Us[:, :, 4:6]))

        def dve_pool(dve, link, c):
            n = 15 + SEQ + DB * 19
            E, A = scratch[:, 0:n], scratch[:, n:2 * n]
            s_of = lambda x: x[:, 15 + SEQ:n].rearrange("p (b t) -> p b t", t=19)
            tok = samples(Z[:, PV + c])
            nc.vector.memset(E[:, 0:15], 0.0)
            nc.vector.tensor_copy(s_of(E)[:, :, 0:15], p_("st_pool").rearrange("p (c b t) -> p c b t", c=2, t=15)[:, c])
            nc.vector.tensor_copy(E[:, 15:15 + SEQ], Z[:, PV + c, 0:SEQ])
            link(nc.vector.tensor_copy(s_of(E)[:, :, 15:19], tok))
            nc.vector.tensor_copy(ST[:, c, 0, 2:17], E[:, SEQ:SEQ + 15])
            link(nc.vector.tensor_copy(ST[:, c, 1:1 + DB, 2:17], s_of(E)[:, :, 4:19]))

            def double(dst, src, step):
                link(nc.vector.tensor_tensor(dst[:, 0:n - 2 * step + 1], src[:, 0:n - 2 * step + 1],
                                             src[:, step:n - step + 1], ALU.add))

            def finish(half, sums, win):
                r = slice(HD * half, HD * half + HD)
                inv = c_("inv_w")[r, c:c + 1]
                off = 16 - win
                table = c_("inv_cnt")[r, 16 * c:16 * c + 16]
                link(nc.vector.tensor_tensor(small[r, 0:16], sums[r, off:off + 16], table, ALU.mult))
                link(nc.vector.tensor_tensor(small[r, 0:16], small[r, 0:16], Z[r, PV + c, 0:16], ALU.subtract))
                link(nc.vector.scalar_tensor_tensor(Z[r, PV + c, 0:SEQ], sums[r, off:off + SEQ], inv, Z[r, PV + c, 0:SEQ], ALU.mult, ALU.subtract))
                link(nc.vector.scalar_tensor_tensor(tok[r], s_of(sums)[r, :, off:off + DT], inv, tok[r], ALU.mult, ALU.subtract))
                return nc.vector.tensor_copy(Z[r, PV + c, 0:16], small[r, 0:16])

            double(A, E, 1)
            double(E, A, 2)
            if c == 0:
                link(finish(0, A, 2))
                last = finish(1, E, 4)
            else:
                double(A, E, 4)
                double(E, A, 8)
                link(finish(0, A, 8))
                last = finish(1, E, 16)
            last.then_inc(d_mixed, 1)
            dve.wait_ge(d_mixed, c + 1)

        def dve_lambda(dve, link):
            lp = p_("lam")
            link(nc.vector.tensor_tensor_reduce(out=small[:, 0:32], in0=lp[:, 0:32], in1=lp[:, 32:64], scale=1.0, scalar=0.0,
                                                op0=ALU.mult, op1=ALU.add, accum_out=lamw[:, 0:1]))
            nc.vector.tensor_tensor_reduce(out=small[:, 0:32], in0=lp[:, 64:96], in1=lp[:, 96:128], scale=1.0, scalar=0.0,
                                           op0=ALU.mult, op1=ALU.add, accum_out=lamw[:, 1:2]).then_inc(lam_sum, 1)
            dve.wait_ge(lam_exp, 1)
            link(nc.vector.tensor_tensor(small[:, 32:33], lamw[:, 3:4], lamw[:, 2:3], ALU.subtract))
            link(nc.vector.tensor_scalar(small[:, 32:33], small[:, 32:33], -LAM_INIT, None, ALU.add))
            nc.vector.tensor_scalar(subln[:, :], p_("subln"), 1.0 - LAM_INIT, None, ALU.mult)
            link(nc.vector.scalar_tensor_tensor(small[:, 33:34], c_("lam_b"), small[:, 32:33], c_("lam_a"), ALU.mult, ALU.add))

        CNT, POS, SGN, KK, THI, CAND, GE, TLO, NEED, TMAG, THR = range(11)

        def col(a, j=None, rows=P):
            return tk[0:rows, a] if j is None else tk[0:rows, a, j:j + 1]

        def count(j, src, scalar, op, out=None):
            at, S, rows = scores(j)
            out = junk[0][0:rows, 0:S] if out is None else out
            scalar = scalar if type(scalar) is float else col(scalar, j, rows)
            return nc.vector.tensor_scalar(out, src[0:rows, at:at + S], scalar, 0.0, op, ALU.add, accum_out=col(CNT, j, rows))

        counted = sem("counted")
        counts = [0]

        def top_prepare(dve, link):
            link(nc.vector.memset(tk[:, :, :], 0.0))
            for j in range(NTOP):
                link(count(j, SC, 0.0, ALU.is_ge))
            link(nc.vector.tensor_scalar(col(POS), col(CNT), float(TOPK), None, ALU.is_ge))
            link(nc.vector.tensor_scalar(col(SGN), col(POS), 2.0, -1.0, ALU.mult, ALU.add))
            link(nc.vector.tensor_tensor(col(KK), col(POS), c_("kdiff"), ALU.mult))
            link(nc.vector.tensor_tensor(col(KK), col(KK), c_("kneg"), ALU.add))
            y = TN[:, 0]
            for j in range(NTOP):
                at, S, rows = scores(j)
                link(nc.vector.tensor_scalar(y[0:rows, 0:S], SC[0:rows, at:at + S], col(SGN, j, rows), 0.0, ALU.mult, ALU.max))
                w, seen = (P, CP) if rows == P else (NS, newcp)
                link(nc.vector.tensor_tensor(y[0:rows, S - w:S], y[0:rows, S - w:S], seen[0:rows, :], ALU.min))
                halves = y.bitcast(u16)
                nc.vector.tensor_copy(y_hi[0:rows, at:at + S], halves[0:rows, 1:2 * S:2])
                link(nc.vector.tensor_copy(y_lo[0:rows, at:at + S], halves[0:rows, 0:2 * S:2]))

        def top_bit(dve, link, src, T, b):
            link(nc.vector.tensor_scalar(col(CAND), col(T), float(2 ** b), None, ALU.add))
            for j in range(NTOP):
                count(j, src, CAND, ALU.is_ge, out=junk[j % 2][0:scores(j)[2], 0:scores(j)[1]]).then_inc(counted, 1)
                counts[0] += 1
                dve.wait_ge(counted, counts[0] - (j < NTOP - 1))
            link(nc.vector.tensor_tensor(col(GE), col(CNT), col(KK), ALU.is_ge))
            link(nc.vector.scalar_tensor_tensor(col(T), col(GE), float(2 ** b), col(T), ALU.mult, ALU.add))

        def top_middle(dve, link):
            for j in range(NTOP):
                at, S, rows = scores(j)
                link(count(j, y_hi, THI, ALU.is_gt))
                last = nc.vector.scalar_tensor_tensor(y_lo[0:rows, at:at + S], y_hi[0:rows, at:at + S], col(THI, j, rows),
                                                      y_lo[0:rows, at:at + S], ALU.is_equal, ALU.mult)
            link(last)
            link(nc.vector.tensor_tensor(col(KK), col(KK), col(CNT), ALU.subtract))

        def top_finish(dve, link):
            nc.vector.memset(ones16, 1.0)
            bits = col(TMAG).bitcast(u16)
            nc.vector.tensor_copy(bits[:, 1:2 * NTOP:2], col(THI))
            link(nc.vector.tensor_copy(bits[:, 0:2 * NTOP:2], col(TLO)))
            link(nc.vector.tensor_tensor(col(THR), col(TMAG), col(SGN), ALU.mult))
            for j in range(NTOP):
                at, S, rows = scores(j)
                count(j, SC, THR, ALU.is_gt, out=y_hi[0:rows, at:at + S])
                last = nc.vector.tensor_scalar(y_lo[0:rows, at:at + S], SC[0:rows, at:at + S], col(THR, j, rows), None, ALU.is_equal)
            link(last)
            link(nc.vector.tensor_scalar(col(NEED), col(CNT), -1.0, float(TOPK), ALU.mult, ALU.add))
            for j in range(NTOP):
                at, S, rows = scores(j)
                cols = (slice(0, rows), slice(at, at + S))
                link(nc.vector.tensor_tensor_scan(junk[0][0:rows, 0:S], ones16[0:rows, 0:S], y_lo[cols], 0.0, ALU.mult, ALU.add))
                link(nc.vector.scalar_tensor_tensor(y_lo[cols], junk[0][0:rows, 0:S], col(NEED, j, rows), y_lo[cols],
                                                    ALU.is_le, ALU.mult))
                link(nc.vector.scalar_tensor_tensor(SC[cols], y_hi[cols], -1.0, y_lo[cols], ALU.add, ALU.add))
                link(nc.vector.tensor_scalar(SC[cols], SC[cols], BIG, None, ALU.mult))

        def top_step(dve, link, n):
            if n == 0:
                top_prepare(dve, link)
            elif n < 16:
                top_bit(dve, link, y_hi, THI, 15 - n)
            elif n == 16:
                top_middle(dve, link)
            elif n < 33:
                top_bit(dve, link, y_lo, TLO, 32 - n)
            elif n == 33:
                top_finish(dve, link)

        def dve_maxima(dve, link, n):
            kind, i, h = ITEMS[n]
            c = 2 * (n % 2)
            if n >= 2:
                dve.wait_ge(p_tr, n - 1)
            for m in range(maps_of(n)):
                u = unit(n, m)
                dve.wait_ge(qk_mm, u + 1)
                src, top = flat(u % 2), mx[:, c + m:c + m + 1]
                if kind in PROMPT:
                    S = (i + 1) * P
                    mask = causal(i) if kind == "diff" or i not in TILES else SC[:, SC_AT[i]:SC_AT[i] + S]
                    last = nc.vector.tensor_tensor_reduce(out=Pb[:, n % 2, m, 0:S], in0=src[:, 0:S], in1=mask, scale=1.0,
                                                          scalar=-3e38, op0=ALU.add, op1=ALU.max, accum_out=top)
                elif m == 1 and kind == "sdiff":
                    last = nc.vector.tensor_tensor_reduce(out=Pb[0:32, n % 2, 0, PAST:NK], in0=src[0:32, 0:NS],
                                                          in1=c_("dmask", NS)[:, i * NS:(i + 1) * NS], scale=1.0,
                                                          scalar=-3e38, op0=ALU.add, op1=ALU.max, accum_out=top[0:32])
                else:
                    at, w = (PAST, NS) if m else (0, PAST)
                    last = nc.vector.tensor_scalar(Pb[0:32, n % 2, 0, at:at + w], src[0:32, 0:w], 0.0, -3e38, ALU.add, ALU.max,
                                                   accum_out=top[0:32])
                last.then_inc(row_max, 1)
            dve.wait_ge(row_max, unit(n) + maps_of(n))
            k = maps_of(n)
            if kind not in PROMPT:
                link(nc.vector.tensor_tensor(mx[0:32, c:c + 1], mx[0:32, c:c + 1], mx[0:32, c + 1:c + 2], ALU.max))
                k = 1
            rows = P if kind in PROMPT else 32
            nc.vector.tensor_scalar(nm[0:rows, c:c + k], mx[0:rows, c:c + k], -SCALE[kind], None, ALU.mult).then_inc(neg_max, 1)

        def dve_combine(dve, link, n):
            kind, i, h = ITEMS[n]
            S, c = (i + 1) * P, 2 * (n % 2)
            dve.wait_ge(exp_done, n + 1)
            if kind == "diff":
                link(nc.vector.reciprocal(cf[:, c:c + 2], sm[:, c:c + 2]))
                p0, p1 = (Pb[:, n % 2, m, 0:S] for m in range(2))
                nc.vector.tensor_scalar(p0, p0, cf[:, c:c + 1], None, ALU.mult)
                link(nc.vector.tensor_tensor(cf[:, c + 1:c + 2], cf[:, c + 1:c + 2], small[:, 32:33], ALU.mult))
                nc.vector.scalar_tensor_tensor(p0, p1, cf[:, c + 1:c + 2], p0, ALU.mult, ALU.add).then_inc(combined, 1)
            elif kind == "dsa":
                a = 4 * (i % 2) + h
                nc.vector.reciprocal(rs4[:, a:a + 1], sm[:, c:c + 1]).then_inc(combined, 1)
            else:
                k, p = cf[0:32, c:c + 1], Pb[0:32, n % 2, 0, 0:NK]
                link(nc.vector.reciprocal(k, sm[0:32, c:c + 1]))
                if kind == "sdiff":
                    link(nc.vector.tensor_tensor(k, k, small[0:32, 33:34], ALU.mult))
                nc.vector.tensor_scalar(p, p, k, None, ALU.mult).then_inc(combined, 1)

        def dve_tile_output(dve, link, n):
            kind, i, h = ITEMS[n]
            tile = tile_no(n)
            dve.wait_ge(pv_mm, n + 1)
            if tile >= 1:
                dve.wait_ge(o_tr, tile)
            heads = lambda x: x.rearrange("p (h d) -> p h d", d=HD)
            o = heads(bank(6 + tile % 2)[:, 0:256])
            if kind == "diff":
                link(nc.vector.tensor_copy(heads(ot), o))
                link(nc.vector.tensor_tensor(osq, ot, ot, ALU.mult))
                link(nc.vector.tensor_reduce(rs4[:, 8:12], heads(osq), AX.X, ALU.add))
                nc.vector.tensor_scalar(rs4[:, 12:16], rs4[:, 8:12], 1.0 / HD, EPS, ALU.mult, ALU.add).then_inc(ss_ready, 1)
                dve.wait_ge(head_rstd, tile + 1)
                nc.vector.tensor_tensor(heads(yt), heads(ot), rs4[:, 16:20].unsqueeze(2).to_broadcast([P, 4, HD]),
                                        ALU.mult).then_inc(yt_ready, 1)
            else:
                a = 4 * (i % 2)
                nc.vector.tensor_tensor(heads(yt), o, rs4[:, a:a + 4].unsqueeze(2).to_broadcast([P, 4, HD]),
                                        ALU.mult).then_inc(yt_ready, 1)

        def dve_item(dve, link, n):
            if n < NI:
                dve_maxima(dve, link, n)
            if 0 <= n - 1 < NI:
                dve_combine(dve, link, n - 1)
            if 0 <= n - 3 < NI and ends_tile(n - 3):
                dve_tile_output(dve, link, n - 3)

        ex = Z[:, DV + 1]
        qcz = ex[0:HD, 0:256].rearrange("p (b r) -> p b r", r=32)
        qdz = ex[:, 256:768].rearrange("p (c b r) -> p c b r", c=2, r=32)
        ka_new, dk_new = ex[:, 768:800], ex[:, 800:864].rearrange("p (c t) -> p c t", c=2)
        kflat = kring.rearrange("p s g c -> p (s g c)")

        def diff_page(b, g):
            at = (b % 2) * NPG * 512 + g * 512
            return pages[:, at:at + 512] if at < 6144 else kflat[:, at - 6144:at - 6144 + 512]

        def diff_pages(b, half):
            at = (b % 2) * NPG * 512 + half * 2048
            x = pages[:, at:at + 2048] if at < 6144 else kflat[:, 0:2048]
            return x.rearrange("p (g c) -> p g c", c=512)

        def dsa_pages(j, b):
            at = ((j % 2) * 2 + b) * NPG * 192
            return pages[:, at:at + NPG * 192].rearrange("p (g c) -> p g c", c=192)

        so = Z[:, GH + 1, 512:1024].rearrange("p (b c) -> p b c", b=DB)
        od, osqs, omean, orstd = (Z[:, GH, 512 + 64 * a:576 + 64 * a] for a in range(4))
        srelu = YF[:, 0:2 * NK].rearrange("p (g k) -> p g k", g=2)
        k_in = [sem("idx_pages0"), sem("idx_pages1")]
        d_in = [sem("diff_pages0"), sem("diff_pages1")]
        c_in = [sem("dsa_pages0"), sem("dsa_pages1")]
        pt_in = sem("page_table_loaded")
        zeroed, copied, wcol_mm, wsel_set = sem("sample_zeroed"), sem("sample_copied"), sem("wcol_product"), sem("wsel_set")
        sidx_mm, sidx_relu, sscore_mm, sscored = sem("sidx_product"), sem("sidx_relu"), sem("sscore_product"), sem("sample_scored")
        dsq, dsum_mm, dmean, drstd, dy = sem("dhead_squares"), sem("dhead_sums"), sem("dhead_means"), sem("dhead_rstd"), sem("dhead_out")
        COLS = [(0, 512), (512, 512), (1024, NS)]

        def load_page(sp, dst, src_of, no, done):
            page = sp.value_load(ptab[0:1, bass.ds(no, 1)], min_val=0, max_val=d["c_pages"].shape[0] - 1)
            sp.dma_start(dst, src_of(bass.ds(page, 1))).then_inc(done, 16)

        def sp_idx_pages(sp):
            sp.wait_ge(pt_in, 16)
            sp.wait_ge(w_used, NZ)
            for b in range(DB):
                if b >= 2:
                    sp.wait_ge(sidx_mm, b - 1)
                for g in range(NPG):
                    load_page(sp, kring[:, b % 2, g], lambda i: d["c_pages"][i, :, 0:P].rearrange("o p c -> p (o c)"),
                              b * NPG + g, k_in[b % 2])

        def item_no(kind, i):
            return ITEMS.index((kind, i, 0))

        def sp_diff_pages(sp):
            for b in range(DB):
                if b == 1:
                    sp.wait_ge(sidx_mm, DB)
                if b >= 2:
                    sp.wait_ge(pv_mm, item_no("sdiff", b - 2) + 1)
                for g in range(NPG):
                    load_page(sp, diff_page(b, g), lambda i: d["d_pages"][i].rearrange("o p c -> p (o c)"), b * NPG + g, d_in[b % 2])

        def sp_dsa_pages(sp):
            sp.wait_ge(pv_mm, item_no("sdiff", DB - 1) + 1)
            for j in range(DB // 2):
                if j >= 2:
                    sp.wait_ge(pv_mm, item_no("sdsa", j - 2) + 1)
                for b in range(2):
                    for g in range(NPG):
                        load_page(sp, dsa_pages(j, b)[:, g], lambda i: d["c_pages"][i].rearrange("o p c -> p (o c)"),
                                  (2 * j + b) * NPG + g, c_in[j % 2])

        def act_sample_copies(act):
            act.wait_ge(zeroed, 1)
            act.wait_ge(outs_stored, 16 * 7)
            for h in range(IDXH):
                half = slice(HD * (h % 2), HD * (h % 2) + HD)
                last = nc.scalar.activation(qis[HD:P, :, h], samples(Z[half, QI + h // 2]), ACT.Copy)
            last.then_inc(copied, 1)
            for h in range(4):
                half = slice(HD * (h % 2), HD * (h % 2) + HD)
                for par in range(2):
                    last = nc.scalar.activation(qcz[:, par:DB:2, par * 16 + h * 4:par * 16 + h * 4 + 4],
                                                samples(Z[half, CQ + h // 2])[:, par:DB:2], ACT.Copy)
            last.then_inc(copied, 1)
            for c in range(2):
                for r in range(4):
                    part = slice(32 * r, 32 * r + 32)
                    at = 16 * c + 4 * r
                    last = nc.scalar.activation(qdz[part, c, :, at:at + 4], samples(Z[part, DQ + c]), ACT.Copy)
            last.then_inc(copied, 1)
            nc.scalar.activation(ka_new, Z[:, KA, SEQ:NT], ACT.Copy)
            nc.scalar.activation(dk_new, Z[:, DK:DK + 2, SEQ:NT], ACT.Copy).then_inc(copied, 1)

        def pe_wcol(pe):
            for g in range(2):
                last = nc.tensor.matmul(bank(7)[:, 8 * g:8 * g + 8], c_(f"e{g}", NS), vtok[0:NS, QT, HD:HD + 8], start=True, stop=True)
            last.then_inc(wcol_mm, 1)

        def dve_wsel(dve, link):
            dve.wait_ge(wcol_mm, 1)
            for g in range(2):
                link(nc.vector.tensor_tensor_reduce(out=small[:, 20:28], in0=bank(7)[:, 8 * g:8 * g + 8], in1=c_("hsel"), scale=1.0,
                                                    scalar=0.0, op0=ALU.mult, op1=ALU.add, accum_out=wcol[:, g:g + 1]))
                nc.vector.tensor_scalar(wsel[:, g], c_(f"sel{g}"), wcol[:, g:g + 1], None, ALU.mult).then_inc(wsel_set, 1)

        def pe_sidx(pe, b):
            pe.wait_ge(k_in[b % 2], 16 * NPG * (b // 2 + 1))
            if b == 0:
                pe.wait_ge(copied, 1)
                pe.wait_ge(maps_cp, 2)
                pe.wait_ge(v_cp, QT + 1)
            if b == 4:
                pe.wait_ge(sidx_relu, 1)
            r = 32 * (b % 4)
            for j, (a, w) in enumerate(COLS):
                keys = kring[HD:P, b % 2].rearrange("p g c -> p (g c)")[:, a:a + w] if j < 2 else Z[HD:P, KA, SEQ:NT]
                last = nc.tensor.matmul(bank(4 + j)[r:r + 32, 0:w], qis[HD:P, b].rearrange("p h t -> p (h t)"), keys, start=True, stop=True)
            last.then_inc(sidx_mm, 1)

        def pe_sscore(pe):
            pe.wait_ge(wsel_set, 2)
            pe.wait_ge(sidx_relu, 2)
            pe.wait_ge(idx_relu, len(IDX))
            for j, (a, w) in enumerate(COLS):
                for g in range(2):
                    last = nc.tensor.matmul(bank(j)[0:NS, 0:w], wsel[:, g], srelu[:, g, a:a + w], start=g == 0, stop=g == 1)
            last.then_inc(sscore_mm, 1)

        def act_sidx(act, g):
            act.wait_ge(sidx_mm, 4 * g + 4)
            for j, (a, w) in enumerate(COLS):
                last = nc.scalar.activation(srelu[:, g, a:a + w], bank(4 + j)[:, 0:w], ACT.Relu, scale=IDX_SCALE)
            last.then_inc(sidx_relu, 1)

        def dve_sscore(dve):
            dve.wait_ge(sscore_mm, 1)
            for j, (a, w) in enumerate(COLS[:2]):
                nc.vector.tensor_copy(SC[0:NS, SC_S + a:SC_S + a + w], bank(j)[0:NS, 0:w])
            nc.vector.tensor_tensor(SC[0:NS, SC_S + PAST:SC_N], bank(2)[0:NS, 0:NS], c_("newmask", NS), ALU.add).then_inc(sscored, 1)

        TAIL = FIRST_DSA + 4

        def act_sdiff_tail(act):
            act.wait_ge(dsum_mm, 1)
            nc.scalar.activation(omean, bank(5)[:, 0:64], ACT.Identity, bias=eps[:, :], scale=1.0 / HD).then_inc(dmean, 1)

        def dve_sdiff_sum(dve, link):
            dve.wait_ge(so_cp, DB)
            O = so.rearrange("p b (c r) -> p c b r", c=2)
            o = od.rearrange("p (c b t) -> p c b t", c=2, t=DT)
            for h in range(4):
                c, half = h // 2, slice(HD * (h % 2), HD * (h % 2) + HD)
                last = nc.vector.tensor_tensor(o[half, c], O[half, c, :, 8 * h:8 * h + 4], O[half, c, :, 8 * h + 4:8 * h + 8], ALU.add)
            link(last)
            nc.vector.tensor_tensor(osqs, od, od, ALU.mult).then_inc(dsq, 1)

        def dve_sdiff_out(dve):
            dve.wait_ge(drstd, 1)
            for c in range(2):
                nc.vector.scalar_tensor_tensor(Z[:, PV + c, SEQ:NT], od[:, 32 * c:32 * c + 32], subln[:, :],
                                               orstd[:, 32 * c:32 * c + 32], ALU.mult, ALU.mult).then_inc(dy, 1)

        def pool_sdiff_tail(pool):
            pool.wait_ge(dmean, 1)
            nc.gpsimd.tensor_tensor(orstd, omean, neghalf[:, 0:1].to_broadcast([P, 64]), ALU.pow).then_inc(drstd, 1)

        def pe_sdiff_tail(pe):
            pe.wait_ge(dsq, 1)
            nc.tensor.matmul(bank(5)[:, 0:64], c_("headones"), osqs, start=True, stop=True).then_inc(dsum_mm, 1)

        H = Z[:, 8:16]
        W_OUT = NZ
        W_FF = W_OUT + KC
        W_PLE = W_FF + 3 * FC
        W_PG = W_PLE + 2
        EXT = 2 + SEQ + DB * 6
        tail = Z[:, 16:23].rearrange("p s t -> p (s t)")
        ge = [tail[:, a * EXT:(a + 1) * EXT] for a in range(2)]
        gv = [tail[:, a * EXT:(a + 1) * EXT] for a in range(2, 4)]
        gu = [tail[:, 4 * EXT + a * NT:4 * EXT + (a + 1) * NT] for a in range(2)]
        st_in = tail[:, 4 * EXT + 2 * NT:][:, 0:FC * DB * 2].rearrange("p (f b t) -> p f b t", f=FC, b=DB)
        st_out = TN[:, 2, 0:FC * 9 * 2].rearrange("p (f b t) -> p f b t", f=FC, b=1 + DB)
        GROUPS = FC // 2
        y_hi_cp, y_lo_cp = sem("mixer_hi"), sem("mixer_lo")
        x_again = [sem(f"x_again{k}") for k in range(KC)]
        h_out = sem("residual_mixed")
        st_loaded, st_stored = sem("ffn_state_loaded"), sem("ffn_state_stored")
        g_cp = sem("gate_copied")
        g_conv = sem("gate_convolved")
        g_silu = sem("gate_silu")
        act_mul = sem("gate_times_up")
        a_hi, a_lo = sem("mlp_hi"), sem("mlp_lo")
        d_mm, h_ffn = sem("down_product"), sem("residual_mlp")
        p_in, p_hi, p_lo = sem("ple_loaded"), sem("ple_hi"), sem("ple_lo")
        ple_mm, ple_cp = sem("ple_product"), sem("ple_copied")
        s_gate, h_ple = sem("ple_gate"), sem("residual_ple")
        mix_stored = sem("mixer_state_stored")
        y_rows = [sem("y_row0"), sem("y_row1")]
        PP = [Z[:, s] for s in (0, 1, 4, 5, 18, 19, 20, 21)]
        norm_ffn = Norm("norm_ffn", lambda k: H[:, k], "g_ffn")
        norm_ple = Norm("norm_ple", lambda k: H[:, k], "g_ple")
        norm_final = Norm("norm_final", lambda k: H[:, k], "g_final", split=False)

        def hi_next(act, n, load_no=None):
            split_hi(act, n, n % 2, n // 2 + 1 if load_no is None else load_no)

        def act_mixers(act):
            act.wait_ge(dy, 2)
            act.wait_ge(so_cp, sample_no(NI))
            act.wait_ge(o_cp, 2 * QT)
            for k in range(KC):
                nc.scalar.activation(xh[:, k], Z[:, k], ACT.Copy).then_inc(y_hi_cp, 1)

        def dve_mixers(dve):
            for k in range(KC):
                dve.wait_ge(y_hi_cp, k + 1)
                nc.vector.tensor_tensor(xl[:, k], Z[:, k], xh[:, k].bitcast(f32), ALU.subtract).then_inc(y_lo_cp, 1)

        def pool_reload(pool):
            pool.wait_ge(pv_mm, NI)
            for k in range(KC):
                pool.dma_start(H[:, k], d["xT"][k]).then_inc(x_again[k], 16)

        def pe_out(pe):
            pe.wait_ge(y_lo_cp, KC)
            for m in range(KC):
                n = W_OUT + m
                pe.wait_ge(w_lo, n + 1)
                if m >= 2:
                    pe.wait_ge(h_out, m - 1)
                block_product(n).then_inc(w_used, 1)

        def block_product(n):
            slot = n % 2
            for c in range(3):
                for k in range(KC):
                    last = three_pass(ps[slot][:, c, 0:TC], lambda w: w[:, slot, k], lambda x: x[:, k, c * TC:(c + 1) * TC],
                                      k == 0, k == KC - 1)
            return last

        def act_out(act):
            for m in range(KC):
                act.wait_ge(w_used, W_OUT + m + 1)
                hi_next(act, W_OUT + m + 2)

        def by_bank(a):
            return a.rearrange("p (c t) -> p c t", c=3)

        def dve_out(dve):
            for m in range(KC):
                dve.wait_ge(w_used, W_OUT + m + 1)
                dve.wait_ge(x_again[m], 16)
                nc.vector.tensor_tensor(by_bank(H[:, m]), by_bank(H[:, m]), ps[(W_OUT + m) % 2][:, 0:3, 0:TC], ALU.add).then_inc(h_out, 1)
                split_lo(dve, W_OUT + m + 2, (W_OUT + m) % 2)

        def gate_block(f):
            g, q = divmod(f, 2)
            return W_FF + (0 if g == 0 else 6 * g - 2) + 2 * q

        def down_block(g):
            return W_FF + (6 * g + 8 if g < GROUPS - 1 else 6 * g + 4)

        def used_before(n):
            return n + 1 - sum(1 for g in range(GROUPS) for half in range(2) if down_block(g) + half <= n)

        def pe_gate_up(pe, g):
            for f in (2 * g, 2 * g + 1):
                n = gate_block(f)
                pe.wait_ge(w_lo, n + 1)
                if f:
                    pe.wait_ge(g_cp, f)
                block_product(n).then_inc(w_used, 1)
                pe.wait_ge(w_lo, n + 2)
                if f:
                    pe.wait_ge(act_mul, f)
                block_product(n + 1).then_inc(w_used, 1)

        def pe_down(pe, g):
            pe.wait_ge(a_lo, 2 * g + 2)
            for m in range(KC):
                n = down_block(g) + m // 4
                if m % 4 == 0:
                    pe.wait_ge(w_lo, n + 1)
                for c in range(3):
                    v = (g * KC + m) * 3 + c
                    if v >= 2:
                        pe.wait_ge(h_ffn, v - 1)
                    for q in range(2):
                        for t, (w, x) in enumerate(((wh, ah), (wl, ah), (wh, al))):
                            last = nc.tensor.matmul(bank(3 + 4 * (v % 2))[:, 0:TC], w[:, n % 2, 4 * q + m % 4],
                                                    x[:, g % 2, q, c * TC:(c + 1) * TC], start=q == 0 and t == 0, stop=q == 1 and t == 2)
                    last.then_inc(d_mm, 1)

        def act_gate_up(act, g):
            for f in (2 * g, 2 * g + 1):
                n = gate_block(f)
                act.wait_ge(w_used, used_before(n))
                hi_next(act, n + 2)
                if f >= 2:
                    act.wait_ge(g_conv, f - 1)
                e, gate = ge[f % 2], ps[n % 2]
                nc.scalar.activation(e[:, 2:2 + 2 * TC].rearrange("p (c t) -> p c t", c=2), gate[:, 0:2, 0:TC], ACT.Copy)
                nc.scalar.activation(e[:, 2 + 2 * TC:2 + SEQ], gate[:, 2, 0:SEQ - 2 * TC], ACT.Copy)
                nc.scalar.activation(e[:, 2 + SEQ:].rearrange("p (b t) -> p b t", t=6)[:, :, 2:6],
                                     gate[:, 2, SEQ - 2 * TC:TC].rearrange("p (b t) -> p b t", t=DT), ACT.Copy).then_inc(g_cp, 1)
                act.wait_ge(g_conv, f + 1)
                nc.scalar.activation(gv[f % 2][:, 0:EXT - 2], gv[f % 2][:, 0:EXT - 2], ACT.Silu).then_inc(g_silu, 1)
                act.wait_ge(w_used, used_before(n + 1))
                hi_next(act, n + 3)
                act.wait_ge(act_mul, f + 1)
                if g >= 2:
                    act.wait_ge(d_mm, (g - 1) * KC * 3)
                nc.scalar.activation(ah[:, g % 2, f % 2], gu[f % 2], ACT.Copy).then_inc(a_hi, 1)

        def act_down(act, g):
            for half in range(2):
                act.wait_ge(d_mm, g * KC * 3 + 12 * (half + 1))
                if down_block(g) + half + 2 < NW:
                    hi_next(act, down_block(g) + half + 2)

        def dve_gate_up(dve, link, g):
            for f in (2 * g, 2 * g + 1):
                n = gate_block(f)
                split_lo(dve, n + 2, n % 2)
                e, v = ge[f % 2], gv[f % 2]
                es = e[:, 2 + SEQ:].rearrange("p (b t) -> p b t", t=6)
                if f < 2:
                    nc.vector.memset(e[:, 0:2], 0.0)
                nc.vector.tensor_copy(es[:, :, 0:2], st_in[:, f])
                dve.wait_ge(g_cp, f + 1)
                nc.vector.tensor_copy(st_out[:, f, 0], e[:, SEQ:SEQ + 2])
                link(nc.vector.tensor_copy(st_out[:, f, 1:], es[:, :, 4:6]))
                w = p_("conv_ffn")[:, 3 * f:3 * f + 3]
                link(nc.vector.tensor_scalar(v[:, 0:EXT - 2], e[:, 0:EXT - 2], w[:, 0:1], None, ALU.mult))
                link(nc.vector.scalar_tensor_tensor(v[:, 0:EXT - 2], e[:, 1:EXT - 1], w[:, 1:2], v[:, 0:EXT - 2], ALU.mult, ALU.add))
                nc.vector.scalar_tensor_tensor(v[:, 0:EXT - 2], e[:, 2:EXT], w[:, 2:3], v[:, 0:EXT - 2], ALU.mult, ALU.add).then_inc(g_conv, 1)
                split_lo(dve, n + 3, (n + 1) % 2)
                dve.wait_ge(g_silu, f + 1)
                up, u = ps[(n + 1) % 2], gu[f % 2]
                nc.vector.tensor_tensor(u[:, 0:2 * TC].rearrange("p (c t) -> p c t", c=2), v[:, 0:2 * TC].rearrange("p (c t) -> p c t", c=2),
                                        up[:, 0:2, 0:TC], ALU.mult)
                nc.vector.tensor_tensor(u[:, 2 * TC:SEQ], v[:, 2 * TC:SEQ], up[:, 2, 0:SEQ - 2 * TC], ALU.mult)
                nc.vector.tensor_tensor(u[:, SEQ:NT].rearrange("p (b t) -> p b t", t=DT),
                                        v[:, 2 + SEQ:EXT].rearrange("p (b t) -> p b t", t=6)[:, :, 0:DT],
                                        up[:, 2, SEQ - 2 * TC:TC].rearrange("p (b t) -> p b t", t=DT), ALU.mult).then_inc(act_mul, 1)
                dve.wait_ge(a_hi, f + 1)
                nc.vector.tensor_tensor(al[:, g % 2, f % 2], u, ah[:, g % 2, f % 2].bitcast(f32), ALU.subtract).then_inc(a_lo, 1)

        def dve_down(dve, g):
            for m in range(KC):
                for c in range(3):
                    v = (g * KC + m) * 3 + c
                    dve.wait_ge(d_mm, v + 1)
                    if v >= KC * 3:
                        dve.wait_ge(h_ffn, v + 1 - KC * 3)
                    cols = H[:, m, c * TC:(c + 1) * TC]
                    nc.vector.tensor_tensor(cols, cols, bank(3 + 4 * (v % 2))[:, 0:TC], ALU.add).then_inc(h_ffn, 1)
                if m % 4 == 3 and down_block(g) + m // 4 + 2 < NW:
                    split_lo(dve, down_block(g) + m // 4 + 2, (down_block(g) + m // 4) % 2)

        ALL_FF = GROUPS * KC * 3

        def pool_ple(pool):
            pool.wait_ge(act_mul, FC)
            pool.wait_ge(a_lo, FC)
            for k in range(2):
                pool.dma_start(Z[:, 16 + k], d["pT"][k]).then_inc(p_in, 16)
            pool.dma_start(d["st_ffn"], st_out).then_inc(st_stored, 16)

        def act_ple_split(act):
            act.wait_ge(p_in, 32)
            act.wait_ge(d_mm, ALL_FF)
            for k in range(2):
                nc.scalar.activation(ah[:, 1, k], Z[:, 16 + k], ACT.Copy).then_inc(p_hi, 1)

        def dve_ple_split(dve):
            for k in range(2):
                dve.wait_ge(p_hi, k + 1)
                nc.vector.tensor_tensor(al[:, 1, k], Z[:, 16 + k], ah[:, 1, k].bitcast(f32), ALU.subtract).then_inc(p_lo, 1)

        def pe_ple(pe):
            pe.wait_ge(p_lo, 2)
            pe.wait_ge(h_ffn, ALL_FF)
            for m in range(KC):
                n = W_PLE + m // 4
                pe.wait_ge(w_lo, n + 1)
                for c in range(3):
                    v = 3 * m + c
                    if v >= 2:
                        pe.wait_ge(ple_cp, v - 1)
                    for q in range(2):
                        for t, (w, x) in enumerate(((wh, ah), (wl, ah), (wh, al))):
                            last = nc.tensor.matmul(bank(3 + 4 * (v % 2))[:, 0:TC], w[:, n % 2, 4 * q + m % 4],
                                                    x[:, 1, q, c * TC:(c + 1) * TC], start=q == 0 and t == 0, stop=q == 1 and t == 2)
                    last.then_inc(ple_mm, 1)

        def act_ple(act):
            for m in range(KC):
                for c in range(3):
                    v = 3 * m + c
                    act.wait_ge(ple_mm, v + 1)
                    nc.scalar.activation(PP[m][:, c * TC:(c + 1) * TC], bank(3 + 4 * (v % 2))[:, 0:TC], ACT.Copy).then_inc(ple_cp, 1)
                if m % 4 == 3:
                    hi_next(act, W_PLE + m // 4 + 2)

        def pe_ple_gate(pe):
            pe.wait_ge(norm_ple.lo, KC)
            for m in range(KC):
                pe.wait_ge(w_lo, W_PG + m + 1)
                if m >= 2:
                    pe.wait_ge(s_gate, m - 1)
                block_product(W_PG + m).then_inc(w_used, 1)

        def act_ple_gate(act):
            for m in range(KC):
                act.wait_ge(w_used, used_before(W_PLE - 1) + m + 1)
                if m + 2 < KC:
                    hi_next(act, W_PG + m + 2)
                if m >= 2:
                    act.wait_ge(h_ple, m - 1)
                nc.scalar.activation(by_bank(TN[:, 1 + m % 2]), ps[(W_PG + m) % 2][:, 0:3, 0:TC], ACT.Sigmoid).then_inc(s_gate, 1)

        def dve_ple_gate(dve, link):
            for m in range(KC):
                if m + 2 < KC:
                    split_lo(dve, W_PG + m + 2, (W_PG + m) % 2)
                dve.wait_ge(s_gate, m + 1)
                link(nc.vector.tensor_tensor(TN[:, 1 + m % 2], TN[:, 1 + m % 2], PP[m], ALU.mult))
                nc.vector.tensor_tensor(H[:, m], H[:, m], TN[:, 1 + m % 2], ALU.add).then_inc(h_ple, 1)

        def final_row_free(dve, k):
            dve.wait_ge(y_rows[k % 2], 16 * (k // 2))
        norm_final.wait_row = final_row_free

        def sp_store(sp):
            for k in range(KC):
                sp.wait_ge(norm_final.xn, k + 1)
                sp.dma_start(d["y"][k], TN[:, 1 + k % 2]).then_inc(y_rows[k % 2], 16)

        block = ctx.enter_context(nc.Block())

        @block.sync
        def _(sp):
            sp.dma_start(cst[:, :], d["consts"]).then_inc(s_const, 16)
            sp.dma_start(par[:, :], d["params"]).then_inc(s_const, 16)
            sp.dma_start(ptab[:, :], d["page_table"]).then_inc(pt_in, 16)
            for k in range(KC):
                sp.dma_start(Z[:, k], d["xT"][k]).then_inc(x_loaded[k], 16)
            for n in range(2):
                sp.dma_start(wr[:, n], d["weights"][n]).then_inc(w_raw[n], 16)
            def load_block(n, slot):
                sp.dma_start(wr[:, slot], d["weights"][bass.ds(n, 1)].rearrange("o p k m -> p (o k) m")).then_inc(w_raw[slot], 16)

            with sp.Fori(1, (NZ - 1) // 2) as j:
                for slot in range(2):
                    sp.wait_ge(w_lo, 2 * j + slot - 1)
                    load_block(2 * j + slot, slot)
            sp.wait_ge(w_lo, NZ - 2)
            load_block(NZ - 1, 0)

            sp_idx_pages(sp)
            sp_diff_pages(sp)
            sp_dsa_pages(sp)
            sp.wait_ge(pv_mm, NI)
            for n in (W_OUT, W_OUT + 1):
                load_block(n, n % 2)
            with sp.Fori((W_OUT + 1) // 2, NW // 2) as j:
                for n, slot in ((2 * j + 1, 1), (2 * j + 2, 0)):
                    sp.wait_ge(w_lo, n - 1)
                    load_block(n, slot)
            sp_store(sp)
            for a in range(2):
                sp.wait_ge(y_rows[a], 16 * KC // 2)


        @block.gpsimd
        def _(pool):
            pool.wait_ge(ones_set, 1)
            norm_mix.pool(pool)
            pool.wait_ge(d_mixed, 2)
            nc.gpsimd.memset(CM, 0.0).then_inc(masks_set, 1)
            pool.wait_ge(masks_set, 1)
            nc.gpsimd.affine_select(out=CM[:, SEQ - P:SEQ], in_=CM[:, SEQ - P:SEQ], compare_op=ALU.is_ge, fill=-BIG, base=0,
                                    pattern=[[-1, P]], channel_multiplier=1).then_inc(masks_set, 1)
            pool.wait_ge(evac, NZ)
            outs = [(d["c_k"], Z[0:HD, KA]), (d["c_idx"], Z[HD:P, KA]), (d["c_v"], Z[0:HD, CV])]
            outs += [(d[name][j], Z[:, at + j]) for name, at in (("d_k", DK), ("d_v", DV)) for j in range(2)]
            for dst, src in outs:
                pool.dma_start(dst, src).then_inc(outs_stored, 16)
            for tile in range(QT):
                pool.wait_ge(ss_ready, tile + 1)
                nc.gpsimd.tensor_tensor(rs4[:, 16:20], rs4[:, 12:16], neghalf[:, 0:4], ALU.pow).then_inc(head_rstd, 1)
            pool_sdiff_tail(pool)
            pool_reload(pool)
            pool.dma_start(st_in, d["st_ffn_in"]).then_inc(st_loaded, 16)
            pool.dma_start(d["st_mix"], ST[:, :, :, :]).then_inc(mix_stored, 16)
            norm_ffn.pool(pool)
            pool_ple(pool)
            norm_ple.pool(pool)
            norm_final.pool(pool)
            pool.wait_ge(outs_stored, 16 * len(outs))
            pool.wait_ge(mix_stored, 16)
            pool.wait_ge(st_stored, 16)


        @block.scalar
        def _(act):
            act.wait_ge(ones_set, 1)
            norm_mix.act(act, lambda e, k: e.wait_ge(x_loaded[k], 16))
            for n in range(2):
                split_hi(act, n, n, 1)
            def step(n, slot, load_no):
                act.wait_ge(w_used, n + 1)
                if type(n) is not int or n + 2 < NZ:
                    split_hi(act, n + 2, slot, load_no)
                nc.scalar.activation(z_slot(n), ps[slot][:, 0:3, 0:TC], ACT.Copy).then_inc(evac, 1)

            def z_slot(n):
                return (Z[:, n] if type(n) is int else Z[:, bass.ds(n, 1)].rearrange("p o t -> p (o t)")).rearrange("p (c t) -> p c t", c=3)
            with act.Fori(0, (NZ - 3) // 2) as j:
                for slot in range(2):
                    step(2 * j + slot, slot, j + 2)
            for n in range(NZ - 3, NZ):
                step(n, n % 2, n // 2 + 2)
            act_values(act)
            act_lambda(act)
            act_sample_copies(act)
            act_maps(act)
            act_idx(act)
            for n in range(NI + 5):
                act_item(act, n)
                if n == TAIL + 1:
                    act_sdiff_tail(act)
            act_mixers(act)
            for n in (W_OUT, W_OUT + 1):
                hi_next(act, n)
            act_out(act)
            norm_ffn.act(act, lambda e, k: e.wait_ge(h_out, k + 1))
            act_gate_up(act, 0)
            for g in range(GROUPS):
                if g + 1 < GROUPS:
                    act_gate_up(act, g + 1)
                act_down(act, g)
            act_ple_split(act)
            act.wait_ge(st_stored, 16)
            norm_ple.act(act, lambda e, k: e.wait_ge(h_ffn, ALL_FF))
            act_ple(act)
            act_ple_gate(act)
            norm_final.act(act, lambda e, k: e.wait_ge(h_ple, KC if k else 1))


        @block.vector
        def _(dve):
            nc.vector.memset(eps[:, :], EPS)
            nc.vector.memset(neghalf[:, :], -0.5)
            nc.vector.memset(ones[:, :], 1.0).then_inc(ones_set, 1)
            dve.wait_ge(s_const, 32)
            norm_mix.dve(dve)
            for n in range(2):
                split_lo(dve, n, n)
            with dve.Fori(1, 6) as j:
                for slot in range(2):
                    split_lo(dve, 2 * j + slot, slot)
            link = Chain(dve, "dve_chain").link
            for n in range(12, NZ):
                split_lo(dve, n, n % 2)
                if n in (13, 14):
                    dve_conv(dve, link, n - 13)
                if n in (15, 17):
                    dve_pool(dve, link, (n - 15) // 2)
            dve.wait_ge(outs_stored, 16 * 7)
            dve.wait_ge(v_cp, QT + 1)
            nc.vector.memset(ex[:, 0:768], 0.0).then_inc(zeroed, 1)
            dve.wait_ge(masks_set, 2)
            nc.vector.tensor_scalar(CP, CM[:, SEQ - P:SEQ], BIG, None, ALU.add)
            link(nc.vector.tensor_scalar(newcp, c_("newmask"), BIG, None, ALU.add))
            dve_lambda(dve, link)
            dve_wsel(dve, link)
            dve_idx(dve)
            dve_sscore(dve)
            for n in range(NI + 5):
                dve_item(dve, link, n)
                if n < FIRST_DSA:
                    top_step(dve, link, n)
                if n == TAIL:
                    dve_sdiff_sum(dve, link)
                if n == TAIL + 2:
                    dve_sdiff_out(dve)
            dve_mixers(dve)
            for n in (W_OUT, W_OUT + 1):
                split_lo(dve, n, n % 2)
            dve_out(dve)
            norm_ffn.dve(dve)
            dve.wait_ge(st_loaded, 16)
            dve_gate_up(dve, link, 0)
            for g in range(GROUPS):
                if g + 1 < GROUPS:
                    dve_gate_up(dve, link, g + 1)
                dve_down(dve, g)
            dve_ple_split(dve)
            norm_ple.dve(dve)
            for half in range(2):
                split_lo(dve, W_PG + half, (W_PG + half) % 2)
            dve_ple_gate(dve, link)
            norm_final.dve(dve)


        @block.tensor
        def _(pe):
            pe.wait_ge(ones_set, 1)
            norm_mix.pe(pe)
            pe.wait_ge(norm_mix.lo, KC)
            for n in range(2):
                project_pe(pe, n, n, True)
            with pe.Fori(1, (NZ - 1) // 2) as j:
                for slot in range(2):
                    project_pe(pe, 2 * j + slot, slot, False)
            project_pe(pe, NZ - 1, (NZ - 1) % 2, False)
            pe.wait_ge(evac, NZ)
            pe_values(pe)
            pe_maps(pe)
            pe.wait_ge(masks_set, 2)
            pe.wait_ge(v_cp, QT + 1)
            pe_wcol(pe)
            pe.wait_ge(maps_cp, 2)
            pe_idx(pe)
            pe_sscore(pe)
            pe.wait_ge(sscored, 1)
            for n in range(NI + 5):
                if n == TAIL + 1:
                    pe_sdiff_tail(pe)
                pe_item(pe, n)
            pe_out(pe)
            norm_ffn.pe(pe)
            pe.wait_ge(norm_ffn.lo, KC)
            pe_gate_up(pe, 0)
            for g in range(GROUPS):
                if g + 1 < GROUPS:
                    pe_gate_up(pe, g + 1)
                pe_down(pe, g)
            norm_ple.pe(pe)
            pe_ple(pe)
            pe_ple_gate(pe)
            norm_final.pe(pe)





def weight_blocks(w_in, w_out, w_gate, w_up, w_down, w_ple, w_ple_gate):
    def rows(w):
        return w.reshape(KC, P, P).transpose(1, 0, 2)

    out = []
    for pieces in IN_COLS:
        w = np.concatenate([w_in[:, a:a + n] for a, n in pieces], axis=1)
        out.append(rows(np.pad(w, ((0, 0), (0, P - w.shape[1])))))
    out += [rows(w_out[:, m * P:(m + 1) * P]) for m in range(KC)]

    def gate_up(g):
        return [rows(w[:, f * P:(f + 1) * P]) for f in (2 * g, 2 * g + 1) for w in (w_gate, w_up)]

    def down(g):
        w = w_down[2 * g * P:(2 * g + 2) * P].reshape(2, P, 2, 4, P)
        return [w[:, :, half].transpose(1, 0, 2, 3).reshape(P, KC, P) for half in range(2)]

    out += gate_up(0)
    for g in range(FC // 2 - 1):
        out += gate_up(g + 1) + down(g)
    out += down(FC // 2 - 1)
    w = w_ple.reshape(2, P, 2, 4, P)
    out += [w[:, :, half].transpose(1, 0, 2, 3).reshape(P, KC, P) for half in range(2)]
    out += [rows(w_ple_gate[:, m * P:(m + 1) * P]) for m in range(KC)]
    assert len(out) == NW
    return np.stack(out)


def constants():
    c = np.zeros((P, CONST_N), np.float32)

    def put(name, a):
        at, n = CONST[name]
        c[0:a.shape[0], at:at + n] = a

    tok = np.arange(NS)
    put("ident", np.eye(P))
    row = np.arange(P)
    put("hsel", (row[:, None] % 32 // 4 == np.arange(8)[None]))
    put("headones", (row[:, None] // HD == row[None] // HD))
    for g in range(2):
        sel = (4 * g + row[:, None] // 32 == tok[None] // DT) & (row[:, None] % DT == tok[None] % DT)
        put(f"sel{g}", sel)
        put(f"e{g}", sel.T)
    own = (np.arange(DB)[None, :, None] == tok // DT) & (tok % DT <= tok[:, None, None] % DT)
    put("dmask", np.where(own, 0.0, -BIG).reshape(NS, DB * NS))
    rep = (row[None] // 16 == tok[:, None] // DT) & (row[None] % DT == tok[:, None] % DT)
    put("rep", rep)
    put("newmask", np.where((tok[:, None] // DT == tok[None] // DT) & (tok[None] % DT <= tok[:, None] % DT), 0.0, -BIG))
    m = row % 8 // 4
    put("lam_a", (m == 0)[:, None])
    put("lam_b", (m == 1)[:, None])
    win = np.array([[2, 8], [4, 16]])[row // HD]
    put("inv_w", 1.0 / win)
    cnt = np.minimum(win[:, :, None], np.arange(1, 17)[None, None])
    put("inv_cnt", (1.0 / cnt).reshape(P, 32))
    valid = np.stack([i * P + row + 1 for i in TILES] + [PAST + row % DT + 1], 1)
    kneg = valid - TOPK + 1
    put("kneg", kneg)
    put("kdiff", TOPK - kneg)
    return c


def parameters(i):
    p = np.zeros((P, PARAM_N), np.float32)

    def put(name, a):
        at, n = PARAM[name]
        p[0:a.shape[0], at:at + n] = a.reshape(a.shape[0], n)

    put("g_mix", i["norm_mix"][0].reshape(KC, P).T)
    put("g_ffn", i["norm_ffn"][0].reshape(KC, P).T)
    put("g_ple", i["norm_ple"][0].reshape(KC, P).T)
    put("g_final", i["norm_final"].reshape(KC, P).T)
    put("conv_a", i["conv_a"][0].reshape(3, 2, P).transpose(2, 1, 0))
    put("pool_scale", i["pool_scale"][0].reshape(2, P).T)
    put("conv_ffn", i["conv_ffn"][0].reshape(3, FC, P).transpose(2, 1, 0))
    put("subln", np.tile(i["diff_subln"][0], 2)[:, None])
    put("lam", np.broadcast_to(i["diff_lambda"][0].reshape(1, P), (P, P)))
    maps = np.zeros((P, 2, P), np.float32)
    for g in range(4):
        r = (g % 2) * HD
        maps[r:r + HD, g // 2, r:r + HD] = i["pool_maps"][0, g]
    put("maps", maps)
    put("st_conv", i["state_conv_a"][0].reshape(DB, 2, 2, P).transpose(3, 2, 0, 1))
    put("st_pool", i["state_pool"][0].reshape(DB, 15, 2, P).transpose(3, 2, 0, 1))
    return p


def kernel(**inputs):
    import numpy as _np
    import concourse.bacc as _bacc
    from concourse import mybir as _mybir
    from concourse.bass_utils import run_bass_kernel_spmd as _run

    i = {k: _np.asarray(v) for k, v in inputs.items()}
    xT = _np.concatenate([i["x_prompt"][0].T, i["x_sample"].reshape(NS, D).T], axis=1).reshape(KC, P, NT)
    pT = _np.concatenate([i["p_prompt"][0, 0].T, i["p_sample"][0].reshape(NS, PLE).T], axis=1).reshape(2, P, NT)
    ck, cv, ci = (i[n][:, 0] for n in ("cache_c_k", "cache_c_v", "cache_c_idx"))
    c_pages = _np.concatenate([_np.concatenate([ck, ci], axis=2).transpose(0, 2, 1), cv], axis=2)
    dk, dv = i["cache_d_k"][:, 0], i["cache_d_v"][:, 0]
    n_phys = dk.shape[0]
    dkT = dk.reshape(n_phys, PAGE, 2, P).transpose(0, 3, 2, 1).reshape(n_phys, P, 2 * PAGE)
    d_pages = _np.concatenate([dkT, dv.reshape(n_phys, PAGE, 256)], axis=2)
    arrays = {
        "xT": xT, "pT": pT, "c_pages": c_pages, "d_pages": d_pages,
        "weights": weight_blocks(i["w_in"][0], i["w_out"][0], i["w_gate"][0], i["w_up"][0], i["w_down"][0],
                                 i["w_ple"][0], i["w_ple_gate"][0]),
        "consts": constants(), "params": parameters(i), 
        "st_ffn_in": i["state_ffn"][0].reshape(DB, 2, FC, P).transpose(3, 2, 0, 1), "page_table": i["page_table"].reshape(1, -1),
    }
    arrays = {k: _np.ascontiguousarray(v) for k, v in arrays.items()}
    nc = _bacc.Bacc("TRN2", target_bir_lowering=False, num_devices=1)
    d = {}
    for name, a in arrays.items():
        d[name] = nc.dram_tensor(f"in_{name}", a.shape, _mybir.dt.from_np(a.dtype), kind="ExternalInput").ap()
    for name, shape in OUTS.items():
        d[name] = nc.dram_tensor(f"out_{name}", shape, _mybir.dt.float32, kind="ExternalOutput").ap()
    build(nc, d)
    r = _run(nc, [{f"in_{k}": v for k, v in arrays.items()}], core_ids=[0]).results[0]
    o = {name: _np.asarray(r[f"out_{name}"]) for name in OUTS}

    def rows(a, width):
        a = a.reshape(-1, NT)[0:width]
        return a[:, :SEQ].T, a[:, SEQ:].T.reshape(DB, DT, width)

    y_p, y_s = rows(o["y"], D)
    res = [y_p[None], y_s]
    st = o["st_mix"]
    conv = st[:, :, :, 0:2]
    pool = st[:, :, :, 2:17]
    for s in (conv, pool):
        s = s.transpose(2, 3, 1, 0).reshape(1 + DB, s.shape[3], 256)
        res += [s[0:1][None], s[1:][None]]
    s = o["st_ffn"].reshape(P, FC, 1 + DB, 2).transpose(2, 3, 1, 0).reshape(1 + DB, 2, FF)
    res += [s[0:1][None], s[1:][None]]
    for a in (o["c_k"], o["c_v"], o["c_idx"]):
        p, s = rows(a, HD)
        res += [p[None, None], s[:, None]]
    for a in (o["d_k"], o["d_v"]):
        p, s = rows(a, 256)
        res += [p.reshape(1, 1, SEQ, 4, HD), s.reshape(DB, 1, DT, 4, HD)]
    return tuple(_np.ascontiguousarray(a) for a in res)
```

```python
import math
from contextlib import ExitStack

import numpy as np
import concourse.bass as bass
from concourse import mybir

P = 128
D = 1024
KC = D // P
SEQ, DB, DT = 1024, 8, 4
NS = DB * DT
NT = SEQ + NS
TC = NT // 3
QT = SEQ // P
PAST, PAGE = 1024, 128
NPG = PAST // PAGE
NK = PAST + NS
FF = 2816
FC = FF // P
PLE = 256
TOPK = 256
HD = 64
IDXH = 8
IDX_SCALE = IDXH ** -0.5 * HD ** -0.5
DSA_SCALE = HD ** -0.5
DIFF_SCALE = 32 ** -0.5
LAM_INIT = 0.8 - 0.6 * math.exp(0.0)
EPS = 1e-6
BIG = 1e30

GB, GC, GH, PV = 0, 2, 4, 6
KA, QI, CQ, DK, DQ, CV, DV, KB = 8, 9, 13, 15, 17, 19, 20, 22
NZ = 22
IN_COLS = ([[(128 * j, 128)] for j in range(8)]
           + [[(1280, 64), (1928, 64)]]
           + [[(1408 + 128 * j, 128)] for j in range(4)]
           + [[(1024, 128)], [(1152, 128)]]
           + [[(2248, 128)], [(2376, 128)], [(1992, 128)], [(2120, 128)]]
           + [[(1344, 64), (1920, 8)], [(2504, 128)], [(2632, 128)]])
TILES = list(range(TOPK // P, QT))
SC_AT = {i: sum((j + 1) * P for j in TILES if j < i) for i in TILES}
SC_S = sum((j + 1) * P for j in TILES)
SC_N = SC_S + NK
NTOP = len(TILES) + 1
ACT_TOP = [NTOP - 2, NTOP - 3, NTOP - 4]
DVE_TOP = [NTOP - 1, 0, 2, 1]


NW = NZ + KC + 3 * FC + 2 + KC
OUTS = {"y": (KC, P, NT), "st_mix": (P, 2, 1 + DB, 17), "st_ffn": (P, FC, 1 + DB, 2), "c_k": (HD, NT), "c_v": (HD, NT),
        "c_idx": (HD, NT), "d_k": (2, P, NT), "d_v": (2, P, NT)}


def layout(pieces):
    at, out = 0, {}
    for name, n in pieces:
        out[name] = (at, n)
        at += n
    return out, at


CONST, CONST_N = layout([("ident", P), ("hsel", 8), ("sel0", 32), ("sel1", 32), ("e0", P), ("e1", P),
                         ("rep", P), ("newmask", NS), ("dmask", DB * NS), ("lam_a", 1), ("lam_b", 1),
                         ("inv_w", 2), ("inv_cnt", 32), ("headones", P), ("kneg", NTOP), ("kdiff", NTOP), ("kmul", NTOP), ("kadd", NTOP)])
PARAM, PARAM_N = layout([("g_mix", KC), ("g_ffn", KC), ("g_ple", KC), ("g_final", KC), ("conv_a", 6),
                         ("pool_scale", 2), ("conv_ffn", FC * 3), ("subln", 1), ("lam", P),
                         ("maps", 2 * P), ("st_conv", 2 * DB * 2), ("st_pool", 2 * DB * 15)])


def build(nc, d):
    f32, f32r, i32 = mybir.dt.float32, mybir.dt.float32r, mybir.dt.int32
    u16, bf16 = mybir.dt.uint16, mybir.dt.bfloat16
    ALU, ACT, AX = mybir.AluOpType, mybir.ActivationFunctionType, mybir.AxisListType
    with ExitStack() as ctx:
        def sb(name, shape, dt=f32):
            return ctx.enter_context(nc.sbuf_tensor(name, shape, dt))

        def sem(name):
            return ctx.enter_context(nc.semaphore(name))

        arena_at = (nc.sbuf_base + 31) // 32 * 32
        arena = sb("arena", [P, 2 * KC * NT])
        xh = nc.alloc_sbuf_tensor_at("xh", [P, KC, NT], f32r, offset=arena_at)
        xl = nc.alloc_sbuf_tensor_at("xl", [P, KC, NT], f32r, offset=arena_at + 4 * KC * NT)
        taken = [0]

        def carve(n):
            taken[0] += n
            assert taken[0] <= 2 * KC * NT
            return arena[:, taken[0] - n:taken[0]]

        vtok = carve((QT + 1) * 384).rearrange("p (t f) -> p t f", f=384)
        SC = carve(SC_N)
        YF = carve(SC_N)
        YY = YF.bitcast(u16)
        y_hi, y_lo = YY[:, 0:SC_N], YY[:, SC_N:2 * SC_N]
        kring = carve(2 * NPG * PAGE).rearrange("p (s g c) -> p s g c", s=2, c=PAGE)
        comb_at = taken[0] - 2 * NPG * PAGE
        qis = carve(IDXH * NS).rearrange("p (b h t) -> p b h t", b=DB, h=IDXH)
        comb = arena[:, comb_at:comb_at + 2 * NT].rearrange("p (a t) -> p a t", a=2)
        wsel = carve(2 * NS).rearrange("p (g t) -> p g t", g=2)
        wcol = carve(2)
        tk = carve(13 * NTOP).rearrange("p (a j) -> p a j", j=NTOP)
        mx = carve(4)
        nm = carve(4)
        sm = carve(4)
        cf = carve(4)
        rs4 = carve(20)
        lamw = carve(4)
        CP = carve(P)
        newcp = carve(NS)
        ST = sb("ST", [P, 2, 1 + DB, 17])
        z_at = (nc.sbuf_base + 31) // 32 * 32
        Z = sb("Z", [P, NZ + 1, NT])
        ah = nc.alloc_sbuf_tensor_at("ah", [P, 2, 2, NT], f32r, offset=z_at)
        al = nc.alloc_sbuf_tensor_at("al", [P, 2, 2, NT], f32r, offset=z_at + 16 * NT)
        kstack = nc.alloc_sbuf_tensor_at("kstack", [P, NT], f32r, offset=z_at + 4 * NT * KB)
        dq_stack = nc.alloc_sbuf_tensor_at("dq_stack", [P, 2, 2, 4, P], f32r, offset=z_at + 4 * NT * DK)
        ring_at = (nc.sbuf_base + 31) // 32 * 32
        pages = sb("pages", [P, 3 * 2 * KC * P])
        wr = nc.alloc_sbuf_tensor_at("wr", [P, 2, KC, P], f32, offset=ring_at)
        wh = nc.alloc_sbuf_tensor_at("wh", [P, 2, KC, P], f32r, offset=ring_at + 8 * KC * P)
        wl = nc.alloc_sbuf_tensor_at("wl", [P, 2, KC, P], f32r, offset=ring_at + 16 * KC * P)
        cst = sb("cst", [P, CONST_N])
        par = sb("par", [P, PARAM_N])
        ones = sb("ones", [P, P])
        ptab = sb("ptab", [1, DB * NPG], i32)
        TN = sb("TN", [P, 3, NT])
        small = sb("small", [P, 40])
        ps = [ctx.enter_context(nc.psum_tensor(f"ps{j}", [P, 4, 512], f32)) for j in range(2)]

        def c_(name, rows=P):
            at, n = CONST[name]
            return cst[0:rows, at:at + n]

        def p_(name):
            at, n = PARAM[name]
            return par[:, at:at + n]

        class Chain:

            def __init__(self, eng, name):
                self.eng, self.sem, self.n, self.offset = eng, sem(name), 0, 0

            def link(self, ins):
                self.n += 1
                ins.then_inc(self.sem, 1)
                self.eng.wait_ge(self.sem, self.offset + self.n)

            def enter(self, passes, links):
                self.start, self.passes, self.links = self.n, passes, links

            def pass_of(self, j):
                self.offset = self.links * j

            def leave(self):
                assert self.n == self.start + self.links
                self.n, self.offset = self.start + self.passes * self.links, 0

            def mark(self, ins):
                self.n += 1
                ins.then_inc(self.sem, 1)
                return self.n

            def until(self, mark):
                self.eng.wait_ge(self.sem, mark)

        s_const = sem("constants_loaded")
        outs_stored = sem("outputs_stored")
        x_loaded = [sem(f"x_loaded{k}") for k in range(KC)]
        ones_set = sem("ones_set")

        w_raw = [sem("w_raw0"), sem("w_raw1")]
        w_hi = sem("w_hi_split")
        w_lo = sem("w_lo_split")
        w_used = sem("w_used")
        evac = sem("evacuated")

        def split_hi(act, n, slot, load_no):
            act.wait_ge(w_raw[slot], 16 * load_no)
            nc.scalar.activation(wh[:, slot], wr[:, slot], ACT.Copy).then_inc(w_hi, 1)

        def split_lo(dve, n, slot):
            dve.wait_ge(w_hi, n + 1)
            nc.vector.tensor_tensor(wl[:, slot], wr[:, slot], wh[:, slot].bitcast(f32), ALU.subtract).then_inc(w_lo, 1)

        def three_pass(out, w_at, x_at, start, stop):
            for t, (w, x) in enumerate(((wh, xh), (wl, xh), (wh, xl))):
                last = nc.tensor.matmul(out, w_at(w), x_at(x), start=start and t == 0, stop=stop and t == 2)
            return last

        def bank(j):
            return ps[j // 4][:, j % 4]

        class Norm:
            def __init__(self, name, src, gain, split=True, pair=1):
                self.src, self.gain, self.split = src, p_(gain), split
                self.factors = ps[pair][:, :, :].rearrange("p a b -> p (a b)")[:, 0:NT]
                self.sq, self.sum, self.stat = sem(name + "_squares"), sem(name + "_sums"), sem(name + "_stat")
                self.std, self.diag, self.bcast = sem(name + "_std"), sem(name + "_diag"), sem(name + "_bcast")
                self.xn, self.hi, self.lo = sem(name + "_scaled"), sem(name + "_hi"), sem(name + "_lo")
                self.rec = sem(name + "_rec")

            def square(self, act, k):
                if k >= 3:
                    act.wait_ge(self.sum, k - 2)
                dst = TN[:, 0] if k == 0 else TN[:, 1 + k % 2]
                nc.scalar.activation(dst, self.src(k), ACT.Square).then_inc(self.sq, 1)

            def add(self, dve, k):
                dve.wait_ge(self.sq, k + 1)
                if k > 1:
                    dve.wait_ge(self.sum, k - 1)
                nc.vector.tensor_tensor(TN[:, 0], TN[:, 0], TN[:, 1 + k % 2], ALU.add).then_inc(self.sum, 1)

            def act(self, act):
                act.wait_ge(self.stat, 1)
                nc.scalar.activation(small[:, 0:QT], bank(0)[:, 0:QT], ACT.Identity, bias=eps[:, :], scale=1.0 / D)
                nc.scalar.activation(small[0:NS, QT:QT + 1], bank(0)[0:NS, QT:QT + 1], ACT.Identity, bias=eps[0:NS, :],
                                     scale=1.0 / D).then_inc(self.std, 1)
                if self.split:
                    for k in range(KC):
                        act.wait_ge(self.xn, k + 1)
                        nc.scalar.activation(xh[:, k], TN[:, 1 + k % 2], ACT.Copy).then_inc(self.hi, 1)

            def dve(self, dve):
                dve.wait_ge(self.rec, 1)
                nc.vector.tensor_tensor(TN[:, 0, 0:SEQ].rearrange("p (t c) -> p t c", c=P),
                                        c_("ident").unsqueeze(1).to_broadcast([P, QT, P]),
                                        small[:, 10:10 + QT].unsqueeze(2).to_broadcast([P, QT, P]), ALU.mult)
                nc.vector.tensor_scalar(diag_s[:, :], c_("ident", NS)[:, 0:NS], small[0:NS, 10 + QT:11 + QT], None,
                                        ALU.mult).then_inc(self.diag, 1)
                dve.wait_ge(self.bcast, 1)
                for k in range(KC + 1):
                    if k < KC:
                        if k >= 2:
                            self.wait_row(dve, k)
                        nc.vector.scalar_tensor_tensor(TN[:, 1 + k % 2], self.src(k), self.gain[:, k:k + 1], self.factors,
                                                       ALU.mult, ALU.mult).then_inc(self.xn, 1)
                    if self.split and k:
                        dve.wait_ge(self.hi, k)
                        nc.vector.tensor_tensor(xl[:, k - 1], TN[:, 1 + (k - 1) % 2], xh[:, k - 1].bitcast(f32),
                                                ALU.subtract).then_inc(self.lo, 1)

            def pool(self, pool):
                pool.wait_ge(self.std, 1)
                nc.gpsimd.tensor_tensor(small[:, 10:10 + QT], small[:, 0:QT], neghalf[:, 0:QT], ALU.pow)
                nc.gpsimd.tensor_tensor(small[0:NS, 10 + QT:11 + QT], small[0:NS, QT:QT + 1], neghalf[0:NS, 0:1],
                                        ALU.pow).then_inc(self.rec, 1)

            def wait_row(self, dve, k):
                if self.split:
                    dve.wait_ge(self.lo, k - 1)

            def pe(self, pe):
                pe.wait_ge(self.sum, KC - 1)
                for t in range(QT + 1):
                    w = P if t < QT else NS
                    last = nc.tensor.matmul(bank(0)[0:w, t:t + 1], TN[:, 0, t * P:t * P + w], ones[:, 0:1],
                                            start=True, stop=True)
                last.then_inc(self.stat, 1)
                pe.wait_ge(self.diag, 1)
                for t in range(QT + 1):
                    w = P if t < QT else NS
                    rhs = TN[:, 0, t * P:(t + 1) * P] if t < QT else diag_s[:, :]
                    last = nc.tensor.matmul(self.factors[:, t * P:t * P + w], ones[0:w, :], rhs, start=True, stop=True)
                last.then_inc(self.bcast, 1)

        diag_s = sb("diag_s", [NS, NS])
        eps = sb("eps", [P, 1])
        neghalf = sb("neghalf", [P, QT])

        norm_mix = Norm("norm_mix", lambda k: Z[:, k], "g_mix")

        def block_product(slot, pe=None, ready=None):
            order = [(k, c) for k in range(KC) for c in range(3)] if ready else [(k, c) for c in range(3) for k in range(KC)]
            for k, c in order:
                if ready and c == 0:
                    pe.wait_ge(ready, k + 1)
                last = three_pass(ps[slot][:, c, 0:TC], lambda w: w[:, slot, k], lambda x: x[:, k, c * TC:(c + 1) * TC],
                                  k == 0, k == KC - 1)
            return last

        def project_pe(pe, n, slot):
            pe.wait_ge(w_lo, n + 1)
            pe.wait_ge(evac, n - 1)
            block_product(slot).then_inc(w_used, 1)

        def pe_stage(pe, first_block, ready, banks_read):
            for m in range(2):
                pe.wait_ge(w_lo, first_block + m + 1)
                block_product(m, pe, None if m else ready).then_inc(w_used, 1)
            with pe.Fori(1, KC // 2) as j:
                for slot in range(2):
                    pe.wait_ge(w_lo, first_block + 2 * j + slot + 1)
                    pe.wait_ge(banks_read, 2 * j + slot - 1)
                    block_product(slot).then_inc(w_used, 1)

        relu = TN[:, 0:2]
        CM = TN[:, 2, 0:SEQ]
        Pb = Z[:, QI:QI + 4].rearrange("p (a b) t -> p a b t", a=2)
        PT = Z[:, CV:CV + 2]
        scratch = TN[:, :, :].rearrange("p a t -> p (a t)")
        junk = [scratch[:, 0:528].bitcast(u16), scratch[:, 528:784].bitcast(u16)]
        act_junk = scratch[:, 784:1296].bitcast(bf16)
        ones16 = scratch[:, 528:1056].bitcast(u16)
        ot, osq, yt = (scratch[:, 1344 + a * 256:1600 + a * 256] for a in range(3))
        samples = lambda a: a[:, SEQ:NT].rearrange("p (b t) -> p b t", t=DT)
        v_tr, v_cp = sem("v_transposed"), sem("v_copied")
        masks_set = sem("masks_set")
        idx_mm, idx_relu, idx_acc = sem("idx_product"), sem("idx_relu"), sem("idx_sum")
        d_mixed, maps_mm, maps_cp = sem("pool_input"), sem("pool_mapped"), sem("pool_copied")
        lam_sum, lam_exp = sem("lambda_sums"), sem("lambda_exps")
        IDX = [(i, h) for i in TILES for h in range(IDXH)]

        def causal(i):
            return CM[:, SEQ - (i + 1) * P:SEQ]

        def scores(j):
            if j < len(TILES):
                i = TILES[j]
                return SC_AT[i], (i + 1) * P, P
            return SC_S, NK, NS

        ITEMS = []
        for i in range(QT):
            ITEMS += [("diff", i, h) for h in range(4)] + [("sdiff", i, 0)]
        pairs = iter(range(DB // 2))
        for i in [*range(1, QT), 0]:
            ITEMS += [("dsa", i, h) for h in range(4)] + ([("sdsa", next(pairs), 0)] if i in (3, 5, 6, 7) else [])
        NI = len(ITEMS)
        PROMPT = ("diff", "dsa")
        FIRST_DSA = ITEMS.index(("dsa", 1, 0))

        def maps_of(n):
            return 1 if ITEMS[n][0] == "dsa" else 2

        def unit(n, m=0):
            return sum(maps_of(a) for a in range(n)) + m

        def tile_no(n):
            return sum(ITEMS[a][0] in PROMPT for a in range(n)) // 4

        def sample_no(n):
            return sum(ITEMS[a][0] not in PROMPT for a in range(n))

        def ends_tile(n):
            return ITEMS[n][0] in PROMPT and ITEMS[n][2] == 3

        qk_mm = sem("logits_product")
        row_max = sem("logits_masked")
        neg_max = sem("negated_maxima")
        exp_done = sem("exponentials")
        combined = sem("maps_combined")
        p_tr = sem("probs_transposed")
        p_cp = sem("probs_copied")
        pv_mm = sem("values_product")
        so_cp = sem("sample_output")
        ss_ready = sem("head_squares")
        head_rstd = sem("head_rstd")
        yt_ready = sem("tile_output")
        o_tr = sem("tile_transposed")
        o_cp = sem("tile_stored")


        def logits(n, m=0):
            return Pb[:, n % 2, m if n < FIRST_DSA else n // 2 % 2]

        def probs(n):
            return comb[:, n % 2] if n < FIRST_DSA else logits(n)

        def flat(pair, rows=slice(0, P)):
            return ps[pair // 2][rows, 2 * (pair % 2):2 * (pair % 2) + 2].rearrange("p a b -> p (a b)")

        def pe_values(pe):
            for t in range(QT + 1):
                w = P if t < QT else NS
                if t >= 2:
                    pe.wait_ge(v_cp, t - 1)
                for j in range(3):
                    last = nc.tensor.transpose(bank(6 + t % 2)[0:w, j * P:(j + 1) * P], Z[:, CV + j, t * P:t * P + w], c_("ident"))
                last.then_inc(v_tr, 1)

        PER_SAMPLE = 5

        LAST_SAMPLE = DB * PER_SAMPLE - 1

        def pe_idx(pe):
            for u, (i, h) in enumerate(IDX):
                if u >= 2:
                    pe.wait_ge(idx_relu, u - 1)
                if h == 0:
                    pe.wait_ge(q_lo, TILES.index(i) + 1)
                if u == 0:
                    pe.wait_ge(keys_lo, 1)
                S = (i + 1) * P
                for a in range(0, S, 512):
                    w = min(512, S - a)
                    for t, q in enumerate((wh, wl)):
                        last = nc.tensor.matmul(flat(u % 2)[:, a:a + w], q[:, i % 2, h], kstack[:, a:a + w], start=t == 0, stop=t == 1)
                last.then_inc(idx_mm, 1)
                if u % PER_SAMPLE == PER_SAMPLE - 1 and u // PER_SAMPLE < DB:
                    pe_sidx(pe, u // PER_SAMPLE)
                if u == LAST_SAMPLE + 2:
                    pe_sscore(pe)

        def pe_maps(pe):
            for c in range(2):
                pe.wait_ge(d_mixed, c + 1)
                for a in range(3):
                    last = nc.tensor.matmul(bank(3 * c + a)[:, 0:TC], p_("maps")[:, c * P:(c + 1) * P],
                                            Z[:, PV + c, a * TC:(a + 1) * TC], start=True, stop=True)
                last.then_inc(maps_mm, 1)

        def pe_logits(pe, n):
            kind, i, h = ITEMS[n]
            for m in range(maps_of(n)):
                u = unit(n, m)
                if u >= 2:
                    pe.wait_ge(row_max, u - 1)
                out = flat(u % 2)
                if kind in PROMPT:
                    S = (i + 1) * P
                    if kind == "diff":
                        r = HD * (h % 2) + 32 * m
                        part, q, k = slice(r, r + 32), DQ + h // 2, DK + h // 2
                    elif h == 0:
                        pe.wait_ge(dq_lo, DSA_TILES.index(n) + 1)
                        pe.wait_ge(keys_lo, 2)
                    for a in range(0, S, 512):
                        w = min(512, S - a)
                        if kind == "dsa":
                            for t in range(2):
                                last = nc.tensor.matmul(out[:, a:a + w], dq_stack[:, (tile_no(n) - QT) % 2, t, h], kstack[:, a:a + w],
                                                        start=t == 0, stop=t == 1)
                            continue
                        last = nc.tensor.matmul(out[:, a:a + w], Z[part, q, i * P:(i + 1) * P], Z[part, k, a:a + w],
                                                start=True, stop=True)
                elif kind == "sdiff":
                    if m == 0:
                        pe.wait_ge(d_in, 16 * NPG * (i + 1))
                    for half in range(1 if m else 2):
                        for c in range(2):
                            keys = dk_new[:, c] if m else diff_pages(half)[:, :, c * P:(c + 1) * P]
                            w = NS if m else 512
                            last = nc.tensor.matmul(out[0:32, half * 512:half * 512 + w], qdz[:, c, i], keys, start=c == 0, stop=c == 1)
                else:
                    if m == 0:
                        pe.wait_ge(c_in[i % 2], 16 * 2 * NPG * (i // 2 + 1))
                    for half in range(1 if m else 2):
                        w = NS if m else 512
                        at = PAST * m + 512 * half
                        dst = out[0:32, half * 512:half * 512 + w]
                        for b in range(2):
                            keys = ka_new[0:HD, :] if m else dsa_pages(i, b)[0:HD, 4 * half:4 * half + 4, 0:P]
                            nc.tensor.matmul(dst, qcz[:, 2 * i + b], keys, start=b == 0, stop=False)
                        last = nc.tensor.matmul(dst, c_("rep", NS)[:, 32 * i:32 * i + 32], SC[0:NS, SC_S + at:SC_S + at + w],
                                                start=False, stop=True)
                last.then_inc(qk_mm, 1)

        def pe_outputs(pe, n):
            kind, i, h = ITEMS[n]
            pe.wait_ge(p_cp, n + 1)
            pt = PT[:, n % 2]
            if kind in PROMPT:
                if h == 0 and tile_no(n) >= 2:
                    pe.wait_ge(o_cp, tile_no(n) - 1)
                v = P + HD * h if kind == "diff" else 0
                for b in range(i + 1):
                    last = nc.tensor.matmul(bank(6 + tile_no(n) % 2)[:, h * HD:(h + 1) * HD], pt[:, b * P:(b + 1) * P],
                                            vtok[:, b, v:v + HD], start=b == 0, stop=b == i)
            else:
                if (kind, i) == ("sdsa", 0):
                    pe.wait_ge(dmean, 1)
                for c in range(2):
                    for g in range(NPG + 1):
                        rows = P if g < NPG else NS
                        if kind == "sdiff":
                            v = diff_pages(g // 4)[:, g % 4, 256 + c * P:256 + (c + 1) * P] if g < NPG else vtok[0:NS, QT, P + c * P:P + (c + 1) * P]
                            out, p = bank(5)[:, c * 32:c * 32 + 32], pt[0:rows, g * 32:g * 32 + 32]
                        else:
                            v = dsa_pages(i, c)[:, g, P:P + HD] if g < NPG else vtok[0:NS, QT, 0:HD]
                            out, p = bank(5)[0:HD, c * 16:c * 16 + 16], pt[0:rows, g * 32 + c * 16:g * 32 + c * 16 + 16]
                        last = nc.tensor.matmul(out, v, p, start=g == 0, stop=g == NPG)
            last.then_inc(pv_mm, 1)

        def pe_transposes(pe, n):
            kind, i, h = ITEMS[n]
            pe.wait_ge(combined, n + 1)
            if n >= 1:
                pe.wait_ge(p_cp, n)
            if n >= 1 and ITEMS[n - 1][0] not in PROMPT:
                pe.wait_ge(so_cp, sample_no(n))
            if kind in PROMPT:
                for b in range(i + 1):
                    last = nc.tensor.transpose(bank(4 + b // 4)[:, (b % 4) * P:(b % 4 + 1) * P],
                                               probs(n)[:, b * P:(b + 1) * P], c_("ident"))
            else:
                for g in range(NPG + 1):
                    w = P if g < NPG else NS
                    last = nc.tensor.transpose(bank(4)[0:w, g * 32:g * 32 + 32], probs(n)[0:32, g * P:g * P + w], c_("ident", 32)[:, 0:32])
            last.then_inc(p_tr, 1)

        def pe_item(pe, n):
            if n < NI:
                pe_logits(pe, n)
            if 0 <= n - 3 < NI:
                pe_outputs(pe, n - 3)
            if 0 <= n - 2 < NI:
                pe_transposes(pe, n - 2)
            if 0 <= n - 5 < NI and ends_tile(n - 5):
                tile = tile_no(n - 5)
                pe.wait_ge(yt_ready, tile + 1)
                for j in range(2):
                    last = nc.tensor.transpose(bank(6 + tile % 2)[:, 256 + j * P:256 + (j + 1) * P], yt[:, j * P:(j + 1) * P], c_("ident"))
                last.then_inc(o_tr, 1)

        def act_values(act):
            for t in range(QT + 1):
                w = P if t < QT else NS
                act.wait_ge(v_tr, t + 1)
                nc.scalar.activation(vtok[0:w, t], bank(6 + t % 2)[0:w, 0:384], ACT.Copy).then_inc(v_cp, 1)

        keys_twice = sem("keys_twice")
        keys_hi, keys_lo = sem("keys_hi"), sem("keys_lo")
        q_hi, q_lo = sem("idx_queries_hi"), sem("idx_queries_lo")
        dq_hi, dq_lo = sem("dsa_queries_hi"), sem("dsa_queries_lo")

        def act_keys(act, rows):
            nc.scalar.activation(kstack[0:HD, 0:SEQ], Z[rows, KA, 0:SEQ], ACT.Copy)
            nc.scalar.activation(kstack[HD:P, 0:SEQ], Z[HD:P, KA, 0:SEQ], ACT.Copy).then_inc(keys_hi, 1)

        def dve_keys(dve, no):
            dve.wait_ge(keys_hi, no)
            nc.vector.tensor_tensor(kstack[HD:P, 0:SEQ], Z[HD:P, KA, 0:SEQ], kstack[HD:P, 0:SEQ].bitcast(f32),
                                    ALU.subtract).then_inc(keys_lo, 1)

        def act_queries(src, dst, i, done):
            for par in range(2):
                for half in range(2):
                    last = nc.scalar.activation(dst[HD * half:HD * half + HD, par::2], Z[HD * par:HD * par + HD, src, i * P:(i + 1) * P],
                                                ACT.Copy)
            last.then_inc(done, 1)

        def dve_queries(chain, src, hi, lo, i, done):
            for par in range(2):
                r = slice(HD * par, HD * par + HD)
                rest = chain.mark(nc.vector.tensor_tensor(lo[r, par::2], Z[r, src, i * P:(i + 1) * P], hi[r, par::2].bitcast(f32), ALU.subtract))
            for par in range(2):
                r, other = slice(HD * par, HD * par + HD), slice(HD * (1 - par), HD * (1 - par) + HD)
                chain.until(rest - 1 + par)
                last = nc.vector.tensor_copy(lo[other, par::2], lo[r, par::2].bitcast(f32))
                if par == 0:
                    chain.mark(last)
            last.then_inc(done, 1)

        def act_idx_queries(act, t):
            if t >= 2:
                act.wait_ge(idx_mm, IDXH * (t - 1))
            i = TILES[t]
            act_queries(slice(QI, QI + 4), wh[:, i % 2], i, q_hi)

        def dve_idx_queries(dve, chain, t):
            dve.wait_ge(q_hi, t + 1)
            i = TILES[t]
            dve_queries(chain, slice(QI, QI + 4), wh[:, i % 2], wl[:, i % 2], i, q_lo)

        DSA_TILES = [a for a, (kind, i, h) in enumerate(ITEMS) if kind == "dsa" and h == 0]
        PREPARE = {a - 2 if a > FIRST_DSA else a - 1: k for k, a in enumerate(DSA_TILES)}

        def act_dsa_queries(act, k):
            first = DSA_TILES[k]
            if k == 0:
                act.wait_ge(qk_mm, unit(FIRST_DSA - 1))
            if k >= 2:
                act.wait_ge(qk_mm, unit(DSA_TILES[k - 1]))
            act_queries(slice(CQ, CQ + 2), dq_stack[:, k % 2, 0], ITEMS[first][1], dq_hi)

        def dve_dsa_queries(dve, chain, k):
            dve.wait_ge(dq_hi, k + 1)
            dve_queries(chain, slice(CQ, CQ + 2), dq_stack[:, k % 2, 0], dq_stack[:, k % 2, 1], ITEMS[DSA_TILES[k]][1], dq_lo)

        KEYS_STEP = FIRST_DSA - 4

        def act_idx(act):
            for u, (i, h) in enumerate(IDX):
                S = (i + 1) * P
                if h == 4 and i + 1 in TILES and i > TILES[0]:
                    act_idx_queries(act, TILES.index(i + 1))
                act.wait_ge(idx_mm, u + 1)
                if u >= 2:
                    act.wait_ge(idx_acc, u - 1)
                nc.scalar.activation(relu[:, u % 2, 0:S], flat(u % 2)[:, 0:S], ACT.Relu, scale=IDX_SCALE).then_inc(idx_relu, 1)
                if u % (4 * PER_SAMPLE) == 4 * PER_SAMPLE - 1 and u <= LAST_SAMPLE:
                    act_sidx(act, u // (4 * PER_SAMPLE))

        def act_lambda(act):
            act.wait_ge(lam_sum, 1)
            nc.scalar.activation(lamw[:, 2:4], lamw[:, 0:2], ACT.Exp).then_inc(lam_exp, 1)

        def act_maps(act):
            for c in range(2):
                act.wait_ge(maps_mm, c + 1)
                for a in range(3):
                    last = nc.scalar.activation(Z[:, GC + c, a * TC:(a + 1) * TC], bank(3 * c + a)[:, 0:TC], ACT.Copy,
                                                scale=p_("pool_scale")[:, c:c + 1])
                last.then_inc(maps_cp, 1)

        SCALE = {"diff": DIFF_SCALE, "sdiff": DIFF_SCALE, "dsa": DSA_SCALE, "sdsa": DSA_SCALE}

        def act_item(act, n):
            if n < NI:
                kind, i, h = ITEMS[n]
                act.wait_ge(neg_max, n + 1)
                prompt = kind in PROMPT
                rows, S = (P, (i + 1) * P) if prompt else (32, NK)
                for m in range(maps_of(n) if prompt else 1):
                    col = 2 * (n % 2) + m
                    p = logits(n, m)[0:rows, 0:S]
                    last = nc.scalar.activation(p, p, ACT.Exp, bias=nm[0:rows, col:col + 1], scale=SCALE[kind], accum_out=sm[0:rows, col:col + 1])
                last.then_inc(exp_done, 1)
            if 0 <= n - 3 < NI and ITEMS[n - 3][0] not in PROMPT:
                kind, i, h = ITEMS[n - 3]
                act.wait_ge(pv_mm, n - 2)
                if kind == "sdiff":
                    last = nc.scalar.activation(so[:, i], bank(5)[:, 0:64], ACT.Copy)
                else:
                    o = bank(5)[0:HD, 0:32].rearrange("p (b h t) -> p h b t", b=2, h=4)
                    for h in range(4):
                        half = slice(HD * (h % 2), HD * (h % 2) + HD)
                        last = nc.scalar.activation(samples(Z[half, GH + h // 2])[:, 2 * i:2 * i + 2], o[:, h], ACT.Copy)
                last.then_inc(so_cp, 1)
            if 0 <= n - 2 < NI:
                kind, i, h = ITEMS[n - 2]
                act.wait_ge(p_tr, n - 1)
                if n - 2 >= 2:
                    act.wait_ge(pv_mm, n - 3)
                pt = PT[:, n % 2]
                if kind in PROMPT:
                    for b in range(0, i + 1, 4):
                        w = min(4, i + 1 - b) * P
                        last = nc.scalar.activation(pt[:, b * P:b * P + w], bank(4 + b // 4)[:, 0:w], ACT.Copy)
                else:
                    nc.scalar.activation(pt[:, 0:NPG * 32], bank(4)[:, 0:NPG * 32], ACT.Copy)
                    last = nc.scalar.activation(pt[0:NS, NPG * 32:NPG * 32 + 32], bank(4)[0:NS, NPG * 32:NPG * 32 + 32], ACT.Copy)
                last.then_inc(p_cp, 1)
            if bit_of(n):
                act_counts(act, n)
            if 0 <= n - 5 < NI and ends_tile(n - 5):
                kind, i, h = ITEMS[n - 5]
                tile = tile_no(n - 5)
                act.wait_ge(o_tr, tile + 1)
                for j in range(2):
                    src = bank(6 + tile % 2)[:, 256 + j * P:256 + (j + 1) * P]
                    dst = Z[:, (PV if kind == "diff" else GH) + j, i * P:(i + 1) * P]
                    last = nc.scalar.activation(dst, src, ACT.Copy, scale=subln[:, :] if kind == "diff" else 1.0)
                last.then_inc(o_cp, 1)

        subln = sb("subln", [P, 1])

        def dve_idx(dve, chain):
            link = chain.link
            for u, (i, h) in enumerate(IDX):
                at, S = SC_AT[i], (i + 1) * P
                dve.wait_ge(idx_relu, u + 1)
                if u:
                    dve.wait_ge(idx_acc, u)
                before = causal(i) if h == 0 else SC[:, at:at + S]
                nc.vector.scalar_tensor_tensor(SC[:, at:at + S], relu[:, u % 2, 0:S], vtok[:, i, HD + h:HD + h + 1], before,
                                               ALU.mult, ALU.add).then_inc(idx_acc, 1)
                if u == LAST_SAMPLE + 4:
                    dve_sscore(dve)
                if h == 4 and i + 1 in TILES and i > TILES[0]:
                    dve_idx_queries(dve, chain, TILES.index(i + 1))
                if i > TILES[0] and h % 2:
                    if h == 1:
                        dve.wait_ge(idx_acc, u - h)
                    top_sign(dve, link, TILES.index(i) - 1, h // 2)

        def dve_conv(dve, link, c):
            n = 2 + SEQ + DB * 6
            U, T = scratch[:, 0:n], scratch[:, n:2 * n]
            Us, Ts = (a[:, 2 + SEQ:n].rearrange("p (b t) -> p b t", t=6) for a in (U, T))
            st = p_("st_conv").rearrange("p (c b t) -> p c b t", c=2, t=2)[:, c]
            w = p_("conv_a")[:, 3 * c:3 * c + 3]
            tok = lambda slot: Z[:, slot, SEQ:NT].rearrange("p (b t) -> p b t", t=DT)
            nc.vector.memset(U[:, 0:2], 0.0)
            nc.vector.tensor_copy(Us[:, :, 0:2], st)
            nc.vector.tensor_tensor(U[:, 2:2 + SEQ], Z[:, GC + c, 0:SEQ], Z[:, GH + c, 0:SEQ], ALU.mult)
            link(nc.vector.tensor_tensor(Us[:, :, 2:6], tok(GC + c), tok(GH + c), ALU.mult))
            link(nc.vector.tensor_scalar(T[:, 0:n - 2], U[:, 0:n - 2], w[:, 0:1], None, ALU.mult))
            link(nc.vector.scalar_tensor_tensor(T[:, 0:n - 2], U[:, 1:n - 1], w[:, 1:2], T[:, 0:n - 2], ALU.mult, ALU.add))
            link(nc.vector.scalar_tensor_tensor(T[:, 0:n - 2], U[:, 2:n], w[:, 2:3], T[:, 0:n - 2], ALU.mult, ALU.add))
            nc.vector.tensor_tensor(Z[:, GB + c, 0:SEQ], Z[:, GB + c, 0:SEQ], T[:, 0:SEQ], ALU.mult)
            nc.vector.tensor_tensor(tok(GB + c), tok(GB + c), Ts[:, :, 0:DT], ALU.mult)
            nc.vector.tensor_copy(ST[:, c, 0, 0:2], U[:, SEQ:SEQ + 2])
            link(nc.vector.tensor_copy(ST[:, c, 1:1 + DB, 0:2], Us[:, :, 4:6]))

        def dve_pool(dve, link, c):
            n = 15 + SEQ + DB * 19
            E, A = scratch[:, 0:n], scratch[:, n:2 * n]
            s_of = lambda x: x[:, 15 + SEQ:n].rearrange("p (b t) -> p b t", t=19)
            tok = samples(Z[:, PV + c])
            nc.vector.memset(E[:, 0:15], 0.0)
            nc.vector.tensor_copy(s_of(E)[:, :, 0:15], p_("st_pool").rearrange("p (c b t) -> p c b t", c=2, t=15)[:, c])
            nc.vector.tensor_copy(E[:, 15:15 + SEQ], Z[:, PV + c, 0:SEQ])
            link(nc.vector.tensor_copy(s_of(E)[:, :, 15:19], tok))
            nc.vector.tensor_copy(ST[:, c, 0, 2:17], E[:, SEQ:SEQ + 15])
            link(nc.vector.tensor_copy(ST[:, c, 1:1 + DB, 2:17], s_of(E)[:, :, 4:19]))

            def double(dst, src, step):
                link(nc.vector.tensor_tensor(dst[:, 0:n - 2 * step + 1], src[:, 0:n - 2 * step + 1],
                                             src[:, step:n - step + 1], ALU.add))

            def finish(half, sums, win):
                r = slice(HD * half, HD * half + HD)
                inv = c_("inv_w")[r, c:c + 1]
                off = 16 - win
                table = c_("inv_cnt")[r, 16 * c:16 * c + 16]
                link(nc.vector.tensor_tensor(small[r, 0:16], sums[r, off:off + 16], table, ALU.mult))
                link(nc.vector.tensor_tensor(small[r, 0:16], small[r, 0:16], Z[r, PV + c, 0:16], ALU.subtract))
                link(nc.vector.scalar_tensor_tensor(Z[r, PV + c, 0:SEQ], sums[r, off:off + SEQ], inv, Z[r, PV + c, 0:SEQ], ALU.mult, ALU.subtract))
                link(nc.vector.scalar_tensor_tensor(tok[r], s_of(sums)[r, :, off:off + DT], inv, tok[r], ALU.mult, ALU.subtract))
                return nc.vector.tensor_copy(Z[r, PV + c, 0:16], small[r, 0:16])

            double(A, E, 1)
            double(E, A, 2)
            if c == 0:
                link(finish(0, A, 2))
                last = finish(1, E, 4)
            else:
                double(A, E, 4)
                double(E, A, 8)
                link(finish(0, A, 8))
                last = finish(1, E, 16)
            last.then_inc(d_mixed, 1)
            dve.wait_ge(d_mixed, c + 1)

        def dve_lambda(dve, link):
            lp = p_("lam")
            link(nc.vector.tensor_tensor_reduce(out=small[:, 0:32], in0=lp[:, 0:32], in1=lp[:, 32:64], scale=1.0, scalar=0.0,
                                                op0=ALU.mult, op1=ALU.add, accum_out=lamw[:, 0:1]))
            nc.vector.tensor_tensor_reduce(out=small[:, 0:32], in0=lp[:, 64:96], in1=lp[:, 96:128], scale=1.0, scalar=0.0,
                                           op0=ALU.mult, op1=ALU.add, accum_out=lamw[:, 1:2]).then_inc(lam_sum, 1)
            dve.wait_ge(lam_exp, 1)
            link(nc.vector.tensor_tensor(small[:, 32:33], lamw[:, 3:4], lamw[:, 2:3], ALU.subtract))
            link(nc.vector.tensor_scalar(small[:, 32:33], small[:, 32:33], -LAM_INIT, None, ALU.add))
            nc.vector.tensor_scalar(subln[:, :], p_("subln"), 1.0 - LAM_INIT, None, ALU.mult)
            link(nc.vector.scalar_tensor_tensor(small[:, 33:34], c_("lam_b"), small[:, 32:33], c_("lam_a"), ALU.mult, ALU.add))

        CNT, POS, SGN, KK, THI, CAND, GE, TLO, NEED, TMAG, THR, RANK, NBIAS = range(13)

        def col(a, j=None, rows=P):
            return tk[0:rows, a] if j is None else tk[0:rows, a, j:j + 1]

        def count(j, src, scalar, op, out):
            at, S, rows = scores(j)
            scalar = scalar if type(scalar) is float else col(scalar, j, rows)
            return nc.vector.tensor_scalar(out, src[0:rows, at:at + S], scalar, 0.0, op, ALU.add, accum_out=col(CNT, j, rows))

        counted = sem("counted")
        cand_set = sem("candidate_set")
        signed = sem("magnitudes_set")
        act_counted = sem("act_counted")
        counts = [0]

        def top_sign(dve, link, j, part):
            at, S, rows = scores(j)
            y = pages[:, 0:S]
            k = lambda a: col(a, j, rows)
            if part == 0:
                link(count(j, SC, 0.0, ALU.is_ge, pages[0:rows, 1056:1056 + (S + 1) // 2].bitcast(u16)[:, 0:S]))
                link(nc.vector.tensor_scalar(k(POS), k(CNT), float(TOPK), None, ALU.is_ge))
            elif part == 1:
                nc.vector.tensor_scalar(k(SGN), k(POS), 2.0, -1.0, ALU.mult, ALU.add)
                link(nc.vector.tensor_tensor(k(KK), k(POS), c_("kdiff")[0:rows, j:j + 1], ALU.mult))
                link(nc.vector.tensor_tensor(k(KK), k(KK), c_("kneg")[0:rows, j:j + 1], ALU.add))
            elif part == 2:
                link(nc.vector.tensor_scalar(y[0:rows, 0:S], SC[0:rows, at:at + S], k(SGN), 0.0, ALU.mult, ALU.max))
                w, seen = (P, CP) if rows == P else (NS, newcp)
                link(nc.vector.tensor_tensor(y[0:rows, S - w:S], y[0:rows, S - w:S], seen[0:rows, :], ALU.min))
            else:
                halves = y.bitcast(u16)
                nc.vector.tensor_copy(y_hi[0:rows, at:at + S], halves[0:rows, 1:2 * S:2])
                nc.vector.tensor_copy(y_lo[0:rows, at:at + S], halves[0:rows, 0:2 * S:2]).then_inc(signed, 1)

        SIGNS = {0: NTOP - 2, 1: NTOP - 1}
        HI_BITS = range(2, 17)
        TIES = {17: range(0, 3), 18: range(3, 5), 19: range(5, NTOP)}
        LO_BITS = range(20, 36)
        MASKS = {36: NTOP - 1} | {37 + j: j for j in range(NTOP - 1)}

        def bit_of(n):
            if n in HI_BITS:
                return y_hi, THI, HI_BITS[-1] - n
            if n in LO_BITS:
                return y_lo, TLO, LO_BITS[-1] - n
            return None

        def bits_before(n):
            return sum(a in HI_BITS or a in LO_BITS for a in range(n))

        def ranks(dve, link):
            link(nc.vector.tensor_tensor(col(RANK), col(KK), c_("kmul"), ALU.mult))
            link(nc.vector.tensor_tensor(col(RANK), col(RANK), c_("kadd"), ALU.add))

        def top_compare(dve, n):
            dve.wait_ge(counted, counts[0])
            dve.wait_ge(act_counted, len(ACT_TOP) * (bits_before(n) + 1))
            return nc.vector.tensor_tensor(col(GE), col(CNT), col(RANK), ALU.is_ge)

        def top_take(dve, n):
            src, T, b = bit_of(n)
            return nc.vector.scalar_tensor_tensor(col(T), col(GE), float(2 ** b), col(T), ALU.mult, ALU.add)

        def top_candidate(dve, n):
            src, T, b = bit_of(n)
            return nc.vector.tensor_scalar(col(CAND), col(T), float(2 ** b), None, ALU.add)

        def top_bias(dve):
            nc.vector.tensor_scalar(col(NBIAS), col(CAND), -1.0, 0.5, ALU.mult, ALU.add).then_inc(cand_set, 1)

        def top_counts(dve, n):
            src, T, b = bit_of(n)
            for t, j in enumerate(DVE_TOP):
                at, S, rows = scores(j)
                if t >= 2:
                    dve.wait_ge(counted, counts[0] - 1)
                count(j, src, CAND, ALU.is_ge, junk[t % 2][0:rows, 0:S]).then_inc(counted, 1)
                counts[0] += 1

        def act_counts(act, n):
            src, T, b = bit_of(n)
            act.wait_ge(cand_set, bits_before(n) + 1)
            for t, j in enumerate(ACT_TOP):
                at, S, rows = scores(j)
                before = bits_before(n) * len(ACT_TOP) + t
                if before:
                    act.wait_ge(act_counted, before)
                nc.scalar.activation(act_junk[:, 0:S], src[:, at:at + S], ACT.Sign, bias=col(NBIAS, j),
                                     accum_out=col(CNT, j)).then_inc(act_counted, 1)

        def top_ties(dve, link, n):
            for j in TIES[n]:
                at, S, rows = scores(j)
                link(count(j, y_hi, THI, ALU.is_gt, junk[0][0:rows, 0:S]))
                last = nc.vector.scalar_tensor_tensor(y_lo[0:rows, at:at + S], y_hi[0:rows, at:at + S], col(THI, j, rows),
                                                      y_lo[0:rows, at:at + S], ALU.is_equal, ALU.mult)
            link(last)
            if n == max(TIES):
                link(nc.vector.tensor_tensor(col(KK), col(KK), col(CNT), ALU.subtract))
                ranks(dve, link)

        def top_thresholds(dve, link):
            nc.vector.memset(ones16, 1.0)
            bits = col(TMAG).bitcast(u16)
            nc.vector.tensor_copy(bits[:, 1:2 * NTOP:2], col(THI))
            link(nc.vector.tensor_copy(bits[:, 0:2 * NTOP:2], col(TLO)))
            link(nc.vector.tensor_tensor(col(THR), col(TMAG), col(SGN), ALU.mult))

        def top_mask(dve, link, j):
            at, S, rows = scores(j)
            cols = (slice(0, rows), slice(at, at + S))
            count(j, SC, THR, ALU.is_gt, out=y_hi[cols])
            link(nc.vector.tensor_scalar(y_lo[cols], SC[cols], col(THR, j, rows), None, ALU.is_equal))
            nc.vector.tensor_scalar(col(NEED, j, rows), col(CNT, j, rows), -1.0, float(TOPK), ALU.mult, ALU.add)
            link(nc.vector.tensor_tensor_scan(junk[0][0:rows, 0:S], ones16[0:rows, 0:S], y_lo[cols], 0.0, ALU.mult, ALU.add))
            link(nc.vector.scalar_tensor_tensor(y_lo[cols], junk[0][0:rows, 0:S], col(NEED, j, rows), y_lo[cols], ALU.is_le, ALU.mult))
            link(nc.vector.scalar_tensor_tensor(SC[cols], y_hi[cols], -1.0, y_lo[cols], ALU.add, ALU.add))
            link(nc.vector.tensor_scalar(SC[cols], SC[cols], BIG, None, ALU.mult))

        def top_step(dve, link, n):
            if n in SIGNS:
                for part in range(4):
                    top_sign(dve, link, SIGNS[n], part)
                if n == max(SIGNS):
                    dve.wait_ge(signed, NTOP)
                    ranks(dve, link)
            elif n in TIES:
                top_ties(dve, link, n)
            elif n in MASKS:
                if n == min(MASKS):
                    top_thresholds(dve, link)
                top_mask(dve, link, MASKS[n])

        def dve_maxima(dve, link, n):
            kind, i, h = ITEMS[n]
            c = 2 * (n % 2)
            if n >= FIRST_DSA + 4:
                dve.wait_ge(p_tr, n - 3)
            for m in range(maps_of(n)):
                u = unit(n, m)
                dve.wait_ge(qk_mm, u + 1)
                src, top = flat(u % 2), mx[:, c + m:c + m + 1]
                if kind in PROMPT:
                    S = (i + 1) * P
                    mask = causal(i) if kind == "diff" or i not in TILES else SC[:, SC_AT[i]:SC_AT[i] + S]
                    last = nc.vector.tensor_tensor_reduce(out=logits(n, m)[:, 0:S], in0=src[:, 0:S], in1=mask, scale=1.0,
                                                          scalar=-3e38, op0=ALU.add, op1=ALU.max, accum_out=top)
                elif m == 1 and kind == "sdiff":
                    last = nc.vector.tensor_tensor_reduce(out=logits(n)[0:32, PAST:NK], in0=src[0:32, 0:NS],
                                                          in1=c_("dmask", NS)[:, i * NS:(i + 1) * NS], scale=1.0,
                                                          scalar=-3e38, op0=ALU.add, op1=ALU.max, accum_out=top[0:32])
                else:
                    at, w = (PAST, NS) if m else (0, PAST)
                    last = nc.vector.tensor_scalar(logits(n)[0:32, at:at + w], src[0:32, 0:w], 0.0, -3e38, ALU.add, ALU.max,
                                                   accum_out=top[0:32])
                last.then_inc(row_max, 1)
            dve.wait_ge(row_max, unit(n) + maps_of(n))
            k = maps_of(n)
            if kind not in PROMPT:
                link(nc.vector.tensor_tensor(mx[0:32, c:c + 1], mx[0:32, c:c + 1], mx[0:32, c + 1:c + 2], ALU.max))
                k = 1
            rows = P if kind in PROMPT else 32
            nc.vector.tensor_scalar(nm[0:rows, c:c + k], mx[0:rows, c:c + k], -SCALE[kind], None, ALU.mult).then_inc(neg_max, 1)

        def sum_col(n):
            return 4 * (tile_no(n) % 2) + ITEMS[n][2]

        def dve_item(dve, chain, n):
            link = chain.link
            if n < NI:
                dve_maxima(dve, link, n)
            kind, i, h = ITEMS[n - 1] if 0 <= n - 1 < NI else (None, 0, 0)
            S, c = (i + 1) * P, 2 * ((n - 1) % 2)
            if kind:
                dve.wait_ge(exp_done, n)
            if kind == "diff":
                a = sum_col(n - 1)
                nc.vector.reciprocal(rs4[:, a:a + 1], sm[:, c:c + 1])
                inverse = chain.mark(nc.vector.reciprocal(cf[:, c + 1:c + 2], sm[:, c + 1:c + 2]))
            last_bit = bit_of(n - 1)
            if last_bit:
                compared = chain.mark(top_compare(dve, n - 1))
            if kind == "diff":
                chain.until(inverse)
                ratio = chain.mark(nc.vector.scalar_tensor_tensor(cf[:, c + 1:c + 2], cf[:, c + 1:c + 2], sm[:, c:c + 1],
                                                                  small[:, 32:33], ALU.mult, ALU.mult))
            if last_bit:
                chain.until(compared)
                taken_bit = chain.mark(top_take(dve, n - 1))
            if kind == "diff":
                chain.until(ratio)
                if n - 1 >= 2:
                    dve.wait_ge(p_tr, n - 2)
                nc.vector.scalar_tensor_tensor(probs(n - 1)[:, 0:S], logits(n - 1, 1)[:, 0:S], cf[:, c + 1:c + 2],
                                               logits(n - 1, 0)[:, 0:S], ALU.mult, ALU.add).then_inc(combined, 1)
            elif kind == "dsa":
                a = sum_col(n - 1)
                nc.vector.reciprocal(rs4[:, a:a + 1], sm[:, c:c + 1]).then_inc(combined, 1)
            elif kind:
                k = cf[0:32, c:c + 1]
                link(nc.vector.reciprocal(k, sm[0:32, c:c + 1]))
                if kind == "sdiff":
                    link(nc.vector.tensor_tensor(k, k, small[0:32, 33:34], ALU.mult))
                    if n - 1 >= 2:
                        dve.wait_ge(p_tr, n - 2)
                nc.vector.tensor_scalar(probs(n - 1)[0:32, 0:NK], logits(n - 1)[0:32, 0:NK], k, None, ALU.mult).then_inc(combined, 1)
            if last_bit:
                chain.until(taken_bit)
            if bit_of(n):
                link(top_candidate(dve, n))
                top_bias(dve)
                top_counts(dve, n)
            if 0 <= n - 4 < NI and ends_tile(n - 4):
                dve_tile_output(dve, link, n - 4)
            if n in PREPARE:
                dve_dsa_queries(dve, chain, PREPARE[n])
            top_step(dve, link, n)

        def dve_tile_output(dve, link, n):
            kind, i, h = ITEMS[n]
            tile = tile_no(n)
            dve.wait_ge(pv_mm, n + 1)
            if tile >= 1:
                dve.wait_ge(o_tr, tile)
            heads = lambda x: x.rearrange("p (h d) -> p h d", d=HD)
            o = heads(bank(6 + tile % 2)[:, 0:256])
            a = 4 * (tile % 2)
            inverse = rs4[:, a:a + 4].unsqueeze(2).to_broadcast([P, 4, HD])
            if kind == "diff":
                link(nc.vector.tensor_tensor(heads(ot), o, inverse, ALU.mult))
                link(nc.vector.tensor_tensor(osq, ot, ot, ALU.mult))
                link(nc.vector.tensor_reduce(rs4[:, 8:12], heads(osq), AX.X, ALU.add))
                nc.vector.tensor_scalar(rs4[:, 12:16], rs4[:, 8:12], 1.0 / HD, EPS, ALU.mult, ALU.add).then_inc(ss_ready, 1)
                dve.wait_ge(head_rstd, tile + 1)
                nc.vector.tensor_tensor(heads(yt), heads(ot), rs4[:, 16:20].unsqueeze(2).to_broadcast([P, 4, HD]),
                                        ALU.mult).then_inc(yt_ready, 1)
            else:
                nc.vector.tensor_tensor(heads(yt), o, inverse, ALU.mult).then_inc(yt_ready, 1)

        ex = Z[:, DV + 1]
        qcz = ex[0:HD, 0:256].rearrange("p (b r) -> p b r", r=32)
        qdz = ex[:, 256:768].rearrange("p (c b r) -> p c b r", c=2, r=32)
        ka_new, dk_new = ex[:, 768:800], ex[:, 800:864].rearrange("p (c t) -> p c t", c=2)

        def diff_page(g):
            return pages[:, g * 512:g * 512 + 512]

        def diff_pages(half):
            return pages[:, half * 2048:half * 2048 + 2048].rearrange("p (g c) -> p g c", c=512)

        def dsa_pages(j, b):
            at = ((j % 2) * 2 + b) * NPG * 192
            return pages[:, at:at + NPG * 192].rearrange("p (g c) -> p g c", c=192)

        so = Z[:, GH + 1, 512:1024].rearrange("p (b c) -> p b c", b=DB)
        od, osqs, omean, orstd = (Z[:, GH, 512 + 64 * a:576 + 64 * a] for a in range(4))
        srelu = PT
        k_in = [sem("idx_pages0"), sem("idx_pages1")]
        d_in = sem("diff_pages")
        c_in = [sem("dsa_pages0"), sem("dsa_pages1")]
        pt_in = sem("page_table_loaded")
        zeroed, copied, wcol_mm, wsel_set = sem("sample_zeroed"), sem("sample_copied"), sem("wcol_product"), sem("wsel_set")
        sidx_mm, sidx_relu, sscore_mm, sscored = sem("sidx_product"), sem("sidx_relu"), sem("sscore_product"), sem("sample_scored")
        dsq, dsum_mm, dmean, drstd, dy = sem("dhead_squares"), sem("dhead_sums"), sem("dhead_means"), sem("dhead_rstd"), sem("dhead_out")
        COLS = [(0, 512), (512, 512), (1024, NS)]

        def load_page(sp, dst, src_of, no, done):
            page = sp.value_load(ptab[0:1, bass.ds(no, 1)], min_val=0, max_val=d["c_pages"].shape[0] - 1)
            sp.dma_start(dst, src_of(bass.ds(page, 1))).then_inc(done, 16)

        def sp_idx_pages(sp):
            sp.wait_ge(pt_in, 16)
            sp.wait_ge(w_used, NZ)
            for b in range(DB):
                if b >= 2:
                    sp.wait_ge(sidx_mm, b - 1)
                for g in range(NPG):
                    load_page(sp, kring[:, b % 2, g], lambda i: d["c_pages"][i, :, 0:P].rearrange("o p c -> p (o c)"),
                              b * NPG + g, k_in[b % 2])

        def item_no(kind, i):
            return ITEMS.index((kind, i, 0))

        def sp_diff_pages(sp):
            for b in range(DB):
                if b:
                    sp.wait_ge(pv_mm, item_no("sdiff", b - 1) + 1)
                else:
                    sp.wait_ge(idx_mm, len(IDX))
                    sp.wait_ge(signed, NTOP)
                for g in range(NPG):
                    load_page(sp, diff_page(g), lambda i: d["d_pages"][i].rearrange("o p c -> p (o c)"), b * NPG + g, d_in)

        def sp_dsa_pages(sp):
            sp.wait_ge(pv_mm, item_no("sdiff", DB - 1) + 1)
            for j in range(DB // 2):
                if j >= 2:
                    sp.wait_ge(pv_mm, item_no("sdsa", j - 2) + 1)
                for b in range(2):
                    for g in range(NPG):
                        load_page(sp, dsa_pages(j, b)[:, g], lambda i: d["c_pages"][i].rearrange("o p c -> p (o c)"),
                                  (2 * j + b) * NPG + g, c_in[j % 2])

        def act_sample_copies(act):
            act.wait_ge(zeroed, 1)
            act.wait_ge(outs_stored, 16 * 7)
            for h in range(IDXH):
                half = slice(HD * (h % 2), HD * (h % 2) + HD)
                last = nc.scalar.activation(qis[HD:P, :, h], samples(Z[half, QI + h // 2]), ACT.Copy)
            last.then_inc(copied, 1)
            for h in range(4):
                half = slice(HD * (h % 2), HD * (h % 2) + HD)
                for par in range(2):
                    last = nc.scalar.activation(qcz[:, par:DB:2, par * 16 + h * 4:par * 16 + h * 4 + 4],
                                                samples(Z[half, CQ + h // 2])[:, par:DB:2], ACT.Copy)
            last.then_inc(copied, 1)
            for c in range(2):
                for r in range(4):
                    part = slice(32 * r, 32 * r + 32)
                    at = 16 * c + 4 * r
                    last = nc.scalar.activation(qdz[part, c, :, at:at + 4], samples(Z[part, DQ + c]), ACT.Copy)
            last.then_inc(copied, 1)
            nc.scalar.activation(ka_new, Z[:, KA, SEQ:NT], ACT.Copy)
            nc.scalar.activation(dk_new, Z[:, DK:DK + 2, SEQ:NT], ACT.Copy).then_inc(copied, 1)

        def pe_wcol(pe):
            for g in range(2):
                last = nc.tensor.matmul(bank(7)[:, 8 * g:8 * g + 8], c_(f"e{g}", NS), vtok[0:NS, QT, HD:HD + 8], start=True, stop=True)
            last.then_inc(wcol_mm, 1)

        def dve_wsel(dve, link):
            dve.wait_ge(wcol_mm, 1)
            for g in range(2):
                link(nc.vector.tensor_tensor_reduce(out=small[:, 20:28], in0=bank(7)[:, 8 * g:8 * g + 8], in1=c_("hsel"), scale=1.0,
                                                    scalar=0.0, op0=ALU.mult, op1=ALU.add, accum_out=wcol[:, g:g + 1]))
                nc.vector.tensor_scalar(wsel[:, g], c_(f"sel{g}"), wcol[:, g:g + 1], None, ALU.mult).then_inc(wsel_set, 1)

        def pe_sidx(pe, b):
            pe.wait_ge(k_in[b % 2], 16 * NPG * (b // 2 + 1))
            if b == 0:
                pe.wait_ge(copied, 1)
                pe.wait_ge(maps_cp, 2)
                pe.wait_ge(v_cp, QT + 1)
            if b == 4:
                pe.wait_ge(sidx_relu, 1)
            r = 32 * (b % 4)
            for j, (a, w) in enumerate(COLS):
                keys = kring[HD:P, b % 2].rearrange("p g c -> p (g c)")[:, a:a + w] if j < 2 else Z[HD:P, KA, SEQ:NT]
                last = nc.tensor.matmul(bank(4 + j)[r:r + 32, 0:w], qis[HD:P, b].rearrange("p h t -> p (h t)"), keys, start=True, stop=True)
            last.then_inc(sidx_mm, 1)

        def pe_sscore(pe):
            pe.wait_ge(wsel_set, 2)
            pe.wait_ge(sidx_relu, 2)
            for j, (a, w) in enumerate(COLS):
                for g in range(2):
                    last = nc.tensor.matmul(bank(4 + j)[0:NS, 0:w], wsel[:, g], srelu[:, g, a:a + w], start=g == 0, stop=g == 1)
            last.then_inc(sscore_mm, 1)

        def act_sidx(act, g):
            act.wait_ge(sidx_mm, 4 * g + 4)
            for j, (a, w) in enumerate(COLS):
                last = nc.scalar.activation(srelu[:, g, a:a + w], bank(4 + j)[:, 0:w], ACT.Relu, scale=IDX_SCALE)
            last.then_inc(sidx_relu, 1)

        def dve_sscore(dve):
            dve.wait_ge(sscore_mm, 1)
            for j, (a, w) in enumerate(COLS[:2]):
                nc.vector.tensor_copy(SC[0:NS, SC_S + a:SC_S + a + w], bank(4 + j)[0:NS, 0:w])
            nc.vector.tensor_tensor(SC[0:NS, SC_S + PAST:SC_N], bank(6)[0:NS, 0:NS], c_("newmask", NS), ALU.add).then_inc(sscored, 1)

        TAIL = FIRST_DSA + 4

        def act_sdiff_tail(act):
            act.wait_ge(dsum_mm, 1)
            nc.scalar.activation(omean, bank(5)[:, 0:64], ACT.Identity, bias=eps[:, :], scale=1.0 / HD).then_inc(dmean, 1)

        def dve_sdiff_sum(dve, chain):
            dve.wait_ge(so_cp, DB)
            O = so.rearrange("p b (c r) -> p c b r", c=2)
            o = od.rearrange("p (c b t) -> p c b t", c=2, t=DT)
            for h in range(4):
                c, half = h // 2, slice(HD * (h % 2), HD * (h % 2) + HD)
                added = chain.mark(nc.vector.tensor_tensor(o[half, c], O[half, c, :, 8 * h:8 * h + 4],
                                                           O[half, c, :, 8 * h + 4:8 * h + 8], ALU.add))
            chain.until(added)
            nc.vector.tensor_tensor(osqs, od, od, ALU.mult).then_inc(dsq, 1)

        def dve_sdiff_out(dve):
            dve.wait_ge(drstd, 1)
            for c in range(2):
                nc.vector.scalar_tensor_tensor(Z[:, PV + c, SEQ:NT], od[:, 32 * c:32 * c + 32], subln[:, :],
                                               orstd[:, 32 * c:32 * c + 32], ALU.mult, ALU.mult).then_inc(dy, 1)

        def pool_sdiff_tail(pool):
            pool.wait_ge(dmean, 1)
            nc.gpsimd.tensor_tensor(orstd, omean, neghalf[:, 0:1].to_broadcast([P, 64]), ALU.pow).then_inc(drstd, 1)

        def pe_sdiff_tail(pe):
            pe.wait_ge(dsq, 1)
            nc.tensor.matmul(bank(5)[:, 0:64], c_("headones"), osqs, start=True, stop=True).then_inc(dsum_mm, 1)

        H = Z[:, 8:16]
        W_OUT = NZ
        W_FF = W_OUT + KC
        W_PLE = W_FF + 3 * FC
        W_PG = W_PLE + 2
        EXT = 2 + SEQ + DB * 6
        tail = Z[:, 16:23].rearrange("p s t -> p (s t)")
        ge = [tail[:, a * EXT:(a + 1) * EXT] for a in range(2)]
        gv = [tail[:, a * EXT:(a + 1) * EXT] for a in range(2, 4)]
        gu = [tail[:, 4 * EXT + a * NT:4 * EXT + (a + 1) * NT] for a in range(2)]
        st_in = tail[:, 4 * EXT + 2 * NT:][:, 0:FC * DB * 2].rearrange("p (f b t) -> p f b t", f=FC, b=DB)
        st_out = TN[:, 2, 0:FC * 9 * 2].rearrange("p (f b t) -> p f b t", f=FC, b=1 + DB)
        GROUPS = FC // 2
        y_hi_cp, y_lo_cp = sem("mixer_hi"), sem("mixer_lo")
        x_again = [sem(f"x_again{k}") for k in range(KC)]
        h_out = sem("residual_mixed")
        st_loaded, st_stored = sem("ffn_state_loaded"), sem("ffn_state_stored")
        w_conv = sem("conv_weights_copied")
        g_cp = sem("gate_copied")
        g_conv = sem("gate_convolved")
        g_silu = sem("gate_silu")
        act_mul = sem("gate_times_up")
        a_hi, a_lo = sem("mlp_hi"), sem("mlp_lo")
        d_mm, h_ffn = sem("down_product"), sem("residual_mlp")
        p_in, p_hi, p_lo = sem("ple_loaded"), sem("ple_hi"), sem("ple_lo")
        ple_mm, ple_cp = sem("ple_product"), sem("ple_copied")
        s_gate, h_ple = sem("ple_gate"), sem("residual_ple")
        mix_stored = sem("mixer_state_stored")
        y_rows = [sem("y_row0"), sem("y_row1")]
        PP = [Z[:, s] for s in (0, 1, 4, 5, 18, 19, 20, 21)]
        SG = [Z[:, s] for s in (2, 3)]
        norm_ffn = Norm("norm_ffn", lambda k: H[:, k], "g_ffn")
        norm_ple = Norm("norm_ple", lambda k: H[:, k], "g_ple")
        norm_final = Norm("norm_final", lambda k: H[:, k], "g_final", split=False)

        def hi_next(act, n, slot=None, load_no=None):
            split_hi(act, n, n % 2 if slot is None else slot, n // 2 + 1 if load_no is None else load_no)

        def act_mixers(act):
            act.wait_ge(dy, 2)
            act.wait_ge(so_cp, sample_no(NI))
            act.wait_ge(o_cp, 2 * QT)
            for k in range(KC):
                nc.scalar.activation(xh[:, k], Z[:, k], ACT.Copy).then_inc(y_hi_cp, 1)

        def dve_mixers(dve):
            for k in range(KC):
                dve.wait_ge(y_hi_cp, k + 1)
                nc.vector.tensor_tensor(xl[:, k], Z[:, k], xh[:, k].bitcast(f32), ALU.subtract).then_inc(y_lo_cp, 1)

        def pool_reload(pool):
            pool.wait_ge(pv_mm, NI)
            for k in range(KC):
                pool.dma_start(H[:, k], d["xT"][k]).then_inc(x_again[k], 16)

        def act_out(act):
            for m in range(KC):
                act.wait_ge(w_used, W_OUT + m + 1)
                hi_next(act, W_OUT + m + 2)
                if m:
                    act.wait_ge(h_out, m)
                    norm_ffn.square(act, m - 1)
            act.wait_ge(h_out, KC)
            norm_ffn.square(act, KC - 1)

        def by_bank(a):
            return a.rearrange("p (c t) -> p c t", c=3)

        def dve_out(dve):
            for m in range(KC):
                dve.wait_ge(w_used, W_OUT + m + 1)
                dve.wait_ge(x_again[m], 16)
                nc.vector.tensor_tensor(by_bank(H[:, m]), by_bank(H[:, m]), ps[(W_OUT + m) % 2][:, 0:3, 0:TC], ALU.add).then_inc(h_out, 1)
                split_lo(dve, W_OUT + m + 2, (W_OUT + m) % 2)
                if m >= 2:
                    norm_ffn.add(dve, m - 1)
            norm_ffn.add(dve, KC - 1)

        def gate_block(g, q, s):
            return W_FF + 2 * q + (0 if s == 0 else 6 * g - 2)

        def down_block(g, s):
            return W_FF + 6 * g + (8 if s < GROUPS - 1 else 4)

        def gates_used(g, q):
            return W_FF + 4 * g + 2 * q + 1

        def chunk(a, f):
            return a[:, bass.ds(f, 1)].rearrange("p o x y -> p (o x) y")

        def pe_gate_up(pe, g, s):
            for q in range(2):
                f, n = 2 * g + q, gate_block(g, q, s)
                first = s == 0 and q == 0
                pe.wait_ge(w_lo, n + 1)
                if not first:
                    pe.wait_ge(g_cp, f)
                block_product(0, pe, norm_ffn.lo if first else None).then_inc(w_used, 1)
                pe.wait_ge(w_lo, n + 2)
                if not first:
                    pe.wait_ge(act_mul, f)
                block_product(1).then_inc(w_used, 1)

        def pe_down(pe, g, s):
            pe.wait_ge(a_lo, 2 * g + 2)
            for m in range(KC):
                if m % 4 == 0:
                    pe.wait_ge(w_lo, down_block(g, s) + m // 4 + 1)
                for c in range(3):
                    v = 3 * m + c
                    if s or v >= 2:
                        pe.wait_ge(h_ffn, g * KC * 3 + v - 1)
                    for q in range(2):
                        for t, (w, x) in enumerate(((wh, ah), (wl, ah), (wh, al))):
                            last = nc.tensor.matmul(bank(3 + 4 * (v % 2))[:, 0:TC], w[:, m // 4, 4 * q + m % 4],
                                                    x[:, s % 2, q, c * TC:(c + 1) * TC], start=q == 0 and t == 0, stop=q == 1 and t == 2)
                    last.then_inc(d_mm, 1)

        def act_gate_up(act, g, s):
            for q in range(2):
                f = 2 * g + q
                load_no = gate_block(g, q, s) // 2 + 2 if s == 0 else W_FF // 2 + 3 * g + q + 1
                act.wait_ge(w_used, gates_used(g, q))
                hi_next(act, None, 0, load_no)
                if s:
                    act.wait_ge(g_conv, f - 1)
                e, gate = ge[q], ps[0]
                nc.scalar.activation(e[:, 2:2 + 2 * TC].rearrange("p (c t) -> p c t", c=2), gate[:, 0:2, 0:TC], ACT.Copy)
                nc.scalar.activation(e[:, 2 + 2 * TC:2 + SEQ], gate[:, 2, 0:SEQ - 2 * TC], ACT.Copy)
                nc.scalar.activation(e[:, 2 + SEQ:].rearrange("p (b t) -> p b t", t=6)[:, :, 2:6],
                                     gate[:, 2, SEQ - 2 * TC:TC].rearrange("p (b t) -> p b t", t=DT), ACT.Copy).then_inc(g_cp, 1)
                act.wait_ge(g_conv, f + 1)
                nc.scalar.activation(gv[q][:, 0:EXT - 2], gv[q][:, 0:EXT - 2], ACT.Silu).then_inc(g_silu, 1)
                act.wait_ge(w_used, gates_used(g, q) + 1)
                hi_next(act, None, 1, load_no)
                act.wait_ge(act_mul, f + 1)
                if s >= 2:
                    act.wait_ge(d_mm, (g - 1) * KC * 3)
                nc.scalar.activation(ah[:, s % 2, q], gu[q], ACT.Copy).then_inc(a_hi, 1)

        def act_down(act, g, s):
            for half in range(2):
                act.wait_ge(d_mm, g * KC * 3 + 12 * (half + 1))
                hi_next(act, None, half, W_FF // 2 + 3 * g + (6 if s < GROUPS - 1 else 4))

        def dve_gate_up(dve, chain, g, s):
            link = chain.link
            for q in range(2):
                f, n = 2 * g + q, gate_block(g, q, s)
                split_lo(dve, n + 2, 0)
                e, v, w = ge[q], gv[q], small[:, 34 + 3 * q:37 + 3 * q]
                es = e[:, 2 + SEQ:].rearrange("p (b t) -> p b t", t=6)
                if s == 0:
                    nc.vector.memset(e[:, 0:2], 0.0)
                nc.vector.tensor_copy(es[:, :, 0:2], chunk(st_in, f))
                nc.vector.tensor_copy(w, p_("conv_ffn")[:, bass.ds(3 * f, 3)]).then_inc(w_conv, 1)
                dve.wait_ge(g_cp, f + 1)
                dve.wait_ge(w_conv, f + 1)
                out = chunk(st_out, f)
                nc.vector.tensor_copy(out[:, 0], e[:, SEQ:SEQ + 2])
                link(nc.vector.tensor_copy(out[:, 1:], es[:, :, 4:6]))
                link(nc.vector.tensor_scalar(v[:, 0:EXT - 2], e[:, 0:EXT - 2], w[:, 0:1], None, ALU.mult))
                link(nc.vector.scalar_tensor_tensor(v[:, 0:EXT - 2], e[:, 1:EXT - 1], w[:, 1:2], v[:, 0:EXT - 2], ALU.mult, ALU.add))
                nc.vector.scalar_tensor_tensor(v[:, 0:EXT - 2], e[:, 2:EXT], w[:, 2:3], v[:, 0:EXT - 2], ALU.mult, ALU.add).then_inc(g_conv, 1)
                dve.wait_ge(g_silu, f + 1)
                dve.wait_ge(w_used, gates_used(g, q) + 1)
                up, u = ps[1], gu[q]
                nc.vector.tensor_tensor(u[:, 0:2 * TC].rearrange("p (c t) -> p c t", c=2), v[:, 0:2 * TC].rearrange("p (c t) -> p c t", c=2),
                                        up[:, 0:2, 0:TC], ALU.mult)
                nc.vector.tensor_tensor(u[:, 2 * TC:SEQ], v[:, 2 * TC:SEQ], up[:, 2, 0:SEQ - 2 * TC], ALU.mult)
                nc.vector.tensor_tensor(u[:, SEQ:NT].rearrange("p (b t) -> p b t", t=DT),
                                        v[:, 2 + SEQ:EXT].rearrange("p (b t) -> p b t", t=6)[:, :, 0:DT],
                                        up[:, 2, SEQ - 2 * TC:TC].rearrange("p (b t) -> p b t", t=DT), ALU.mult).then_inc(act_mul, 1)
                if q == 0 or s == 0:
                    split_lo(dve, n + 3, 1)
                    dve_rest(dve, g, q, s)

        def dve_rest(dve, g, q, s):
            dve.wait_ge(a_hi, 2 * g + q + 1)
            nc.vector.tensor_tensor(al[:, s % 2, q], gu[q], ah[:, s % 2, q].bitcast(f32), ALU.subtract).then_inc(a_lo, 1)

        def dve_down(dve, g, s):
            for m in range(KC):
                if m == 1 and s + 1 < GROUPS:
                    split_lo(dve, down_block(g, s) + 1, 1)
                if m == 2 and s + 1 < GROUPS:
                    dve_rest(dve, g + 1, 1, s + 1)
                for c in range(3):
                    v = 3 * m + c
                    dve.wait_ge(d_mm, g * KC * 3 + v + 1)
                    if s:
                        dve.wait_ge(h_ffn, (g - 1) * KC * 3 + v + 1)
                    cols = H[:, m, c * TC:(c + 1) * TC]
                    nc.vector.tensor_tensor(cols, cols, bank(3 + 4 * (v % 2))[:, 0:TC], ALU.add).then_inc(h_ffn, 1)
                if m % 4 == 3:
                    split_lo(dve, down_block(g, s) + m // 4 + 2, m // 4)

        def groups(eng, gate_up, down, chain=None):
            gate_up(0, 0)
            gate_up(1, 1)
            down(0, 0)
            PASSES = (GROUPS - 3) // 2
            if chain:
                chain.enter(PASSES, 3 * 4)
            with eng.Fori(0, PASSES) as j:
                if chain:
                    chain.pass_of(j)
                for r in range(2):
                    gate_up(2 * j + r + 2, r + 2)
                    down(2 * j + r + 1, r + 1)
            if chain:
                chain.leave()
            gate_up(GROUPS - 1, GROUPS - 1)
            down(GROUPS - 2, GROUPS - 2)
            down(GROUPS - 1, GROUPS - 1)

        ALL_FF = GROUPS * KC * 3

        def pool_ple(pool):
            pool.wait_ge(act_mul, FC)
            pool.wait_ge(a_lo, FC)
            for k in range(2):
                pool.dma_start(Z[:, 16 + k], d["pT"][k]).then_inc(p_in, 16)
            pool.dma_start(d["st_ffn"], st_out).then_inc(st_stored, 16)

        def act_ple_split(act):
            act.wait_ge(p_in, 32)
            act.wait_ge(d_mm, ALL_FF)
            for k in range(2):
                nc.scalar.activation(ah[:, 1, k], Z[:, 16 + k], ACT.Copy).then_inc(p_hi, 1)

        def dve_ple_split(dve):
            for k in range(2):
                dve.wait_ge(p_hi, k + 1)
                nc.vector.tensor_tensor(al[:, 1, k], Z[:, 16 + k], ah[:, 1, k].bitcast(f32), ALU.subtract).then_inc(p_lo, 1)

        def pe_ple(pe):
            pe.wait_ge(p_lo, 2)
            pe.wait_ge(h_ffn, ALL_FF)
            for m in range(KC):
                n = W_PLE + m // 4
                pe.wait_ge(w_lo, n + 1)
                for c in range(3):
                    v = 3 * m + c
                    if v >= 2:
                        pe.wait_ge(ple_cp, v - 1)
                    for q in range(2):
                        for t, (w, x) in enumerate(((wh, ah), (wl, ah), (wh, al))):
                            last = nc.tensor.matmul(bank(3 + 4 * (v % 2))[:, 0:TC], w[:, n % 2, 4 * q + m % 4],
                                                    x[:, 1, q, c * TC:(c + 1) * TC], start=q == 0 and t == 0, stop=q == 1 and t == 2)
                    last.then_inc(ple_mm, 1)

        def act_ple(act, m):
            for c in range(3):
                v = 3 * m + c
                act.wait_ge(ple_mm, v + 1)
                nc.scalar.activation(PP[m][:, c * TC:(c + 1) * TC], bank(3 + 4 * (v % 2))[:, 0:TC], ACT.Copy).then_inc(ple_cp, 1)
            if m % 4 == 3:
                hi_next(act, W_PLE + m // 4 + 2)

        def act_ple_gate(act):
            for m in range(KC):
                act.wait_ge(w_used, W_FF + 4 * GROUPS + m + 1)
                if m + 2 < KC:
                    hi_next(act, W_PG + m + 2)
                if m >= 2:
                    act.wait_ge(h_ple, m - 1)
                nc.scalar.activation(by_bank(SG[m % 2]), ps[(W_PG + m) % 2][:, 0:3, 0:TC], ACT.Sigmoid).then_inc(s_gate, 1)
                if m:
                    act.wait_ge(h_ple, m)
                    norm_final.square(act, m - 1)
            act.wait_ge(h_ple, KC)
            norm_final.square(act, KC - 1)

        def dve_ple_gate(dve, link):
            for m in range(KC):
                if m + 2 < KC:
                    split_lo(dve, W_PG + m + 2, (W_PG + m) % 2)
                dve.wait_ge(s_gate, m + 1)
                link(nc.vector.tensor_tensor(SG[m % 2], SG[m % 2], PP[m], ALU.mult))
                nc.vector.tensor_tensor(H[:, m], H[:, m], SG[m % 2], ALU.add).then_inc(h_ple, 1)
                if m >= 2:
                    norm_final.add(dve, m - 1)
            norm_final.add(dve, KC - 1)

        def final_row_free(dve, k):
            dve.wait_ge(y_rows[k % 2], 16 * (k // 2))
        norm_final.wait_row = final_row_free

        def sp_store(sp):
            for k in range(KC):
                sp.wait_ge(norm_final.xn, k + 1)
                sp.dma_start(d["y"][k], TN[:, 1 + k % 2]).then_inc(y_rows[k % 2], 16)

        block = ctx.enter_context(nc.Block())

        @block.sync
        def _(sp):
            sp.dma_start(cst[:, :], d["consts"]).then_inc(s_const, 16)
            sp.dma_start(par[:, :], d["params"]).then_inc(s_const, 16)
            sp.dma_start(ptab[:, :], d["page_table"]).then_inc(pt_in, 16)
            for k in range(KC):
                sp.dma_start(Z[:, k], d["xT"][k]).then_inc(x_loaded[k], 16)
            for n in range(2):
                sp.dma_start(wr[:, n], d["weights"][n]).then_inc(w_raw[n], 16)
            def load_block(n, slot):
                sp.dma_start(wr[:, slot], d["weights"][bass.ds(n, 1)].rearrange("o p k m -> p (o k) m")).then_inc(w_raw[slot], 16)

            with sp.Fori(1, NZ // 2) as j:
                for slot in range(2):
                    sp.wait_ge(w_lo, 2 * j + slot - 1)
                    load_block(2 * j + slot, slot)
            sp_idx_pages(sp)
            sp_diff_pages(sp)
            sp_dsa_pages(sp)
            sp.wait_ge(pv_mm, item_no("sdsa", DB // 2 - 1) + 1)
            for n in (W_OUT, W_OUT + 1):
                load_block(n, n % 2)
            with sp.Fori(W_OUT // 2 + 1, NW // 2) as j:
                for n, slot in ((2 * j, 0), (2 * j + 1, 1)):
                    sp.wait_ge(w_lo, n - 1)
                    load_block(n, slot)
            sp_store(sp)
            for a in range(2):
                sp.wait_ge(y_rows[a], 16 * KC // 2)


        @block.gpsimd
        def _(pool):
            pool.wait_ge(ones_set, 1)
            norm_mix.pool(pool)
            pool.wait_ge(d_mixed, 2)
            nc.gpsimd.memset(CM, 0.0).then_inc(masks_set, 1)
            pool.wait_ge(masks_set, 1)
            nc.gpsimd.affine_select(out=CM[:, SEQ - P:SEQ], in_=CM[:, SEQ - P:SEQ], compare_op=ALU.is_ge, fill=-BIG, base=0,
                                    pattern=[[-1, P]], channel_multiplier=1).then_inc(masks_set, 1)
            pool.wait_ge(evac, NZ)
            outs = [(d["c_k"], Z[0:HD, KA]), (d["c_idx"], Z[HD:P, KA]), (d["c_v"], Z[0:HD, CV])]
            outs += [(d[name][j], Z[:, at + j]) for name, at in (("d_k", DK), ("d_v", DV)) for j in range(2)]
            for dst, src in outs:
                pool.dma_start(dst, src).then_inc(outs_stored, 16)
            for tile in range(QT):
                pool.wait_ge(ss_ready, tile + 1)
                nc.gpsimd.tensor_tensor(rs4[:, 16:20], rs4[:, 12:16], neghalf[:, 0:4], ALU.pow).then_inc(head_rstd, 1)
            pool_sdiff_tail(pool)
            pool_reload(pool)
            pool.dma_start(st_in, d["st_ffn_in"]).then_inc(st_loaded, 16)
            pool.dma_start(d["st_mix"], ST[:, :, :, :]).then_inc(mix_stored, 16)
            norm_ffn.pool(pool)
            pool_ple(pool)
            norm_ple.pool(pool)
            norm_final.pool(pool)
            pool.wait_ge(outs_stored, 16 * len(outs))
            pool.wait_ge(mix_stored, 16)
            pool.wait_ge(st_stored, 16)


        @block.scalar
        def _(act):
            act.wait_ge(ones_set, 1)
            for k in range(KC):
                act.wait_ge(x_loaded[k], 16)
                norm_mix.square(act, k)
            for n in range(2):
                split_hi(act, n, n, 1)
            norm_mix.act(act)
            def step(n, slot, load_no):
                act.wait_ge(w_used, n + 1)
                if type(n) is not int or n + 2 < NZ:
                    split_hi(act, n + 2, slot, load_no)
                nc.scalar.activation(z_slot(n), ps[slot][:, 0:3, 0:TC], ACT.Copy).then_inc(evac, 1)

            def z_slot(n):
                return (Z[:, n] if type(n) is int else Z[:, bass.ds(n, 1)].rearrange("p o t -> p (o t)")).rearrange("p (c t) -> p c t", c=3)
            with act.Fori(0, (NZ - 2) // 2) as j:
                for slot in range(2):
                    step(2 * j + slot, slot, j + 2)
            for n in range(NZ - 2, NZ):
                step(n, n % 2, n // 2 + 2)
            act_values(act)
            act_keys(act, slice(HD, P))
            for t in range(2):
                act_idx_queries(act, t)
            act_maps(act)
            act_lambda(act)
            act_sample_copies(act)
            act_idx(act)
            for n in range(NI + 6):
                act_item(act, n)
                if n == KEYS_STEP:
                    nc.scalar.activation(Z[HD:P, KA, 0:SEQ], Z[0:HD, KA, 0:SEQ], ACT.Copy).then_inc(keys_twice, 1)
                    act.wait_ge(keys_twice, 1)
                    act_keys(act, slice(0, HD))
                if n in PREPARE:
                    act_dsa_queries(act, PREPARE[n])
                if n == TAIL + 1:
                    act_sdiff_tail(act)
            for n in (W_OUT, W_OUT + 1):
                hi_next(act, n)
            act_mixers(act)
            act_out(act)
            norm_ffn.act(act)
            groups(act, lambda g, s: act_gate_up(act, g, s), lambda g, s: act_down(act, g, s))
            act_ple_split(act)
            act.wait_ge(st_stored, 16)
            act.wait_ge(h_ffn, ALL_FF)
            for k in range(KC):
                norm_ple.square(act, k)
                act_ple(act, k)
            norm_ple.act(act)
            act_ple_gate(act)
            norm_final.act(act)


        @block.vector
        def _(dve):
            nc.vector.memset(eps[:, :], EPS)
            nc.vector.memset(neghalf[:, :], -0.5)
            nc.vector.memset(ones[:, :], 1.0).then_inc(ones_set, 1)
            dve.wait_ge(s_const, 32)
            for k in range(1, KC):
                norm_mix.add(dve, k)
            for n in range(2):
                split_lo(dve, n, n)
            norm_mix.dve(dve)
            with dve.Fori(1, 6) as j:
                for slot in range(2):
                    split_lo(dve, 2 * j + slot, slot)
            chain = Chain(dve, "dve_chain")
            link = chain.link
            for n in range(12, NZ):
                split_lo(dve, n, n % 2)
                if n in (13, 14):
                    dve_conv(dve, link, n - 13)
                if n in (15, 17):
                    dve_pool(dve, link, (n - 15) // 2)
            dve.wait_ge(evac, NZ)
            dve_keys(dve, 1)
            dve.wait_ge(w_used, NZ)
            for t in range(2):
                dve_idx_queries(dve, chain, t)
            dve_lambda(dve, link)
            dve.wait_ge(v_cp, QT + 1)
            dve.wait_ge(outs_stored, 16 * 7)
            nc.vector.memset(ex[:, 0:768], 0.0).then_inc(zeroed, 1)
            dve.wait_ge(masks_set, 2)
            nc.vector.tensor_scalar(CP, CM[:, SEQ - P:SEQ], BIG, None, ALU.add)
            link(nc.vector.tensor_scalar(newcp, c_("newmask"), BIG, None, ALU.add))
            link(nc.vector.memset(tk[:, :, :], 0.0))
            dve_wsel(dve, link)
            dve_idx(dve, chain)
            for n in range(NI + 6):
                dve_item(dve, chain, n)
                if n == KEYS_STEP + 1:
                    dve_keys(dve, 2)
                if n == TAIL:
                    dve_sdiff_sum(dve, chain)
                if n == TAIL + 2:
                    dve_sdiff_out(dve)
            for n in (W_OUT, W_OUT + 1):
                split_lo(dve, n, n % 2)
            dve_mixers(dve)
            dve_out(dve)
            norm_ffn.dve(dve)
            dve.wait_ge(st_loaded, 16)
            groups(dve, lambda g, s: dve_gate_up(dve, chain, g, s), lambda g, s: dve_down(dve, g, s), chain)
            dve_ple_split(dve)
            for k in range(1, KC):
                norm_ple.add(dve, k)
            for half in range(2):
                split_lo(dve, W_PG + half, (W_PG + half) % 2)
            norm_ple.dve(dve)
            dve_ple_gate(dve, link)
            norm_final.dve(dve)


        @block.tensor
        def _(pe):
            pe.wait_ge(ones_set, 1)
            norm_mix.pe(pe)
            for n in range(2):
                pe.wait_ge(w_lo, n + 1)
                block_product(n, pe, None if n else norm_mix.lo).then_inc(w_used, 1)
            with pe.Fori(1, NZ // 2) as j:
                for slot in range(2):
                    project_pe(pe, 2 * j + slot, slot)
            pe.wait_ge(evac, NZ)
            pe_values(pe)
            pe_maps(pe)
            pe.wait_ge(masks_set, 2)
            pe.wait_ge(v_cp, QT + 1)
            pe_wcol(pe)
            pe.wait_ge(maps_cp, 2)
            pe_idx(pe)
            pe.wait_ge(sscored, 1)
            pe.wait_ge(idx_relu, len(IDX))
            for n in range(NI + 6):
                if n == TAIL + 1:
                    pe_sdiff_tail(pe)
                pe_item(pe, n)
            pe_stage(pe, W_OUT, y_lo_cp, h_out)
            norm_ffn.pe(pe)
            groups(pe, lambda g, s: pe_gate_up(pe, g, s), lambda g, s: pe_down(pe, g, s))
            pe_ple(pe)
            norm_ple.pe(pe)
            pe_stage(pe, W_PG, norm_ple.lo, s_gate)
            norm_final.pe(pe)





def weight_blocks(w_in, w_out, w_gate, w_up, w_down, w_ple, w_ple_gate):
    def rows(w):
        return w.reshape(KC, P, P).transpose(1, 0, 2)

    out = []
    for pieces in IN_COLS:
        w = np.concatenate([w_in[:, a:a + n] for a, n in pieces], axis=1)
        out.append(rows(np.pad(w, ((0, 0), (0, P - w.shape[1])))))
    out += [rows(w_out[:, m * P:(m + 1) * P]) for m in range(KC)]

    def gate_up(g):
        return [rows(w[:, f * P:(f + 1) * P]) for f in (2 * g, 2 * g + 1) for w in (w_gate, w_up)]

    def down(g):
        w = w_down[2 * g * P:(2 * g + 2) * P].reshape(2, P, 2, 4, P)
        return [w[:, :, half].transpose(1, 0, 2, 3).reshape(P, KC, P) for half in range(2)]

    out += gate_up(0)
    for g in range(FC // 2 - 1):
        out += gate_up(g + 1) + down(g)
    out += down(FC // 2 - 1)
    w = w_ple.reshape(2, P, 2, 4, P)
    out += [w[:, :, half].transpose(1, 0, 2, 3).reshape(P, KC, P) for half in range(2)]
    out += [rows(w_ple_gate[:, m * P:(m + 1) * P]) for m in range(KC)]
    assert len(out) == NW
    return np.stack(out)


def constants():
    c = np.zeros((P, CONST_N), np.float32)

    def put(name, a):
        at, n = CONST[name]
        c[0:a.shape[0], at:at + n] = a

    tok = np.arange(NS)
    put("ident", np.eye(P))
    row = np.arange(P)
    put("hsel", (row[:, None] % 32 // 4 == np.arange(8)[None]))
    put("headones", (row[:, None] // HD == row[None] // HD))
    for g in range(2):
        sel = (4 * g + row[:, None] // 32 == tok[None] // DT) & (row[:, None] % DT == tok[None] % DT)
        put(f"sel{g}", sel)
        put(f"e{g}", sel.T)
    own = (np.arange(DB)[None, :, None] == tok // DT) & (tok % DT <= tok[:, None, None] % DT)
    put("dmask", np.where(own, 0.0, -BIG).reshape(NS, DB * NS))
    rep = (row[None] // 16 == tok[:, None] // DT) & (row[None] % DT == tok[:, None] % DT)
    put("rep", rep)
    put("newmask", np.where((tok[:, None] // DT == tok[None] // DT) & (tok[None] % DT <= tok[:, None] % DT), 0.0, -BIG))
    m = row % 8 // 4
    put("lam_a", (m == 0)[:, None])
    put("lam_b", (m == 1)[:, None])
    win = np.array([[2, 8], [4, 16]])[row // HD]
    put("inv_w", 1.0 / win)
    cnt = np.minimum(win[:, :, None], np.arange(1, 17)[None, None])
    put("inv_cnt", (1.0 / cnt).reshape(P, 32))
    valid = np.stack([i * P + row + 1 for i in TILES] + [PAST + row % DT + 1], 1)
    kneg = valid - TOPK + 1
    put("kneg", kneg)
    put("kdiff", TOPK - kneg)
    by_act = np.isin(np.arange(NTOP), ACT_TOP)
    put("kmul", np.broadcast_to(np.where(by_act, 2.0, 1.0), (P, NTOP)))
    kadd = np.where(by_act, [-(i + 1.0) * P for i in TILES] + [0.0], np.zeros((P, 1)))
    kadd[NS:, -1] = 1.0
    put("kadd", kadd)
    return c


def parameters(i):
    p = np.zeros((P, PARAM_N), np.float32)

    def put(name, a):
        at, n = PARAM[name]
        p[0:a.shape[0], at:at + n] = a.reshape(a.shape[0], n)

    put("g_mix", i["norm_mix"][0].reshape(KC, P).T)
    put("g_ffn", i["norm_ffn"][0].reshape(KC, P).T)
    put("g_ple", i["norm_ple"][0].reshape(KC, P).T)
    put("g_final", i["norm_final"].reshape(KC, P).T)
    put("conv_a", i["conv_a"][0].reshape(3, 2, P).transpose(2, 1, 0))
    put("pool_scale", i["pool_scale"][0].reshape(2, P).T)
    put("conv_ffn", i["conv_ffn"][0].reshape(3, FC, P).transpose(2, 1, 0))
    put("subln", np.tile(i["diff_subln"][0], 2)[:, None])
    put("lam", np.broadcast_to(i["diff_lambda"][0].reshape(1, P), (P, P)))
    maps = np.zeros((P, 2, P), np.float32)
    for g in range(4):
        r = (g % 2) * HD
        maps[r:r + HD, g // 2, r:r + HD] = i["pool_maps"][0, g]
    put("maps", maps)
    put("st_conv", i["state_conv_a"][0].reshape(DB, 2, 2, P).transpose(3, 2, 0, 1))
    put("st_pool", i["state_pool"][0].reshape(DB, 15, 2, P).transpose(3, 2, 0, 1))
    return p


def kernel(**inputs):
    import numpy as _np
    import concourse.bacc as _bacc
    from concourse import mybir as _mybir
    from concourse.bass_utils import run_bass_kernel_spmd as _run

    i = {k: _np.asarray(v) for k, v in inputs.items()}
    xT = _np.concatenate([i["x_prompt"][0].T, i["x_sample"].reshape(NS, D).T], axis=1).reshape(KC, P, NT)
    pT = _np.concatenate([i["p_prompt"][0, 0].T, i["p_sample"][0].reshape(NS, PLE).T], axis=1).reshape(2, P, NT)
    ck, cv, ci = (i[n][:, 0] for n in ("cache_c_k", "cache_c_v", "cache_c_idx"))
    c_pages = _np.concatenate([_np.concatenate([ck, ci], axis=2).transpose(0, 2, 1), cv], axis=2)
    dk, dv = i["cache_d_k"][:, 0], i["cache_d_v"][:, 0]
    n_phys = dk.shape[0]
    dkT = dk.reshape(n_phys, PAGE, 2, P).transpose(0, 3, 2, 1).reshape(n_phys, P, 2 * PAGE)
    d_pages = _np.concatenate([dkT, dv.reshape(n_phys, PAGE, 256)], axis=2)
    arrays = {
        "xT": xT, "pT": pT, "c_pages": c_pages, "d_pages": d_pages,
        "weights": weight_blocks(i["w_in"][0], i["w_out"][0], i["w_gate"][0], i["w_up"][0], i["w_down"][0],
                                 i["w_ple"][0], i["w_ple_gate"][0]),
        "consts": constants(), "params": parameters(i), 
        "st_ffn_in": i["state_ffn"][0].reshape(DB, 2, FC, P).transpose(3, 2, 0, 1), "page_table": i["page_table"].reshape(1, -1),
    }
    arrays = {k: _np.ascontiguousarray(v) for k, v in arrays.items()}
    nc = _bacc.Bacc("TRN2", target_bir_lowering=False, num_devices=1)
    d = {}
    for name, a in arrays.items():
        d[name] = nc.dram_tensor(f"in_{name}", a.shape, _mybir.dt.from_np(a.dtype), kind="ExternalInput").ap()
    for name, shape in OUTS.items():
        d[name] = nc.dram_tensor(f"out_{name}", shape, _mybir.dt.float32, kind="ExternalOutput").ap()
    build(nc, d)
    r = _run(nc, [{f"in_{k}": v for k, v in arrays.items()}], core_ids=[0]).results[0]
    o = {name: _np.asarray(r[f"out_{name}"]) for name in OUTS}

    def rows(a, width):
        a = a.reshape(-1, NT)[0:width]
        return a[:, :SEQ].T, a[:, SEQ:].T.reshape(DB, DT, width)

    y_p, y_s = rows(o["y"], D)
    res = [y_p[None], y_s]
    st = o["st_mix"]
    conv = st[:, :, :, 0:2]
    pool = st[:, :, :, 2:17]
    for s in (conv, pool):
        s = s.transpose(2, 3, 1, 0).reshape(1 + DB, s.shape[3], 256)
        res += [s[0:1][None], s[1:][None]]
    s = o["st_ffn"].reshape(P, FC, 1 + DB, 2).transpose(2, 3, 1, 0).reshape(1 + DB, 2, FF)
    res += [s[0:1][None], s[1:][None]]
    for a in (o["c_k"], o["c_v"], o["c_idx"]):
        p, s = rows(a, HD)
        res += [p[None, None], s[:, None]]
    for a in (o["d_k"], o["d_v"]):
        p, s = rows(a, 256)
        res += [p.reshape(1, 1, SEQ, 4, HD), s.reshape(DB, 1, DT, 4, HD)]
    return tuple(_np.ascontiguousarray(a) for a in res)
```
